# Optimizing a Trainium2 kernel written in Bass

```python
import jax, jax.numpy as jnp
from jax import lax
import numpy as np

D_MODEL = 1024
BATCH = 1
SEQ = 2048
DEPTH = 1

GRID_W = 64
N_HEADS = 8
N_KV_HEADS = 2
HEAD_DIM = 64
ATTN_WIDTH = N_HEADS * HEAD_DIM
KV_WIDTH = N_KV_HEADS * HEAD_DIM
CONV_WIDTH = D_MODEL // 2
CONV_KSIZE = 31
Q_BLOCK = 128
ROPE_THETA = 10000.0
HALF_ROT = HEAD_DIM // 2
N_GROUPS = 4
EXPERTS_PER_GROUP = 8
N_EXPERTS = N_GROUPS * EXPERTS_PER_GROUP
TOP_K = 2
D_EXPERT = D_MODEL // 2
MOE_BLOCK = 128
EPS = 1e-6
SPLITS = (2 * CONV_WIDTH,
          2 * CONV_WIDTH + ATTN_WIDTH,
          2 * CONV_WIDTH + ATTN_WIDTH + KV_WIDTH,
          2 * CONV_WIDTH + ATTN_WIDTH + 2 * KV_WIDTH,
          2 * CONV_WIDTH + ATTN_WIDTH + 2 * KV_WIDTH + D_MODEL)
IN_WIDTH = 2 * CONV_WIDTH + ATTN_WIDTH + 2 * KV_WIDTH + 2 * D_MODEL

kernel_name = "hybrid_conv_axialgqa_hmoe_block"

def rmsnorm(x, g):
    xf = x.astype(jnp.float32)
    y = xf * lax.rsqrt(jnp.mean(xf * xf, axis=-1, keepdims=True) + EPS) * g.astype(jnp.float32)
    return y.astype(x.dtype)

def layernorm(x, g, b):
    xf = x.astype(jnp.float32)
    mu = jnp.mean(xf, axis=-1, keepdims=True)
    var = jnp.mean(jnp.square(xf - mu), axis=-1, keepdims=True)
    y = (xf - mu) * lax.rsqrt(var + EPS) * g.astype(jnp.float32) + b.astype(jnp.float32)
    return y.astype(x.dtype)

def depthwise_conv(u, w, b):
    pad = CONV_KSIZE // 2
    out = lax.conv_general_dilated(
        u, w[:, None, :].astype(u.dtype), window_strides=(1,), padding=[(pad, pad)],
        dimension_numbers=('NWC', 'WIO', 'NWC'), feature_group_count=u.shape[-1])
    return out + b.astype(u.dtype)

def axial_rope_angles(seq_len):
    rows = seq_len // GRID_W
    row_idx = jnp.repeat(jnp.arange(rows, dtype=jnp.int32), GRID_W).astype(jnp.float32)
    col_idx = jnp.tile(jnp.arange(GRID_W, dtype=jnp.int32), rows).astype(jnp.float32)
    inv_freq = ROPE_THETA ** (-jnp.arange(0, HALF_ROT, 2, dtype=jnp.float32) / HALF_ROT)
    return row_idx[:, None] * inv_freq, col_idx[:, None] * inv_freq

def rotate(xs, ang):
    cos = jnp.cos(ang)[None, :, None, :]
    sin = jnp.sin(ang)[None, :, None, :]
    x1, x2 = jnp.split(xs.astype(jnp.float32), 2, axis=-1)
    return jnp.concatenate([x1 * cos - x2 * sin, x2 * cos + x1 * sin], axis=-1).astype(xs.dtype)

def apply_axial_rope(x, ang_row, ang_col):
    xr, xc = jnp.split(x, 2, axis=-1)
    return jnp.concatenate([rotate(xr, ang_row), rotate(xc, ang_col)], axis=-1)

def axial_gqa_attention(q, k, v):
    B, S = q.shape[:2]
    nb = S // Q_BLOCK
    G = N_HEADS // N_KV_HEADS
    qb = q.reshape(B, nb, Q_BLOCK, N_KV_HEADS, G, HEAD_DIM).transpose(1, 0, 3, 4, 2, 5)
    kt = k.transpose(0, 2, 1, 3)
    vt = v.transpose(0, 2, 1, 3)
    scale = HEAD_DIM ** -0.5

    def block(qblk):
        s = jnp.einsum('bkgqd,bksd->bkgqs', qblk, kt).astype(jnp.float32) * scale
        p = jax.nn.softmax(s, axis=-1)
        return jnp.einsum('bkgqs,bksd->bkgqd', p.astype(vt.dtype), vt)

    o = lax.map(block, qb)
    return o.transpose(1, 0, 4, 2, 3, 5).reshape(B, S, ATTN_WIDTH)

def hierarchical_moe(h, w_group, b_group, w_router, b_router, w_gate, w_up, w_down):
    B, S, D = h.shape
    N = B * S
    xt = h.reshape(N, D)
    grp_prob = jax.nn.softmax((xt @ w_group).astype(jnp.float32) + b_group.astype(jnp.float32), axis=-1)
    grp_p, grp_idx = lax.top_k(grp_prob, 1)
    exp_logits = ((xt @ w_router).astype(jnp.float32) + b_router.astype(jnp.float32)).reshape(
        N, N_GROUPS, EXPERTS_PER_GROUP)
    in_grp = jnp.take_along_axis(exp_logits, grp_idx[:, :, None], axis=1)[:, 0]
    top_p, top_local = lax.top_k(jax.nn.softmax(in_grp, axis=-1), TOP_K)
    top_p = top_p / jnp.sum(top_p, axis=-1, keepdims=True)
    weights = grp_p * top_p
    expert_idx = grp_idx * EXPERTS_PER_GROUP + top_local

    A = N * TOP_K
    e_flat = expert_idx.reshape(A)
    w_flat = weights.reshape(A)
    tok_flat = jnp.arange(A, dtype=jnp.int32) // TOP_K
    order = jnp.argsort(e_flat)
    e_sorted = e_flat[order]
    counts = jnp.zeros((N_EXPERTS,), jnp.int32).at[e_flat].add(1)
    padded = (counts + MOE_BLOCK - 1) // MOE_BLOCK * MOE_BLOCK
    starts = jnp.cumsum(counts) - counts
    pends = jnp.cumsum(padded)
    pstarts = pends - padded
    dest = pstarts[e_sorted] + (jnp.arange(A, dtype=jnp.int32) - starts[e_sorted])
    P = A + N_EXPERTS * MOE_BLOCK
    n_blocks = P // MOE_BLOCK
    slot_tok = jnp.full((P,), N, jnp.int32).at[dest].set(tok_flat[order])
    slot_w = jnp.zeros((P,), jnp.float32).at[dest].set(w_flat[order])
    block_expert = jnp.minimum(
        jnp.searchsorted(pends, jnp.arange(n_blocks, dtype=jnp.int32) * MOE_BLOCK, side='right'),
        N_EXPERTS - 1).astype(jnp.int32)
    x_pad = jnp.concatenate([xt, jnp.zeros((1, D), xt.dtype)], axis=0)
    xb = x_pad[slot_tok].reshape(n_blocks, MOE_BLOCK, D)

    def expert_block(args):
        xblk, e = args
        return (jax.nn.silu(xblk @ w_gate[e]) * (xblk @ w_up[e])) @ w_down[e]

    yb = lax.map(expert_block, (xb, block_expert)).reshape(P, D)
    yb = yb * slot_w[:, None].astype(yb.dtype)
    y = jax.ops.segment_sum(yb, slot_tok, num_segments=N + 1)[:N]
    return y.reshape(B, S, D)

def setup_inputs(seed: int = 0) -> dict:
    key = jax.random.key(seed)
    ks = jax.random.split(key, 32)
    f32 = jnp.float32
    L, D = DEPTH, D_MODEL

    def nrm(k, shape, scale):
        return jax.random.normal(k, shape, f32) * scale

    def gain(k, shape):
        return 1.0 + 0.05 * jax.random.normal(k, shape, f32)

    return {
        "x": jax.random.normal(ks[0], (BATCH, SEQ, D), f32),
        "c": jax.random.normal(ks[1], (BATCH, D), f32),
        "w_ada": nrm(ks[2], (L, D, 6 * D), 0.5 * D ** -0.5),
        "b_ada": nrm(ks[3], (L, 6 * D), 0.02),
        "g_pre_mix": gain(ks[4], (L, D)),
        "g_post_mix": gain(ks[5], (L, D)),
        "w_in": nrm(ks[6], (L, D, IN_WIDTH), D ** -0.5),
        "w_dw": nrm(ks[7], (L, CONV_KSIZE, CONV_WIDTH), CONV_KSIZE ** -0.5),
        "b_dw": nrm(ks[8], (L, CONV_WIDTH), 0.02),
        "conv_ln_g": gain(ks[9], (L, CONV_WIDTH)),
        "conv_ln_b": nrm(ks[10], (L, CONV_WIDTH), 0.02),
        "w_conv_out": nrm(ks[11], (L, CONV_WIDTH, D), CONV_WIDTH ** -0.5),
        "q_norm_g": gain(ks[12], (L, HEAD_DIM)),
        "k_norm_g": gain(ks[13], (L, HEAD_DIM)),
        "w_attn_out": nrm(ks[14], (L, ATTN_WIDTH, D), ATTN_WIDTH ** -0.5),
        "w_out": nrm(ks[15], (L, D, D), D ** -0.5),
        "g_pre_ffn": gain(ks[16], (L, D)),
        "g_post_ffn": gain(ks[17], (L, D)),
        "w_group": nrm(ks[18], (L, D, N_GROUPS), D ** -0.5),
        "b_group": nrm(ks[19], (L, N_GROUPS), 0.01),
        "w_router": nrm(ks[20], (L, D, N_EXPERTS), D ** -0.5),
        "b_router": nrm(ks[21], (L, N_EXPERTS), 0.01),
        "w_e_gate": nrm(ks[22], (L, N_EXPERTS, D, D_EXPERT), D ** -0.5),
        "w_e_up": nrm(ks[23], (L, N_EXPERTS, D, D_EXPERT), D ** -0.5),
        "w_e_down": nrm(ks[24], (L, N_EXPERTS, D_EXPERT, D), D_EXPERT ** -0.5),
    }

def reference(x, c, w_ada, b_ada, g_pre_mix, g_post_mix, w_in, w_dw, b_dw, conv_ln_g, conv_ln_b,
              w_conv_out, q_norm_g, k_norm_g, w_attn_out, w_out, g_pre_ffn, g_post_ffn,
              w_group, b_group, w_router, b_router, w_e_gate, w_e_up, w_e_down):
    B, S, D = x.shape
    ang_row, ang_col = axial_rope_angles(S)
    for l in range(DEPTH):
        ada = jax.nn.silu(c) @ w_ada[l] + b_ada[l]
        sh1, sc1, gt1, sh2, sc2, gt2 = jnp.split(ada[:, None, :], 6, axis=-1)

        h = rmsnorm(x, g_pre_mix[l]) * (1.0 + sc1) + sh1
        z = h @ w_in[l]
        u_glu, q, k, v, g_conv, g_attn = jnp.split(z, SPLITS, axis=-1)

        a, ag = jnp.split(u_glu, 2, axis=-1)
        u = depthwise_conv(a * jax.nn.sigmoid(ag), w_dw[l], b_dw[l])
        u = layernorm(u, conv_ln_g[l], conv_ln_b[l])
        conv_out = jax.nn.silu(u) @ w_conv_out[l]

        q = apply_axial_rope(rmsnorm(q.reshape(B, S, N_HEADS, HEAD_DIM), q_norm_g[l]), ang_row, ang_col)
        k = apply_axial_rope(rmsnorm(k.reshape(B, S, N_KV_HEADS, HEAD_DIM), k_norm_g[l]), ang_row, ang_col)
        v = v.reshape(B, S, N_KV_HEADS, HEAD_DIM)
        attn_out = axial_gqa_attention(q, k, v) @ w_attn_out[l]

        merged = jax.nn.sigmoid(g_conv) * conv_out + jax.nn.sigmoid(g_attn) * attn_out
        x = x + gt1 * rmsnorm(merged @ w_out[l], g_post_mix[l])

        h = rmsnorm(x, g_pre_ffn[l]) * (1.0 + sc2) + sh2
        y = hierarchical_moe(h, w_group[l], b_group[l], w_router[l], b_router[l],
                             w_e_gate[l], w_e_up[l], w_e_down[l])
        x = x + gt2 * rmsnorm(y, g_post_ffn[l])
    return x


_drawn_inputs = setup_inputs


def setup_inputs(seed=0):
    import zlib

    import numpy as np

    out = dict(_drawn_inputs(seed))
    spreads = {}
    factors = {'q_norm_g': 4.602, 'k_norm_g': 5.433, 'g_post_ffn': 4.17, 'b_router': 3.945}
    for name, (base, spread) in spreads.items():
        noise = np.random.default_rng([zlib.crc32(name.encode()), seed]).standard_normal(out[name].shape)
        drawn = base * np.exp(spread * noise) if base else spread * noise
        out[name] = __import__('jax').numpy.asarray(drawn.astype(out[name].dtype))
    for name, factor in factors.items():
        out[name] = (out[name] * factor).astype(out[name].dtype)
    return out
```

```python
from contextlib import ExitStack

import concourse.bass as bass
import numpy as np
from concourse import mybir

F32 = mybir.dt.float32
I32 = mybir.dt.int32
U32 = mybir.dt.uint32
ACT = mybir.ActivationFunctionType
ALU = mybir.AluOpType
AX = mybir.AxisListType

P = 128
BANK = 512
S, D = 2048, 1024
HEADS, KV_HEADS, HEAD = 8, 2, 64
GRID_W, ROPE_THETA = 64, 10000.0
CONV, TAPS = 512, 31
GROUPS, PER_GROUP, D_EXPERT = 4, 8, 512
EXPERTS = GROUPS * PER_GROUP
EPS = 1e-6

NT = S // P
KD = D // P
KC = CONV // P
KF = D_EXPERT // P
CH = 512
NC = S // CH
ATT = HEADS * HEAD
KV = KV_HEADS * HEAD
QK = ATT + KV
ROWS = 4 * D // BANK
HALF = S // 2
PAD = TAPS // 2
BLOCKS = 2 * S // P + EXPERTS
LOGITS = GROUPS + EXPERTS
COL_GLU, COL_QKV, COL_GATE = 0, 2 * CONV, 2 * CONV + ATT + 2 * KV
BIG = 1.0e30


class Arena:

    def __init__(self, tensor, size):
        self.tensor, self.size, self.at = tensor, size, 0

    def take(self, *shape):
        n = int(np.prod(shape))
        view = self.tensor[:, self.at:self.at + n]
        self.at += (n + 7) // 8 * 8
        assert self.at <= self.size, (self.at, self.size)
        if len(shape) > 1:
            names = "abcd"[:len(shape)]
            view = view.rearrange(f"p ({' '.join(names)}) -> p {' '.join(names)}",
                                  **{n: s for n, s in zip(names[1:], shape[1:])})
        return view


class Order:

    def __init__(self, eng, sem, turn=0, per=0, base=0):
        self.eng, self.sem, self.n = eng, sem, turn * per + base
        self.k = 0

    def link(self, ins):
        ins.then_inc(self.sem, 1)
        self.k += 1
        self.eng.wait_ge(self.sem, self.n + self.k)


def encoder_block(nc, t, out):
    ctx = ExitStack()
    with ctx:
        def dram(name, shape, dt=F32):
            return nc.dram_tensor(name, shape, dt, kind="Internal").ap()

        ARENA = 53200
        arena = Arena(ctx.enter_context(nc.sbuf_tensor("arena", [P, ARENA], F32)), ARENA)
        banks = ctx.enter_context(nc.psum_tensor("banks", [P, 8, BANK], F32))
        take = arena.take

        def wide(b, n):
            return banks[:, b:b + (n + BANK - 1) // BANK, :].rearrange("p a b -> p (a b)")[:, 0:n]

        qk_scr = dram("qk_scr", [NT, P, ATT + 2 * KV])
        q_scr = dram("q_scr", [NT + 1, P, ATT])
        gate_scr = dram("gate_scr", [2 * KD, P, S])
        o_scr = dram("o_scr", [NT, P, ATT])
        x1_scr = dram("x1_scr", [S, D])
        h2_scr = dram("h2_scr", [S, D])
        y_scr = dram("y_scr", [BLOCKS * P, D])

        ident = take(P)
        ones = take(P)
        mean_w = take(P)
        before = take(P)
        eps_t = take(1)
        c_col = take(KD)
        c_silu = take(KD)
        vec = take(24)
        shift1 = take(KD)
        scale1 = take(KD)
        rbias = take(LOGITS)
        logits = take(NT, LOGITS)
        conv_g, conv_b, dw_b = take(KC), take(KC), take(KC)
        dw_w = take(KC, TAPS)
        kv_at = arena.at
        v_sb = take(NT, KV)
        kT = take(KV_HEADS, S)
        early = arena.at
        hT = take(KD, S)
        after_hT = arena.at
        conv = take(KC, S)
        after_conv = arena.at
        rows = take(4, D)
        after_rows = arena.at

        arena.at = early
        ada_w = [take(KD, D) for _ in range(2)]
        arena.at = after_hT
        xt = [take(D) for _ in range(2)]
        junk = take(D)
        hs = [take(KD, P) for _ in range(2)]
        w_qkv = take(KD, ATT + 2 * KV)
        qk = [take(QK) for _ in range(2)]
        sq = take(QK)
        rot = take(QK)
        roped = [take(ATT + 2 * KV) for _ in range(2)]
        gain = take(QK)
        cos_t, sin_t = take(NT, HEAD), take(NT, HEAD)
        st = [take(2) for _ in range(2)]
        hst = [take(2 * (HEADS + KV_HEADS)) for _ in range(2)]

        tin = [take(ATT + 2 * KV) for _ in range(2)]
        qout = [take(ATT) for _ in range(2)]
        end_turn = arena.at

        arena.at = after_rows
        wcol = [take(KD, P) for _ in range(2)]
        glu = take(S + 2 * PAD)
        sg = take(S)
        gate_out = [take(S) for _ in range(2)]

        end_gates = arena.at
        w_ada_row = [take(KD, BANK)]
        arena.at = early
        w_ada_row.append(take(KD, BANK))
        gains = take(3, D)
        c_wide = sg[:, 0:KD * P].rearrange("p (k n) -> p k n", n=P)

        arena.at = after_rows
        UNITS = 2 * HEADS
        qb = take(ATT // P, P)
        prob = [take(HALF) for _ in range(2)]
        probT = [take(BANK) for _ in range(2)]
        neg_max, total = take(UNITS), take(UNITS)
        neg_top, fade, mass, norm, share = take(4), take(8), take(8), take(4), take(8)
        o_parts = take(8, HEAD)
        o_out = take(2, 4, HEAD)

        arena.at = early
        w_co = take(KC, D)
        w_ao = take(KC, D)
        w_o = take(KD, D)
        assert arena.at <= after_hT
        arena.at = kv_at
        o_in = take(CH // P, ATT)
        oT = take(KC, CH)
        cT = take(KC, CH)
        assert arena.at <= early
        squares = o_in.rearrange("p a b -> p (a b)").rearrange("p (k n) -> p k n", n=CH)
        arena.at = after_rows
        gate_a = take(KD, CH)
        gate_c = take(KD, CH)
        inv_dev = take(CH)
        xm = [take(D) for _ in range(2)]
        ym = [take(D) for _ in range(2)]
        h2T = take(KD, P)
        w_r = take(KD, LOGITS)
        mst = [take(4) for _ in range(2)]

        arena.at = after_rows
        iota = take(P)
        iota_i = take(P).bitcast(I32)
        token = take(NT)
        token_i = take(NT).bitcast(I32)
        slots_of = take(2, NT)
        slots_i = take(2, NT).bitcast(I32)
        slots_hi = take(2, NT)
        slots_lo = take(2, NT)
        weights = take(2, NT)
        block_expert = take(BLOCKS)
        block_expert_i = take(BLOCKS).bitcast(I32)
        LISTS = BLOCKS + 2
        slot_token = take(LISTS).bitcast(I32)
        in_block = [take(P) for _ in range(2)]
        of_block = [take(LISTS) for _ in range(2)]
        zeros = take(P)
        after_route = arena.at
        top_g, sum_g, exp_g = take(NT), take(NT), take(NT, GROUPS)
        hot_g, cand_g, first_g = take(NT, GROUPS), take(NT, GROUPS), take(NT)
        masked = take(NT, EXPERTS)
        cand = take(NT, EXPERTS)
        hot = [take(NT, EXPERTS) for _ in range(2)]
        picked = take(NT, EXPERTS)
        top, first = [take(NT) for _ in range(2)], take(NT)
        ratio = take(NT)
        base = take(NT + 1, EXPERTS)
        blocks_of = take(EXPERTS, NT)
        run = [take(EXPERTS) for _ in range(2)]
        counts = take(EXPERTS)
        started = arena.at
        reached = take(BLOCKS, EXPERTS)

        arena.at = early
        w_g = [take(KD, D_EXPERT) for _ in range(2)]
        w_u = [take(KD, D_EXPERT) for _ in range(2)]
        w_d = [take(KF, D) for _ in range(2)]
        assert arena.at <= after_conv
        arena.at = after_route
        xg = [take(D) for _ in range(2)]
        xT = [take(KD, P) for _ in range(2)]
        act_g = take(D_EXPERT)
        act_u = take(D_EXPERT)
        actT = take(KF, P)
        ys = [take(D) for _ in range(2)]

        arena.at = early
        yj = [[take(D) for _ in range(2)] for _ in range(2)]
        xj = [take(D) for _ in range(2)]
        jjunk = take(D)
        jst = [take(2) for _ in range(2)]

        x_v = t["x"].rearrange("a (t p) d -> (a t) p d", p=P)
        w_ada_v = t["w_ada"].rearrange("l (k p) n -> p (l k) n", p=P)
        w_in_v = t["w_in"].rearrange("l (k p) n -> p (l k) n", p=P)
        out_v = out.rearrange("a (t p) d -> (a t) p d", p=P)

        def col(ap1d, n):
            return ap1d.rearrange("(k p) -> p k", p=P)

        def end_phase(sems):
            nc.clear_and_free_semaphores(sems)
            nc.all_engine_barrier()

        def project():
            sems = []
            with ExitStack() as own:
                def sem(name):
                    sems.append(nc.alloc_semaphore(name))
                    return sems[-1]

                s_const = sem("s_const")
                s_vec = sem("s_vec")
                s_convvec = sem("s_convvec")
                s_rows = sem("s_rows")
                s_csilu = sem("s_csilu")
                s_wada = [sem(f"s_wada{n}") for n in range(2)]
                s_ada_mm = sem("s_ada_mm")
                s_ada_col = sem("s_ada_col")
                s_x = [sem(f"s_x{s}") for s in range(2)]
                s_xss = [sem(f"s_xss{s}") for s in range(2)]
                s_xroot = [sem(f"s_xroot{s}") for s in range(2)]
                s_xn = [sem(f"s_xn{s}") for s in range(2)]
                s_xT = [sem(f"s_xT{s}") for s in range(2)]
                s_hs_a = [sem(f"s_hs_a{s}") for s in range(2)]
                s_hs_v = [sem(f"s_hs_v{s}") for s in range(2)]
                s_hT = [sem(f"s_hT{s}") for s in range(2)]
                s_qkv = [sem(f"s_qkv{s}") for s in range(2)]
                s_qkc = [sem(f"s_qkc{s}") for s in range(2)]
                s_hss = [sem(f"s_hss{s}") for s in range(2)]
                s_hroot = [sem(f"s_hroot{s}") for s in range(2)]
                s_rope = [sem(f"s_rope{s}") for s in range(2)]
                s_ropeout = [sem(f"s_ropeout{s}") for s in range(2)]
                s_wqkv = sem("s_wqkv")
                s_tab = sem("s_tab")
                o_gain = sem("o_gain")
                o_act1 = sem("o_act1")
                o_dve1 = sem("o_dve1")
                s_tin = [sem(f"s_tin{s}") for s in range(2)]
                s_tT = [sem(f"s_tT{s}") for s in range(2)]
                s_tq = [sem(f"s_tq{s}") for s in range(2)]
                s_tk = [sem(f"s_tk{s}") for s in range(2)]
                s_tout = [sem(f"s_tout{s}") for s in range(2)]
                s_wcol = [sem(f"s_wcol{s}") for s in range(2)]
                s_zT = [sem(f"s_zT{s}") for s in range(2)]
                s_sg = sem("s_sg")
                s_glu = sem("s_glu")
                s_pad = sem("s_pad")
                o_conv = sem("o_conv")
                s_conv = sem("s_conv")
                s_gateev = [sem(f"s_gateev{s}") for s in range(2)]
                s_gateout = [sem(f"s_gateout{s}") for s in range(2)]
                s_brow = sem("s_brow")
                s_gains = sem("s_gains")
                s_warow = [sem(f"s_warow{s}") for s in range(2)]
                s_cwide = sem("s_cwide")
                s_arow = [sem(f"s_arow{s}") for s in range(2)]
                s_rowadd = [sem(f"s_rowadd{s}") for s in range(2)]
                o_rows = sem("o_rows")
                block = own.enter_context(nc.Block())

                @block.sync
                def _(sp):
                    with nc.allow_non_contiguous_dma(reason="short vectors as columns"):
                        sp.dma_start(c_col, col(t["c"][0], KD)).then_inc(s_vec, 16)
                        sp.dma_start(vec[:, 0:16], col(t["b_ada"][0, 0:2 * D], 16)).then_inc(s_vec, 16)
                        sp.dma_start(vec[:, 16:24], col(t["g_pre_mix"][0], KD)).then_inc(s_vec, 16)
                    for n in range(2):
                        sp.dma_start(ada_w[n], w_ada_v[:, :, n * D:(n + 1) * D]).then_inc(s_wada[n], 16)
                    sp.dma_start(gain[:, 0:HEAD], t["q_norm_g"][0:1, :].to_broadcast([P, HEAD])).then_inc(s_tab, 16)
                    sp.dma_start(gain[:, ATT:ATT + HEAD], t["k_norm_g"][0:1, :].to_broadcast([P, HEAD])).then_inc(s_tab, 16)
                    sp.dma_start(cos_t, t["rope_cos"].rearrange("(t p) n -> p t n", p=P)).then_inc(s_tab, 16)
                    sp.dma_start(sin_t, t["rope_sin"].rearrange("(t p) n -> p t n", p=P)).then_inc(s_tab, 16)
                    sp.dma_start(w_qkv, w_in_v[:, :, COL_QKV:COL_GATE]).then_inc(s_wqkv, 16)
                    with nc.allow_non_contiguous_dma(reason="short vectors as columns"):
                        sp.dma_start(dw_b, col(t["b_dw"][0], KC)).then_inc(s_convvec, 16)
                        sp.dma_start(conv_g, col(t["conv_ln_g"][0], KC)).then_inc(s_convvec, 16)
                        sp.dma_start(conv_b, col(t["conv_ln_b"][0], KC)).then_inc(s_convvec, 16)
                        for k in range(KC):
                            sp.dma_start(dw_w[:, k, :], t["w_dw"][0, :, k * P:(k + 1) * P].rearrange("j p -> p j")
                                         ).then_inc(s_convvec, 16)
                    with sp.Fori(0, NT // 2) as i:
                        for s in range(2):
                            sp.wait_ge(s_xT[s], i)
                            sp.dma_start(xt[s], x_v[2 * i + s]).then_inc(s_x[s], 16)
                        for s in range(2):
                            sp.wait_ge(s_hs_a[s], i + 1)
                            sp.wait_ge(s_hs_v[s], i + 1)
                            if s == 0:
                                sp.wait_ge(s_ada_mm, 16)
                            sp.dma_start(hT[:, :, bass.ts(2 * i + s, P)], hs[s]).then_inc(s_hT[s], 16)
                        for s in range(2):
                            sp.wait_ge(s_rope[s], 2 * i + 2)
                            sp.dma_start(qk_scr[2 * i + s], roped[s]).then_inc(s_ropeout[s], 16)
                    sp.wait_ge(s_ropeout[0], 16 * (NT // 2))
                    sp.wait_ge(s_ropeout[1], 16 * (NT // 2))
                    with sp.Fori(0, NT // 2) as i:
                        for s in range(2):
                            sp.wait_ge(s_tT[s], i)
                            sp.dma_start(tin[s], qk_scr[2 * i + s]).then_inc(s_tin[s], 16)
                        for s in range(2):
                            sp.wait_ge(s_tq[s], i + 1)
                            sp.dma_start(q_scr[2 * i + s], qout[s]).then_inc(s_tout[s], 16)
                    sp.dma_start(q_scr[NT], qout[1]).then_inc(s_tout[1], 16)
                    sp.wait_ge(s_hT[0], 16 * (NT // 2))
                    with sp.Fori(0, KC) as m:
                        for s in range(2):
                            sp.wait_ge(s_zT[s], m)
                            sp.dma_start(wcol[s], w_in_v[:, :, bass.ds(m * P + s * CONV, P)]).then_inc(s_wcol[s], 16)
                    with sp.Fori(0, KD) as m:
                        for s in range(2):
                            sp.wait_ge(s_zT[s], m + KC)
                            sp.dma_start(wcol[s], w_in_v[:, :, bass.ds(m * 2 * P + s * P + COL_GATE, P)]
                                         ).then_inc(s_wcol[s], 16)
                        for s in range(2):
                            sp.wait_ge(s_gateev[s], m + 1)
                            sp.dma_start(gate_scr[2 * m + s], gate_out[s]).then_inc(s_gateout[s], 16)

                    w_row_v = w_ada_v[:, :, 2 * D:6 * D]
                    sp.dma_start(rows.rearrange("p a b -> p (a b)"),
                                 t["b_ada"][0:1, 2 * D:6 * D].to_broadcast([P, 4 * D])).then_inc(s_brow, 16)
                    sp.wait_ge(s_zT[0], KC + KD)
                    sp.wait_ge(s_zT[1], KC + KD)
                    for n, name in enumerate(("g_post_mix", "g_pre_ffn", "g_post_ffn")):
                        sp.dma_start(gains[:, n, :], t[name][0:1, :].to_broadcast([P, D])).then_inc(s_gains, 16)
                    with sp.Fori(0, ROWS // 2) as i:
                        for s in range(2):
                            sp.wait_ge(s_arow[s], i)
                            sp.dma_start(w_ada_row[s], w_row_v[:, :, bass.ts(2 * i + s, BANK)]).then_inc(s_warow[s], 16)
                    sp.wait_ge(s_tout[0], 16 * (NT // 2))
                    sp.wait_ge(s_tout[1], 16 * (NT // 2) + 16)
                    for s in range(2):
                        sp.wait_ge(s_gateout[s], 16 * KD)

                @block.gpsimd
                def _(pool):
                    order = Order(pool, sem("o_pool"))
                    order.link(nc.gpsimd.memset(ident, 0.0))
                    nc.gpsimd.affine_select(out=ident, in_=ident, compare_op=ALU.not_equal, fill=1.0, base=0,
                                            pattern=[[-1, P]], channel_multiplier=1).then_inc(s_const, 1)
                    nc.gpsimd.memset(ones, 1.0).then_inc(s_const, 1)
                    nc.gpsimd.memset(mean_w, 1.0 / CONV).then_inc(s_const, 1)
                    nc.gpsimd.memset(eps_t, EPS).then_inc(s_const, 1)
                    order.link(nc.gpsimd.memset(before, 1.0))
                    nc.gpsimd.affine_select(out=before, in_=before, compare_op=ALU.is_gt, fill=0.0, base=0,
                                            pattern=[[1, P]], channel_multiplier=-1).then_inc(s_const, 1)

                @block.scalar
                def _(act):
                    act.wait_ge(s_vec, 48)
                    nc.scalar.activation(c_silu, c_col, ACT.Silu).then_inc(s_csilu, 1)
                    act.wait_ge(s_const, 5)
                    with act.Fori(0, NT // 2) as i:
                        order = Order(act, o_act1, i, 2)
                        for s in range(2):
                            act.wait_ge(s_x[s], 16 * i + 16)
                            order.link(nc.scalar.activation(junk, xt[s], ACT.Square, accum_out=st[s][:, 0:1]))
                            nc.scalar.activation(st[s][:, 1:2], st[s][:, 0:1], ACT.Sqrt, bias=eps_t, scale=1.0 / D
                                                 ).then_inc(s_xroot[s], 1)
                        for s in range(2):
                            act.wait_ge(s_xT[s], i + 1)
                            act.wait_ge(s_qkv[s], i)
                            act.wait_ge(s_hT[s], 16 * i)
                            for k in range(KD // 2):
                                ins = nc.scalar.activation(hs[s][:, k, :], wide(2 * s, D)[:, k * P:(k + 1) * P],
                                                           ACT.Identity, bias=shift1[:, k:k + 1], scale=scale1[:, k:k + 1])
                            ins.then_inc(s_hs_a[s], 1)
                        for s in range(2):
                            act.wait_ge(s_qkv[s], i + 1)
                            act.wait_ge(s_rope[s], 2 * i)
                            nc.scalar.activation(qk[s], wide(4 + 2 * s, QK), ACT.Copy).then_inc(s_qkc[s], 1)
                            nc.scalar.activation(v_sb[:, 2 * i + s, :], wide(4 + 2 * s, QK + KV)[:, QK:QK + KV], ACT.Copy
                                                 ).then_inc(s_qkc[s], 1)
                            if s == 1:
                                act.wait_ge(s_hss[0], i + 1)
                            else:
                                act.wait_ge(s_hss[1], i)
                            nc.scalar.activation(sq, wide(4 + 2 * s, QK), ACT.Square).then_inc(s_qkc[s], 1)
                            act.wait_ge(s_hss[s], i + 1)
                            nc.scalar.activation(hst[s][:, 10:20], hst[s][:, 0:10], ACT.Sqrt, bias=eps_t,
                                                 scale=1.0 / HEAD).then_inc(s_hroot[s], 1)
                    with act.Fori(0, NT // 2) as i:
                        for s in range(2):
                            act.wait_ge(s_tT[s], i + 1)
                            nc.scalar.activation(kT[:, :, bass.ts(2 * i + s, P)],
                                                 banks[:, 2 * s + 1, 0:2 * P].rearrange("p (g n) -> p g n", g=2),
                                                 ACT.Copy).then_inc(s_tk[s], 1)
                    with act.Fori(0, KC) as m:
                        act.wait_ge(s_zT[1], m + 1)
                        act.wait_ge(s_glu, m)
                        nc.scalar.activation(sg, wide(4, S), ACT.Sigmoid).then_inc(s_sg, 1)
                    with act.Fori(0, KD) as m:
                        for s in range(2):
                            act.wait_ge(s_zT[s], m + KC + 1)
                            act.wait_ge(s_gateout[s], 16 * m)
                            nc.scalar.activation(gate_out[s], wide(4 * s, S), ACT.Sigmoid).then_inc(s_gateev[s], 1)

                @block.vector
                def _(dve):
                    order = Order(dve, sem("o_dve0"))
                    dve.wait_ge(s_ada_mm, 16)
                    dve.wait_ge(s_vec, 48)
                    order.link(nc.vector.tensor_tensor(shift1, banks[:, 0, 0:KD], vec[:, 0:KD], ALU.add))
                    order.link(nc.vector.tensor_tensor(scale1, banks[:, 0, KD:2 * KD], vec[:, KD:2 * KD], ALU.add))
                    order.link(nc.vector.scalar_tensor_tensor(out=scale1, in0=scale1, scalar=1.0, in1=vec[:, 16:24],
                                                              op0=ALU.add, op1=ALU.mult))
                    dve.wait_ge(s_tab, 64)
                    order.link(nc.vector.tensor_scalar(gain[:, HEAD:2 * HEAD], gain[:, 0:HEAD], HEAD ** -0.5, None, ALU.mult))
                    order.link(nc.vector.tensor_copy(gain[:, 0:HEAD], gain[:, HEAD:2 * HEAD]))
                    for h in range(2, HEADS):
                        nc.vector.tensor_copy(gain[:, h * HEAD:(h + 1) * HEAD], gain[:, HEAD:2 * HEAD])
                    order.link(nc.vector.tensor_copy(gain[:, ATT + HEAD:ATT + 2 * HEAD], gain[:, ATT:ATT + HEAD]))

                    def heads(ap):
                        return ap.rearrange("p (h d) -> p h d", d=HEAD)

                    with dve.Fori(0, NT // 2) as i:
                        order = Order(dve, o_dve1, i, 14)
                        for s in range(2):
                            dve.wait_ge(s_xroot[s], i + 1)
                            order.link(nc.vector.reciprocal(st[s][:, 0:1], st[s][:, 1:2]))
                            nc.vector.tensor_scalar(xt[s], xt[s], st[s][:, 0:1], None, ALU.mult).then_inc(s_xn[s], 1)
                        for s in range(2):
                            dve.wait_ge(s_xT[s], i + 1)
                            dve.wait_ge(s_qkv[s], i)
                            dve.wait_ge(s_hT[s], 16 * i)
                            for k in range(KD // 2, KD):
                                ins = nc.vector.tensor_scalar(hs[s][:, k, :], wide(2 * s, D)[:, k * P:(k + 1) * P],
                                                              scale1[:, k:k + 1], shift1[:, k:k + 1], ALU.mult, ALU.add)
                            ins.then_inc(s_hs_v[s], 1)
                        for s in range(2):
                            dve.wait_ge(s_qkc[s], 3 * i + 3)
                            nc.vector.tensor_reduce(hst[s][:, 0:10], heads(sq), AX.X, ALU.add).then_inc(s_hss[s], 1)
                            dve.wait_ge(s_hroot[s], i + 1)
                            order.link(nc.vector.reciprocal(hst[s][:, 0:10], hst[s][:, 10:20]))
                            order.link(nc.vector.tensor_tensor(
                                heads(qk[s]), heads(qk[s]),
                                hst[s][:, 0:10].rearrange("p (h o) -> p h o", o=1).to_broadcast([P, 10, HEAD]), ALU.mult))
                            order.link(nc.vector.tensor_tensor(qk[s], qk[s], gain, ALU.mult))
                            pairs = qk[s].rearrange("p (h a b n) -> p h a b n", h=10, a=2, b=2)
                            turned = rot.rearrange("p (h a b n) -> p h a b n", h=10, a=2, b=2)
                            sins = sin_t[:, 2 * i + s, :].rearrange("p (o a b n) -> p o a b n", o=1, a=2, b=2)
                            for b in range(2):
                                order.link(nc.vector.tensor_tensor(turned[:, :, :, b, :], pairs[:, :, :, 1 - b, :],
                                                                   sins[:, :, :, b, :].to_broadcast([P, 10, 2, 16]), ALU.mult))
                            cosb = cos_t[:, 2 * i + s, :].rearrange("p (o d) -> p o d", o=1)
                            order.link(nc.vector.tensor_tensor(heads(qk[s]), heads(qk[s]), cosb.to_broadcast([P, 10, HEAD]),
                                                               ALU.mult))
                            dve.wait_ge(s_ropeout[s], 16 * i)
                            nc.vector.tensor_tensor(roped[s][:, 0:ATT], qk[s][:, 0:ATT], rot[:, 0:ATT], ALU.add
                                                    ).then_inc(s_rope[s], 1)
                            kk = [a[:, ATT:QK].rearrange("p (g o d) -> p g o d", g=2, o=1).to_broadcast([P, 2, 2, HEAD])
                                  for a in (qk[s], rot)]
                            nc.vector.tensor_tensor(roped[s][:, ATT:].rearrange("p (g o d) -> p g o d", g=2, o=2),
                                                    kk[0], kk[1], ALU.add).then_inc(s_rope[s], 1)
                            dve.wait_ge(s_rope[s], 2 * i + 2)
                    with dve.Fori(0, NT // 2) as i:
                        for s in range(2):
                            dve.wait_ge(s_tT[s], i + 1)
                            dve.wait_ge(s_tout[s], 16 * i)
                            nc.vector.tensor_copy(qout[s], banks[:, 2 * s, :]).then_inc(s_tq[s], 1)
                    nc.vector.memset(glu[:, 0:PAD], 0.0).then_inc(s_pad, 1)
                    nc.vector.memset(glu[:, PAD + S:], 0.0).then_inc(s_pad, 1)
                    dve.wait_ge(s_pad, 2)
                    dve.wait_ge(s_convvec, 16 * (3 + KC))
                    with dve.Fori(0, KC) as m:
                        order = Order(dve, o_conv, m, TAPS)
                        dve.wait_ge(s_sg, m + 1)
                        dve.wait_ge(s_zT[0], m + 1)
                        nc.vector.tensor_tensor(glu[:, PAD:PAD + S], wide(0, S), sg, ALU.mult).then_inc(s_glu, 1)
                        dve.wait_ge(s_glu, m + 1)
                        order.link(nc.vector.tensor_scalar(conv[:, m, :], glu[:, 0:S], dw_w[:, m, 0:1], dw_b[:, bass.ds(m, 1)],
                                                           ALU.mult, ALU.add))
                        for j in range(1, TAPS):
                            order.link(nc.vector.scalar_tensor_tensor(
                                out=conv[:, m, :], in0=glu[:, j:j + S], scalar=dw_w[:, m, j:j + 1], in1=conv[:, m, :],
                                op0=ALU.mult, op1=ALU.add))

                    for k in range(KD):
                        ins = nc.vector.tensor_scalar(c_wide[:, k, :], ones, c_silu[:, k:k + 1], None, ALU.mult)
                    ins.then_inc(s_cwide, 1)
                    row_banks = rows.rearrange("p a (b n) -> p (a b) n", n=BANK)
                    dve.wait_ge(s_brow, 16)
                    with dve.Fori(0, ROWS // 2) as i:
                        for s in range(2):
                            dve.wait_ge(s_arow[s], i + 1)
                            nc.vector.tensor_tensor(row_banks[:, 2 * i + s, :], banks[:, s, :], row_banks[:, 2 * i + s, :],
                                                    ALU.add).then_inc(s_rowadd[s], 1)
                    order = Order(dve, o_rows)
                    dve.wait_ge(s_gains, 48)
                    for s in range(2):
                        dve.wait_ge(s_rowadd[s], ROWS // 2)
                    order.link(nc.vector.tensor_tensor(rows[:, 0, :], rows[:, 0, :], gains[:, 0, :], ALU.mult))
                    order.link(nc.vector.scalar_tensor_tensor(out=rows[:, 2, :], in0=rows[:, 2, :], scalar=1.0,
                                                              in1=gains[:, 1, :], op0=ALU.add, op1=ALU.mult))
                    order.link(nc.vector.tensor_tensor(rows[:, 3, :], rows[:, 3, :], gains[:, 2, :], ALU.mult))

                @block.tensor
                def _(pe):
                    pe.wait_ge(s_csilu, 1)
                    for n in range(16):
                        if n % KD == 0:
                            pe.wait_ge(s_wada[n // KD], 16)
                        for k in range(KD):
                            ins = nc.tensor.matmul(banks[:, 0, n:n + 1], ada_w[n // KD][:, k, (n % KD) * P:(n % KD + 1) * P],
                                                   c_silu[:, k:k + 1], start=(k == 0), stop=(k == KD - 1))
                        ins.then_inc(s_ada_mm, 1)
                    pe.wait_ge(s_const, 5)
                    pe.wait_ge(s_wqkv, 16)
                    with pe.Fori(0, NT // 2) as i:
                        for s in range(2):
                            pe.wait_ge(s_xn[s], i + 1)
                            pe.wait_ge(s_hs_a[s], i)
                            pe.wait_ge(s_hs_v[s], i)
                            for k in range(KD):
                                ins = nc.tensor.transpose(wide(2 * s, D)[:, k * P:(k + 1) * P], xt[s][:, k * P:(k + 1) * P],
                                                          ident)
                            ins.then_inc(s_xT[s], 1)
                        for s in range(2):
                            pe.wait_ge(s_hs_a[s], i + 1)
                            pe.wait_ge(s_hs_v[s], i + 1)
                            pe.wait_ge(s_qkc[s], 3 * i)
                            for k in range(KD):
                                nc.tensor.matmul(banks[:, 4 + 2 * s, :], hs[s][:, k, :], w_qkv[:, k, 0:ATT],
                                                 start=(k == 0), stop=(k == KD - 1))
                            for k in range(KD):
                                ins = nc.tensor.matmul(banks[:, 5 + 2 * s, 0:2 * KV], hs[s][:, k, :],
                                                       w_qkv[:, k, ATT:ATT + 2 * KV], start=(k == 0), stop=(k == KD - 1))
                            ins.then_inc(s_qkv[s], 1)
                    with pe.Fori(0, NT // 2) as i:
                        for s in range(2):
                            pe.wait_ge(s_tin[s], 16 * i + 16)
                            pe.wait_ge(s_tq[s], i)
                            pe.wait_ge(s_tk[s], i)
                            for j in range(6):
                                ins = nc.tensor.transpose(wide(2 * s, 6 * P)[:, j * P:(j + 1) * P],
                                                          tin[s][:, j * P:(j + 1) * P], ident)
                            ins.then_inc(s_tT[s], 1)
                    pe.wait_ge(s_hT[0], 16 * (NT // 2))
                    pe.wait_ge(s_hT[1], 16 * (NT // 2))
                    pe.wait_ge(s_tq[1], NT // 2)
                    pe.wait_ge(s_tk[1], NT // 2)

                    def project(s, turn):
                        pe.wait_ge(s_wcol[s], 16 * turn + 16)
                        for k in range(KD):
                            for n in range(S // BANK):
                                ins = nc.tensor.matmul(banks[:, 4 * s + n, :], wcol[s][:, k, :],
                                                       hT[:, k, n * BANK:(n + 1) * BANK], start=(k == 0), stop=(k == KD - 1))
                        ins.then_inc(s_zT[s], 1)

                    with pe.Fori(0, KC) as m:
                        for s in range(2):
                            pe.wait_ge(s_glu, m)
                            project(s, m)
                    with pe.Fori(0, KD) as m:
                        for s in range(2):
                            pe.wait_ge(s_glu, KC)
                            pe.wait_ge(s_gateev[s], m)
                            project(s, m + KC)
                    pe.wait_ge(s_cwide, 1)
                    for s in range(2):
                        pe.wait_ge(s_gateev[s], KD)
                    with pe.Fori(0, ROWS // 2) as i:
                        for s in range(2):
                            pe.wait_ge(s_warow[s], 16 * i + 16)
                            pe.wait_ge(s_rowadd[s], i)
                            for k in range(KD):
                                ins = nc.tensor.matmul(banks[:, s, :], c_wide[:, k, :], w_ada_row[s][:, k, :],
                                                       start=(k == 0), stop=(k == KD - 1))
                            ins.then_inc(s_arow[s], 1)
                    for s in range(2):
                        pe.wait_ge(s_rowadd[s], ROWS // 2)

            end_phase(sems)

        def attend():
            sems = []
            with ExitStack() as own:
                def sem(name):
                    sems.append(nc.alloc_semaphore(name))
                    return sems[-1]

                s_q = [sem(f"s_q{p}") for p in range(4)]
                s_qk = [sem(f"s_qk{s}") for s in range(2)]
                s_max = [sem(f"s_max{s}") for s in range(2)]
                s_exp = [sem(f"s_exp{s}") for s in range(2)]
                s_pT = [sem(f"s_pT{g}") for g in range(2)]
                s_pTe = [sem(f"s_pTe{g}") for g in range(2)]
                s_pv = [sem(f"s_pv{g}") for g in range(2)]
                s_fade = [sem(f"s_fade{g}") for g in range(2)]
                s_faded = [sem(f"s_faded{g}") for g in range(2)]
                s_oread = [sem(f"s_oread{g}") for g in range(2)]
                s_osum = [sem(f"s_osum{g}") for g in range(2)]
                s_oout = [sem(f"s_oout{g}") for g in range(2)]
                o_join = sem("o_join")
                s_wmerge = sem("s_wmerge")
                s_rb = sem("s_rb")
                s_oin = sem("s_oin")
                s_ga, s_gc = sem("s_ga"), sem("s_gc")
                s_mu, s_centred, s_sq, s_var, s_dev = sem("s_mu"), sem("s_centred"), sem("s_sq"), sem("s_var"), sem("s_dev")
                s_cnorm, s_cT = sem("s_cnorm"), sem("s_cT")
                s_oT = sem("s_oT")
                s_oTa, s_oTv = sem("s_oTa"), sem("s_oTv")
                s_branch = [sem(f"s_branch{b}") for b in range(2)]
                s_used = [sem(f"s_used{b}") for b in range(2)]
                s_merged = sem("s_merged")
                s_wout = [sem(f"s_wout{b}") for b in range(2)]
                s_xm = [sem(f"s_xm{b}") for b in range(2)]
                s_ydev = [sem(f"s_ydev{b}") for b in range(2)]
                s_x1 = [sem(f"s_x1{b}") for b in range(2)]
                s_x1out = [sem(f"s_x1out{b}") for b in range(2)]
                s_x1dev = [sem(f"s_x1dev{b}") for b in range(2)]
                s_h2 = [sem(f"s_h2{b}") for b in range(2)]
                s_h2out = [sem(f"s_h2out{b}") for b in range(2)]
                s_h2T, s_h2Ta, s_h2Tv = sem("s_h2T"), sem("s_h2Ta"), sem("s_h2Tv")
                s_logit, s_logitc = sem("s_logit"), sem("s_logitc")
                o_merge, o_mact = sem("o_merge"), sem("o_mact")
                block = own.enter_context(nc.Block())

                @block.sync
                def _(sp):
                    for p in range(4):
                        sp.dma_start(qb[:, p, :], q_scr[0][:, p * P:(p + 1) * P]).then_inc(s_q[p], 16)
                    for w, name in ((w_co, "w_conv_out"), (w_ao, "w_attn_out"), (w_o, "w_out")):
                        sp.dma_start(w, t[name].rearrange("l (k p) n -> p (l k) n", p=P)).then_inc(s_wmerge, 16)
                    with sp.Fori(0, NT) as i:
                        for p in range(4):
                            sp.wait_ge(s_qk[1], 8 * i + 2 * p + 2)
                            sp.dma_start(qb[:, p, :], q_scr[i + 1][:, p * P:(p + 1) * P]).then_inc(s_q[p], 16)
                            if p == 3:
                                for g in range(2):
                                    sp.wait_ge(s_osum[g], i + 1)
                                    sp.dma_start(o_scr[i][:, g * 4 * HEAD:(g + 1) * 4 * HEAD],
                                                 o_out[:, g].rearrange("p a b -> p (a b)")).then_inc(s_oout[g], 16)
                    for g in range(2):
                        sp.wait_ge(s_oout[g], 16 * NT)
                    sp.wait_ge(s_exp[1], 8 * NT)
                    with nc.allow_non_contiguous_dma(reason="36 columns of two matrices"):
                        sp.dma_start(w_r[:, :, 0:GROUPS], t["w_group"].rearrange("l (k p) n -> p (l k) n", p=P)
                                     ).then_inc(s_rb, 16)
                        sp.dma_start(w_r[:, :, GROUPS:], t["w_router"].rearrange("l (k p) n -> p (l k) n", p=P)
                                     ).then_inc(s_rb, 16)
                    sp.dma_start(rbias[:, 0:GROUPS], t["b_group"][0:1, :].to_broadcast([P, GROUPS])).then_inc(s_rb, 16)
                    sp.dma_start(rbias[:, GROUPS:], t["b_router"][0:1, :].to_broadcast([P, EXPERTS])).then_inc(s_rb, 16)
                    with sp.Fori(0, NC) as i:
                        sp.wait_ge(s_var, i)
                        sp.dma_start(o_in, o_scr.rearrange("(c t) p n -> c p t n", c=NC)[i]).then_inc(s_oin, 16)
                        for b in range(2):
                            sp.wait_ge(s_wout[b], 2 * i)
                        for gate, sm, first_tile in ((gate_a, s_ga, KD), (gate_c, s_gc, 0)):
                            sp.dma_start(gate, gate_scr[first_tile:first_tile + KD, :, bass.ts(i, CH)]
                                         .rearrange("k p n -> p k n")).then_inc(sm, 16)
                        for j in range(CH // P):
                            b, n = j % 2, 2 * i + j // 2
                            sp.wait_ge(s_x1out[b], 16 * n)
                            sp.dma_start(xm[b], x_v[4 * i + j]).then_inc(s_xm[b], 16)
                            if j % 2:
                                for b in range(2):
                                    sp.wait_ge(s_x1[b], n + 1)
                                    sp.dma_start(x1_scr[bass.ds(i * CH + (j - 1 + b) * P, P), :], xm[b]
                                                 ).then_inc(s_x1out[b], 16)
                                    sp.wait_ge(s_h2[b], n + 1)
                                    sp.dma_start(h2_scr[bass.ds(i * CH + (j - 1 + b) * P, P), :], ym[b]
                                                 ).then_inc(s_h2out[b], 16)
                    for b in range(2):
                        sp.wait_ge(s_x1out[b], 16 * (NT // 2))
                        sp.wait_ge(s_h2out[b], 16 * (NT // 2))

                @block.scalar
                def _(act):
                    def fade_group(i, g):
                        act.wait_ge(s_fade[g], i + 1)
                        nc.scalar.activation(fade, fade, ACT.Exp).then_inc(s_faded[g], 1)

                    def exp(s, turn, u):
                        act.wait_ge(s_max[s], turn)
                        nc.scalar.activation(prob[s], wide(2 * s, HALF), ACT.Exp, bias=neg_max[:, u:u + 1],
                                             accum_out=total[:, u:u + 1]).then_inc(s_exp[s], 1)

                    exp(0, 1, 0)
                    with act.Fori(0, NT) as i:
                        for u in range(UNITS):
                            if u + 1 < UNITS:
                                exp((u + 1) % 2, 8 * i + (u + 1) // 2 + 1, u + 1)
                            act.wait_ge(s_pT[1], UNITS * i + u + 1)
                            nc.scalar.activation(probT[1], banks[:, 5, :], ACT.Copy).then_inc(s_pTe[1], 1)
                            if u % 8 == 0 and u:
                                fade_group(i, 0)
                        exp(0, 8 * i + 9, 0)
                        fade_group(i, 1)

                    with act.Fori(0, NC) as i:
                        order = Order(act, o_mact, i, 2 * (CH // P))
                        act.wait_ge(s_oT, i + 1)
                        for j in range(2):
                            ins = nc.scalar.activation(oT[:, j, :], banks[:, 1 + j, :], ACT.Copy)
                        ins.then_inc(s_oTa, 1)
                        act.wait_ge(s_centred, i + 1)
                        nc.scalar.activation(squares, cT, ACT.Square).then_inc(s_sq, 1)
                        act.wait_ge(s_var, i + 1)
                        nc.scalar.activation(inv_dev, banks[:, 0, :], ACT.Sqrt, bias=eps_t).then_inc(s_dev, 1)
                        act.wait_ge(s_cnorm, i + 1)
                        for k in range(KC):
                            ins = nc.scalar.activation(cT[:, k, :], cT[:, k, :], ACT.Silu, bias=conv_b[:, k:k + 1],
                                                       scale=conv_g[:, k:k + 1])
                        ins.then_inc(s_cT, 1)

                        def h2T_out(n):
                            act.wait_ge(s_h2T, n + 1)
                            nc.scalar.activation(h2T[:, 0:4, :], banks[:, 5, :].rearrange("p (k n) -> p k n", n=P), ACT.Copy
                                                 ).then_inc(s_h2Ta, 1)

                        for j in range(CH // P):
                            b, n = j % 2, 2 * i + j // 2
                            y = wide(1 + 2 * b, D)
                            act.wait_ge(s_wout[b], n + 1)
                            act.wait_ge(s_h2out[b], 16 * n)
                            act.wait_ge(s_h2Tv, 4 * i + j - 1 if j else 4 * i)
                            order.link(nc.scalar.activation(ym[b], y, ACT.Square, accum_out=mst[b][:, 0:1]))
                            nc.scalar.activation(mst[b][:, 1:2], mst[b][:, 0:1], ACT.Sqrt, bias=eps_t, scale=1.0 / D
                                                 ).then_inc(s_ydev[b], 1)
                            act.wait_ge(s_x1[b], n + 1)
                            order.link(nc.scalar.activation(ym[b], xm[b], ACT.Square, accum_out=mst[b][:, 2:3]))
                            nc.scalar.activation(mst[b][:, 3:4], mst[b][:, 2:3], ACT.Sqrt, bias=eps_t, scale=1.0 / D
                                                 ).then_inc(s_x1dev[b], 1)
                            if j:
                                h2T_out(4 * i + j - 1)
                        h2T_out(4 * i + 3)

                @block.vector
                def _(dve):
                    def unit_max(s, turn, u):
                        dve.wait_ge(s_qk[s], turn)
                        nc.vector.tensor_reduce(neg_max[:, u:u + 1], wide(2 * s, HALF), AX.X, ALU.max, negate=True
                                                ).then_inc(s_max[s], 1)

                    def join_halves(order, i, g):
                        dve.wait_ge(s_pv[1], UNITS * i + 8 * g + 8)
                        halves = lambda a: a.rearrange("p (h o) -> p h o", o=2)
                        one = lambda a: a.rearrange("p (h o) -> p h o", o=1)
                        nm = halves(neg_max[:, 8 * g:8 * g + 8])
                        order.link(nc.vector.tensor_reduce(neg_top, nm, AX.X, ALU.min))
                        nc.vector.tensor_tensor(halves(fade), one(neg_top).to_broadcast([P, 4, 2]), nm, ALU.subtract
                                                ).then_inc(s_fade[g], 1)
                        dve.wait_ge(s_faded[g], i + 1)
                        order.link(nc.vector.tensor_tensor(mass, fade, total[:, 8 * g:8 * g + 8], ALU.mult))
                        order.link(nc.vector.tensor_reduce(norm, halves(mass), AX.X, ALU.add))
                        order.link(nc.vector.reciprocal(norm, norm))
                        order.link(nc.vector.tensor_tensor(halves(share), halves(fade), one(norm).to_broadcast([P, 4, 2]),
                                                           ALU.mult))
                        nc.vector.tensor_tensor(o_parts, banks[:, 6 + g, :].rearrange("p (u d) -> p u d", d=HEAD),
                                                one(share).to_broadcast([P, 8, HEAD]), ALU.mult).then_inc(s_oread[g], 1)
                        dve.wait_ge(s_oread[g], i + 1)
                        dve.wait_ge(s_oout[g], 16 * i)
                        parts = o_parts.rearrange("p (h o) d -> p h o d", o=2)
                        nc.vector.tensor_tensor(o_out[:, g], parts[:, :, 0, :], parts[:, :, 1, :], ALU.add
                                                ).then_inc(s_osum[g], 1)

                    unit_max(0, 1, 0)
                    with dve.Fori(0, NT) as i:
                        order = Order(dve, o_join, i, 10)
                        for u in range(UNITS):
                            if u + 1 < UNITS:
                                unit_max((u + 1) % 2, 8 * i + (u + 1) // 2 + 1, u + 1)
                            else:
                                unit_max(0, 8 * i + 9, 0)
                            dve.wait_ge(s_pT[0], UNITS * i + u + 1)
                            nc.vector.tensor_copy(probT[0], banks[:, 4, :]).then_inc(s_pTe[0], 1)
                            if u == 8:
                                join_halves(order, i, 0)
                        join_halves(order, i, 1)

                    with dve.Fori(0, NC) as i:
                        order = Order(dve, o_merge, i, 1 + 4 * (CH // P))
                        dve.wait_ge(s_oT, i + 1)
                        for j in range(2, 4):
                            ins = nc.vector.tensor_copy(oT[:, j, :], banks[:, 1 + j, :])
                        ins.then_inc(s_oTv, 1)
                        dve.wait_ge(s_mu, i + 1)
                        one = banks[:, 0, :].rearrange("p (o n) -> p o n", o=1).to_broadcast([P, KC, CH])
                        nc.vector.tensor_tensor(cT, conv[:, :, bass.ts(i, CH)], one, ALU.subtract).then_inc(s_centred, 1)
                        dve.wait_ge(s_ga, 16 * i + 16)

                        def branch(d, gate, fold):
                            n = 8 * i + (KD + d if fold else d) // 2 + 1
                            dve.wait_ge(s_branch[d % 2], n)
                            ins = nc.vector.tensor_tensor(gate[:, d, :], banks[:, 5 + d % 2, :], gate[:, d, :], ALU.mult)
                            ins.then_inc(s_used[d % 2], 1)
                            if fold:
                                dve.wait_ge(s_used[d % 2], n)
                                nc.vector.tensor_tensor(gate_a[:, d, :], gate_a[:, d, :], gate_c[:, d, :], ALU.add
                                                        ).then_inc(s_merged, 1)

                        for d in range(2):
                            branch(d, gate_a, False)
                        dve.wait_ge(s_dev, i + 1)
                        order.link(nc.vector.reciprocal(inv_dev, inv_dev))
                        nc.vector.tensor_tensor(cT, cT, inv_dev.rearrange("p (o n) -> p o n", o=1).to_broadcast([P, KC, CH]),
                                                ALU.mult).then_inc(s_cnorm, 1)
                        for d in range(2, KD):
                            branch(d, gate_a, False)
                        dve.wait_ge(s_gc, 16 * i + 16)
                        for d in range(KD):
                            branch(d, gate_c, True)

                        def h2T_out(n):
                            dve.wait_ge(s_h2T, n + 1)
                            nc.vector.tensor_copy(h2T[:, 4:8, :], banks[:, 6, :].rearrange("p (k n) -> p k n", n=P)
                                                  ).then_inc(s_h2Tv, 1)
                            dve.wait_ge(s_logit, n + 1)
                            nc.vector.tensor_copy(logits[:, bass.ds(n, 1), :].rearrange("p a b -> p (a b)"),
                                                  banks[:, 7, 0:LOGITS]).then_inc(s_logitc, 1)

                        for j in range(CH // P):
                            b, n = j % 2, 2 * i + j // 2
                            y = wide(1 + 2 * b, D)
                            dve.wait_ge(s_ydev[b], n + 1)
                            order.link(nc.vector.reciprocal(mst[b][:, 0:1], mst[b][:, 1:2]))
                            order.link(nc.vector.scalar_tensor_tensor(out=ym[b], in0=y, scalar=mst[b][:, 0:1],
                                                                      in1=rows[:, 0, :], op0=ALU.mult, op1=ALU.mult))
                            dve.wait_ge(s_xm[b], 16 * n + 16)
                            nc.vector.tensor_tensor(xm[b], xm[b], ym[b], ALU.add).then_inc(s_x1[b], 1)
                            dve.wait_ge(s_x1dev[b], n + 1)
                            order.link(nc.vector.reciprocal(mst[b][:, 2:3], mst[b][:, 3:4]))
                            order.link(nc.vector.scalar_tensor_tensor(out=ym[b], in0=xm[b], scalar=mst[b][:, 2:3],
                                                                      in1=rows[:, 2, :], op0=ALU.mult, op1=ALU.mult))
                            nc.vector.tensor_tensor(ym[b], ym[b], rows[:, 1, :], ALU.add).then_inc(s_h2[b], 1)
                            if j:
                                h2T_out(4 * i + j - 1)
                        h2T_out(4 * i + 3)

                @block.tensor
                def _(pe):
                    def scores(u, turn_q, turn_exp):
                        h, half = u // 2, u % 2
                        at = HEAD * (h % 2)
                        pe.wait_ge(s_q[h // 2], turn_q)
                        pe.wait_ge(s_exp[u % 2], turn_exp)
                        for n in range(HALF // BANK):
                            key = half * HALF + n * BANK
                            ins = nc.tensor.matmul(banks[:, 2 * (u % 2) + n, :], qb[at:at + HEAD, h // 2, :],
                                                   kT[at:at + HEAD, h // 4, key:key + BANK], start=True, stop=True)
                        ins.then_inc(s_qk[u % 2], 1)

                    def turn_probs(i, u, g):
                        pe.wait_ge(s_exp[u % 2], 8 * i + u // 2 + 1)
                        pe.wait_ge(s_pTe[g], UNITS * i + u)
                        for j in range(4):
                            ins = nc.tensor.transpose(banks[:, 4 + g, j * P:(j + 1) * P],
                                                      prob[u % 2][:, (4 * g + j) * P:(4 * g + j + 1) * P], ident)
                        ins.then_inc(s_pT[g], 1)

                    def values(i, u, g):
                        kv, half = u // 8, u % 2
                        pe.wait_ge(s_pTe[g], UNITS * i + u + 1)
                        if u % 8 == 0 and g == 0:
                            pe.wait_ge(s_oread[kv], i)
                        for j in range(4):
                            ins = nc.tensor.matmul(banks[:, 6 + kv, (u % 8) * HEAD:(u % 8 + 1) * HEAD],
                                                   probT[g][:, j * P:(j + 1) * P],
                                                   v_sb[:, half * 8 + 4 * g + j, kv * HEAD:(kv + 1) * HEAD],
                                                   start=(g == 0 and j == 0), stop=(g == 1 and j == 3))
                        ins.then_inc(s_pv[g], 1)

                    scores(0, 16, 0)
                    with pe.Fori(0, NT) as i:
                        for u in range(UNITS):
                            if u + 1 < UNITS:
                                scores(u + 1, 16 * i + 16, 8 * i + (u + 1) // 2)
                            else:
                                scores(0, 16 * i + 32, 8 * i + 8)
                            turn_probs(i, u, 0)
                            if u:
                                values(i, u - 1, 1)
                            turn_probs(i, u, 1)
                            values(i, u, 0)
                        values(i, UNITS - 1, 1)

                    pe.wait_ge(s_wmerge, 48)
                    pe.wait_ge(s_rb, 64)
                    pe.wait_ge(s_oread[0], NT)
                    pe.wait_ge(s_oread[1], NT)
                    pe.wait_ge(s_max[0], 8 * NT + 1)
                    with pe.Fori(0, NC) as i:
                        pe.wait_ge(s_dev, i)
                        for k in range(KC):
                            ins = nc.tensor.matmul(banks[:, 0, :], mean_w, conv[:, k, bass.ts(i, CH)],
                                                   start=(k == 0), stop=(k == KC - 1))
                        ins.then_inc(s_mu, 1)
                        pe.wait_ge(s_oin, 16 * i + 16)
                        for b in range(2):
                            pe.wait_ge(s_h2[b], 2 * i)
                        for j in range(KC):
                            for n in range(CH // P):
                                ins = nc.tensor.transpose(banks[:, 1 + j, n * P:(n + 1) * P], o_in[:, n, j * P:(j + 1) * P],
                                                          ident)
                        ins.then_inc(s_oT, 1)
                        pe.wait_ge(s_oTa, i + 1)
                        pe.wait_ge(s_oTv, i + 1)
                        pe.wait_ge(s_logitc, 4 * i)

                        def branch(d, w, src, turn):
                            pe.wait_ge(s_used[d % 2], turn)
                            for k in range(KC):
                                ins = nc.tensor.matmul(banks[:, 5 + d % 2, :], w[:, k, d * P:(d + 1) * P], src[:, k, :],
                                                       start=(k == 0), stop=(k == KC - 1))
                            ins.then_inc(s_branch[d % 2], 1)

                        for d in range(KD):
                            branch(d, w_ao, oT, 8 * i + d // 2)
                            if d == 1:
                                pe.wait_ge(s_sq, i + 1)
                                for k in range(KC):
                                    ins = nc.tensor.matmul(banks[:, 0, :], mean_w, squares[:, k, :],
                                                           start=(k == 0), stop=(k == KC - 1))
                                ins.then_inc(s_var, 1)
                        pe.wait_ge(s_cT, i + 1)
                        for d in range(KD):
                            branch(d, w_co, cT, 8 * i + 4 + d // 2)
                        pe.wait_ge(s_merged, KD * i + KD)

                        def route_logits(n, b, turn):
                            pe.wait_ge(s_h2[b], turn + 1)
                            pe.wait_ge(s_h2Ta, n)
                            pe.wait_ge(s_h2Tv, n)
                            for k in range(KD):
                                ins = nc.tensor.transpose(banks[:, 5 + k // 4, (k % 4) * P:(k % 4 + 1) * P],
                                                          ym[b][:, k * P:(k + 1) * P], ident)
                            ins.then_inc(s_h2T, 1)
                            pe.wait_ge(s_h2Ta, n + 1)
                            pe.wait_ge(s_h2Tv, n + 1)
                            pe.wait_ge(s_logitc, n)
                            for k in range(KD):
                                ins = nc.tensor.matmul(banks[:, 7, 0:LOGITS], h2T[:, k, :], w_r[:, k, :],
                                                       start=(k == 0), stop=(k == KD - 1))
                            ins.then_inc(s_logit, 1)

                        for j in range(CH // P):
                            b, n = j % 2, 2 * i + j // 2
                            pe.wait_ge(s_h2[b], n)
                            for o in range(2):
                                for k in range(KD):
                                    ins = nc.tensor.matmul(banks[:, 1 + 2 * b + o, :], gate_a[:, k, j * P:(j + 1) * P],
                                                           w_o[:, k, o * BANK:(o + 1) * BANK],
                                                           start=(k == 0), stop=(k == KD - 1))
                            ins.then_inc(s_wout[b], 1)
                            if j:
                                route_logits(4 * i + j - 1, 1 - b, 2 * i + (j - 1) // 2)
                        route_logits(4 * i + 3, 1, 2 * i + 1)

            end_phase(sems)

        def experts():
            sems = []
            with ExitStack() as own:
                def sem(name):
                    sems.append(nc.alloc_semaphore(name))
                    return sems[-1]

                o_route = sem("o_route")
                s_iota = sem("s_iota")
                s_gdiff, s_gexp, s_ediff, s_eexp = sem("s_gdiff"), sem("s_gexp"), sem("s_ediff"), sem("s_eexp")
                s_picked, s_rank = sem("s_picked"), sem("s_rank")
                s_onehot = [sem(f"s_onehot{a}") for a in range(2)]
                s_list = [sem(f"s_list{a}") for a in range(2)]
                s_blocks, s_lists = sem("s_blocks"), sem("s_lists")
                s_wg = [sem(f"s_wg{s}") for s in range(2)]
                s_wu = [sem(f"s_wu{s}") for s in range(2)]
                s_wd = [sem(f"s_wd{s}") for s in range(2)]
                s_xg = [sem(f"s_xg{s}") for s in range(2)]
                s_xgT = [sem(f"s_xgT{s}") for s in range(2)]
                s_xTa = [sem(f"s_xTa{s}") for s in range(2)]
                s_xTv = [sem(f"s_xTv{s}") for s in range(2)]
                s_gate = sem("s_gate")
                s_up = [sem(f"s_up{s}") for s in range(2)]
                s_silu, s_act, s_actT, s_actTe = sem("s_silu"), sem("s_act"), sem("s_actT"), sem("s_actTe")
                s_down = [sem(f"s_down{s}") for s in range(2)]
                s_ya = [sem(f"s_ya{s}") for s in range(2)]
                s_yv = [sem(f"s_yv{s}") for s in range(2)]
                s_yout = [sem(f"s_yout{s}") for s in range(2)]
                s_yj = [sem(f"s_yj{s}") for s in range(2)]
                s_xj = [sem(f"s_xj{s}") for s in range(2)]
                s_jsum = [sem(f"s_jsum{s}") for s in range(2)]
                s_jdev = [sem(f"s_jdev{s}") for s in range(2)]
                s_jout = [sem(f"s_jout{s}") for s in range(2)]
                s_out = [sem(f"s_out{s}") for s in range(2)]
                o_jdve, o_jact = sem("o_jdve"), sem("o_jact")
                block = own.enter_context(nc.Block())

                @block.sync
                def _(sp):
                    sp.wait_ge(s_blocks, 1)
                    with sp.Fori(0, BLOCKS // 2) as i:
                        for s in range(2):
                            e = sp.value_load(block_expert_i[0:1, bass.ds(2 * i + s, 1)], min_val=0, max_val=EXPERTS - 1)
                            sp.wait_ge(s_up[s], i)
                            for w, name, sm in ((w_g[s], "w_e_gate", s_wg[s]), (w_u[s], "w_e_up", s_wu[s])):
                                sp.dma_start(w, t[name][0, bass.ds(e, 1)].rearrange("e (k p) n -> p (e k) n", p=P)
                                             ).then_inc(sm, 16)
                            sp.wait_ge(s_down[s], i)
                            sp.dma_start(w_d[s], t["w_e_down"][0, bass.ds(e, 1)].rearrange("e (k p) n -> p (e k) n", p=P)
                                         ).then_inc(s_wd[s], 16)
                    for s in range(2):
                        sp.wait_ge(s_down[s], BLOCKS // 2)
                    with sp.Fori(0, NT // 2) as i:
                        for s in range(2):
                            sp.wait_ge(s_out[s], 16 * i)
                            sp.dma_start(xj[s], x1_scr[bass.ts(2 * i + s, P), :]).then_inc(s_xj[s], 16)
                        for s in range(2):
                            sp.wait_ge(s_jout[s], i + 1)
                            sp.dma_start(out_v[2 * i + s], xj[s]).then_inc(s_out[s], 16)
                    for s in range(2):
                        sp.wait_ge(s_out[s], 16 * (NT // 2))

                @block.gpsimd
                def _(pool):
                    nc.gpsimd.iota(iota_i, [[1, P]], base=0, channel_multiplier=0).then_inc(s_iota, 1)
                    nc.gpsimd.iota(token_i, [[P, NT]], base=0, channel_multiplier=1).then_inc(s_iota, 1)
                    pool.wait_ge(s_lists, 1)
                    for j in range(BLOCKS + 1):
                        s = j % 2
                        pool.wait_ge(s_xgT[s], j // 2)
                        nc.gpsimd.indirect_dma_start(out=xg[s], out_offset=None, in_=h2_scr[:, :],
                                                     in_offset=bass.IndirectOffsetOnAxis(
                                                         ap=slot_token[:, j:j + 1], axis=0)).then_inc(s_xg[s], 16)
                    for s in range(2):
                        pool.wait_ge(s_yout[s], 16 * (BLOCKS // 2))
                        pool.wait_ge(s_down[s], BLOCKS // 2)
                    for n in range(NT):
                        s = n % 2
                        pool.wait_ge(s_jout[s], n // 2)
                        for a in range(2):
                            nc.gpsimd.indirect_dma_start(out=yj[s][a], out_offset=None, in_=y_scr[:, :],
                                                         in_offset=bass.IndirectOffsetOnAxis(
                                                             ap=slots_i[:, a, n:n + 1], axis=0)).then_inc(s_yj[s], 16)

                @block.scalar
                def _(act):
                    act.wait_ge(s_gdiff, 1)
                    nc.scalar.activation(exp_g, exp_g, ACT.Exp).then_inc(s_gexp, 1)
                    act.wait_ge(s_ediff, 1)
                    nc.scalar.activation(ratio, ratio, ACT.Exp).then_inc(s_eexp, 1)

                    def xT_out(s, turn):
                        act.wait_ge(s_xgT[s], turn)
                        nc.scalar.activation(xT[s][:, 0:4, :], banks[:, 2, :].rearrange("p (k n) -> p k n", n=P), ACT.Copy
                                             ).then_inc(s_xTa[s], 1)

                    xT_out(0, 1)
                    with act.Fori(0, BLOCKS // 2) as i:
                        for s in range(2):
                            act.wait_ge(s_gate, 2 * i + s + 1)
                            nc.scalar.activation(act_g, banks[:, 0, :], ACT.Silu).then_inc(s_silu, 1)
                            xT_out(1 - s, i + 1 + s)
                            act.wait_ge(s_actT, 2 * i + s + 1)
                            nc.scalar.activation(actT, banks[:, 4, :].rearrange("p (k n) -> p k n", n=P), ACT.Copy
                                                 ).then_inc(s_actTe, 1)
                            act.wait_ge(s_down[s], i + 1)
                            act.wait_ge(s_yout[s], 16 * i)
                            nc.scalar.activation(ys[s][:, 0:BANK], banks[:, 5, :], ACT.Copy).then_inc(s_ya[s], 1)
                            act.wait_ge(s_ya[s], i + 1)
                            act.wait_ge(s_yv[s], i + 1)
                            act.dma_start(y_scr[bass.ts(2 * i + s, P), :], ys[s]).then_inc(s_yout[s], 16)
                    with act.Fori(0, NT // 2) as i:
                        order = Order(act, o_jact, i, 2)
                        for s in range(2):
                            act.wait_ge(s_jsum[s], i + 1)
                            order.link(nc.scalar.activation(jjunk, yj[s][0], ACT.Square, accum_out=jst[s][:, 0:1]))
                            nc.scalar.activation(jst[s][:, 1:2], jst[s][:, 0:1], ACT.Sqrt, bias=eps_t, scale=1.0 / D
                                                 ).then_inc(s_jdev[s], 1)

                @block.vector
                def _(dve):
                    order = Order(dve, o_route)
                    L = order.link
                    tt, ts = nc.vector.tensor_tensor, nc.vector.tensor_scalar

                    def over(ap, n):
                        return ap.rearrange("p (a o) -> p a o", o=1).to_broadcast([P, ap.shape[1], n])

                    def along(ap, n):
                        return ap.rearrange("p (o a) -> p o a", o=1).to_broadcast([P, n, ap.shape[1]])

                    dve.wait_ge(s_iota, 2)
                    L(nc.vector.tensor_copy(iota, iota_i))
                    L(nc.vector.tensor_copy(token, token_i))
                    L(nc.vector.memset(zeros, 0.0))
                    L(tt(logits, logits, along(rbias, NT), ALU.add))
                    lg, le = logits[:, :, 0:GROUPS], logits[:, :, GROUPS:]
                    L(nc.vector.tensor_reduce(top_g, lg, AX.X, ALU.max))
                    tt(exp_g, lg, over(top_g, GROUPS), ALU.subtract).then_inc(s_gdiff, 1)

                    def first_of(scores, best, n, cand, low, hot):
                        L(tt(cand, scores, over(best, n), ALU.is_equal))
                        L(nc.vector.scalar_tensor_tensor(out=cand, in0=cand, scalar=-64.0, in1=along(iota[:, 0:n], NT),
                                                         op0=ALU.mult, op1=ALU.add))
                        L(nc.vector.tensor_reduce(low, cand, AX.X, ALU.min))
                        L(tt(hot, cand, over(low, n), ALU.is_equal))

                    first_of(lg, top_g, GROUPS, cand_g, first_g, hot_g)
                    hot_wide = over(hot_g.rearrange("p t g -> p (t g)"), PER_GROUP)
                    by_group = lambda a: a.rearrange("p t (g e) -> p (t g) e", e=PER_GROUP)
                    L(nc.vector.tensor_copy(picked, le))
                    L(tt(by_group(masked), by_group(picked), hot_wide, ALU.mult))
                    L(ts(cand_g, hot_g, BIG, -BIG, ALU.mult, ALU.add))
                    L(tt(by_group(masked), by_group(masked), over(cand_g.rearrange("p t g -> p (t g)"), PER_GROUP), ALU.add))
                    L(nc.vector.tensor_reduce(top[0], masked, AX.X, ALU.max))
                    first_of(masked, top[0], EXPERTS, cand, first, hot[0])
                    L(nc.vector.scalar_tensor_tensor(out=masked, in0=hot[0], scalar=-4.0 * BIG, in1=masked,
                                                     op0=ALU.mult, op1=ALU.add))
                    L(nc.vector.tensor_reduce(top[1], masked, AX.X, ALU.max))
                    first_of(masked, top[1], EXPERTS, cand, first, hot[1])
                    tt(picked, hot[0], hot[1], ALU.add).then_inc(s_picked, 1)
                    tt(ratio, top[1], top[0], ALU.subtract).then_inc(s_ediff, 1)
                    dve.wait_ge(s_gexp, 1)
                    L(nc.vector.tensor_reduce(sum_g, exp_g, AX.X, ALU.add))
                    dve.wait_ge(s_eexp, 1)
                    L(nc.vector.scalar_tensor_tensor(out=sum_g, in0=ratio, scalar=1.0, in1=sum_g, op0=ALU.add, op1=ALU.mult))
                    L(nc.vector.reciprocal(weights[:, 0, :], sum_g))
                    L(tt(weights[:, 1, :], weights[:, 0, :], ratio, ALU.mult))
                    dve.wait_ge(s_rank, 1)
                    L(nc.vector.memset(base[:, 0, :], 0.0))
                    totals = banks[:, 1, :].rearrange("p (t e) -> p t e", e=EXPERTS)
                    for n in range(NT):
                        L(tt(base[:, n + 1, :], base[:, n, :], totals[:, n, :], ALU.add))
                    L(ts(blocks_of.rearrange("p e n -> p (e n)")[:, 0:NT], iota[:, 0:NT], float(P), None, ALU.mult))
                    L(nc.vector.tensor_copy(run[1][:, 0:NT], blocks_of.rearrange("p e n -> p (e n)")[:, 0:NT]))
                    L(tt(blocks_of, over(base[:, NT, :], NT), along(run[1][:, 0:NT], EXPERTS), ALU.is_gt))
                    L(nc.vector.tensor_reduce(counts, blocks_of, AX.X, ALU.add))
                    L(nc.vector.tensor_copy(run[0], counts))
                    side = 0
                    for step in (1, 2, 4, 8, 16):
                        L(nc.vector.tensor_copy(run[1 - side][:, 0:step], run[side][:, 0:step]))
                        L(tt(run[1 - side][:, step:], run[side][:, step:], run[side][:, 0:EXPERTS - step], ALU.add))
                        side = 1 - side
                    ends = run[side]
                    L(tt(reached, over(iota[:, 0:BLOCKS], EXPERTS), along(ends, BLOCKS), ALU.is_ge))
                    L(nc.vector.tensor_reduce(block_expert, reached, AX.X, ALU.add))
                    L(ts(block_expert, block_expert, float(EXPERTS - 1), None, ALU.min))
                    nc.vector.tensor_copy(block_expert_i, block_expert).then_inc(s_blocks, 1)
                    L(tt(run[1 - side], ends, counts, ALU.subtract))
                    L(ts(run[1 - side], run[1 - side], float(P), None, ALU.mult))
                    slot = cand
                    L(tt(slot, banks[:, 0, :].rearrange("p (t e) -> p t e", e=EXPERTS), base[:, 0:NT, :], ALU.add))
                    L(tt(slot, slot, along(run[1 - side], NT), ALU.add))
                    for a in range(2):
                        L(tt(masked, slot, hot[a], ALU.mult))
                        L(nc.vector.tensor_reduce(slots_of[:, a, :], masked, AX.X, ALU.add))
                    L(nc.vector.tensor_copy(slots_i, slots_of))
                    hi_i, lo_i = picked.rearrange("p a b -> p (a b)")[:, 0:2 * NT].bitcast(I32), cand.rearrange(
                        "p a b -> p (a b)")[:, 0:2 * NT].bitcast(I32)
                    flat = lambda a: a.rearrange("p a b -> p (a b)")
                    L(ts(hi_i, flat(slots_i), 7, None, ALU.logical_shift_right))
                    L(ts(lo_i, flat(slots_i), P - 1, None, ALU.bitwise_and))
                    L(nc.vector.tensor_copy(flat(slots_hi), hi_i))
                    L(nc.vector.tensor_copy(flat(slots_lo), lo_i))
                    with dve.Fori(0, NT) as i:
                        for a in range(2):
                            dve.wait_ge(s_list[a], i)
                            ts(in_block[a], iota, slots_lo[:, a, bass.ds(i, 1)], None, ALU.is_equal).then_inc(s_onehot[a], 1)
                            ts(of_block[a], iota[:, 0:LISTS], slots_hi[:, a, bass.ds(i, 1)], token[:, bass.ds(i, 1)],
                               ALU.is_equal, ALU.mult).then_inc(s_onehot[a], 1)
                    dve.wait_ge(s_list[1], NT + 1)
                    nc.vector.tensor_copy(slot_token, banks[:, 2, 0:LISTS]).then_inc(s_lists, 1)

                    def xT_out(s, turn):
                        dve.wait_ge(s_xgT[s], turn)
                        nc.vector.tensor_copy(xT[s][:, 4:8, :], banks[:, 3, :].rearrange("p (k n) -> p k n", n=P)
                                              ).then_inc(s_xTv[s], 1)

                    xT_out(0, 1)
                    with dve.Fori(0, BLOCKS // 2) as i:
                        for s in range(2):
                            dve.wait_ge(s_silu, 2 * i + s + 1)
                            dve.wait_ge(s_up[s], i + 1)
                            tt(act_u, act_g, banks[:, 1, :], ALU.mult).then_inc(s_act, 1)
                            xT_out(1 - s, i + 1 + s)
                            dve.wait_ge(s_down[s], i + 1)
                            dve.wait_ge(s_yout[s], 16 * i)
                            nc.vector.tensor_copy(ys[s][:, BANK:], banks[:, 6, :]).then_inc(s_yv[s], 1)
                    with dve.Fori(0, NT // 2) as i:
                        order = Order(dve, o_jdve, i, 6)
                        for s in range(2):
                            dve.wait_ge(s_yj[s], 32 * i + 32)
                            order.link(ts(yj[s][0], yj[s][0], weights[:, 0, bass.ds(2 * i + s, 1)], None, ALU.mult))
                            nc.vector.scalar_tensor_tensor(
                                out=yj[s][0], in0=yj[s][1], scalar=weights[:, 1, bass.ds(2 * i + s, 1)], in1=yj[s][0],
                                op0=ALU.mult, op1=ALU.add).then_inc(s_jsum[s], 1)
                            dve.wait_ge(s_jdev[s], i + 1)
                            order.link(nc.vector.reciprocal(jst[s][:, 0:1], jst[s][:, 1:2]))
                            order.link(nc.vector.scalar_tensor_tensor(out=yj[s][1], in0=yj[s][0], scalar=jst[s][:, 0:1],
                                                                      in1=rows[:, 3, :], op0=ALU.mult, op1=ALU.mult))
                            dve.wait_ge(s_xj[s], 16 * i + 16)
                            nc.vector.tensor_tensor(xj[s], xj[s], yj[s][1], ALU.add).then_inc(s_jout[s], 1)

                @block.tensor
                def _(pe):
                    pe.wait_ge(s_picked, 1)
                    flat_picked = picked.rearrange("p t e -> p (t e)")
                    nc.tensor.matmul(banks[:, 0, :], before, flat_picked, start=True, stop=True)
                    nc.tensor.matmul(banks[:, 1, :], ones, flat_picked, start=True, stop=True).then_inc(s_rank, 1)
                    pe.wait_ge(s_onehot[0], 2)
                    nc.tensor.matmul(banks[:, 2, 0:LISTS], zeros, of_block[0], start=True, stop=False)
                    with pe.Fori(0, NT) as i:
                        for a in range(2):
                            pe.wait_ge(s_onehot[a], 2 * i + 2)
                            nc.tensor.matmul(banks[:, 2, 0:LISTS], in_block[a], of_block[a], start=False, stop=False
                                             ).then_inc(s_list[a], 1)
                    nc.tensor.matmul(banks[:, 2, 0:LISTS], zeros, of_block[0], start=False, stop=True
                                     ).then_inc(s_list[1], 1)
                    pe.wait_ge(s_lists, 1)

                    def turn_tokens(s, turn, turn_x):
                        pe.wait_ge(s_xg[s], 16 * turn)
                        pe.wait_ge(s_xTa[1 - s], turn_x)
                        pe.wait_ge(s_xTv[1 - s], turn_x)
                        for k in range(KD):
                            ins = nc.tensor.transpose(banks[:, 2 + k // 4, (k % 4) * P:(k % 4 + 1) * P],
                                                      xg[s][:, k * P:(k + 1) * P], ident)
                        ins.then_inc(s_xgT[s], 1)

                    turn_tokens(0, 1, 0)
                    with pe.Fori(0, BLOCKS // 2) as i:
                        for s in range(2):
                            pe.wait_ge(s_xTa[s], i + 1)
                            pe.wait_ge(s_xTv[s], i + 1)
                            pe.wait_ge(s_wg[s], 16 * i + 16)
                            pe.wait_ge(s_act, 2 * i + s)
                            for k in range(KD):
                                ins = nc.tensor.matmul(banks[:, 0, :], xT[s][:, k, :], w_g[s][:, k, :],
                                                       start=(k == 0), stop=(k == KD - 1))
                            ins.then_inc(s_gate, 1)
                            pe.wait_ge(s_wu[s], 16 * i + 16)
                            for k in range(KD):
                                ins = nc.tensor.matmul(banks[:, 1, :], xT[s][:, k, :], w_u[s][:, k, :],
                                                       start=(k == 0), stop=(k == KD - 1))
                            ins.then_inc(s_up[s], 1)
                            turn_tokens(1 - s, i + 1 + s, i + 1)
                            pe.wait_ge(s_act, 2 * i + s + 1)
                            for k in range(KF):
                                ins = nc.tensor.transpose(banks[:, 4, k * P:(k + 1) * P], act_u[:, k * P:(k + 1) * P], ident)
                            ins.then_inc(s_actT, 1)
                            pe.wait_ge(s_actTe, 2 * i + s + 1)
                            pe.wait_ge(s_wd[s], 16 * i + 16)
                            if s == 0:
                                pe.wait_ge(s_ya[1], i)
                                pe.wait_ge(s_yv[1], i)
                            else:
                                pe.wait_ge(s_ya[0], i + 1)
                                pe.wait_ge(s_yv[0], i + 1)
                            for o in range(2):
                                for k in range(KF):
                                    ins = nc.tensor.matmul(banks[:, 5 + o, :], actT[:, k, :],
                                                           w_d[s][:, k, o * BANK:(o + 1) * BANK],
                                                           start=(k == 0), stop=(k == KF - 1))
                            ins.then_inc(s_down[s], 1)

        project()
        attend()
        experts()


NAMES = ["x", "c", "w_ada", "b_ada", "g_pre_mix", "g_post_mix", "w_in", "w_dw", "b_dw", "conv_ln_g", "conv_ln_b",
         "w_conv_out", "q_norm_g", "k_norm_g", "w_attn_out", "w_out", "g_pre_ffn", "g_post_ffn", "w_group",
         "b_group", "w_router", "b_router", "w_e_gate", "w_e_up", "w_e_down"]


def rope_tables():
    half = HEAD // 2
    freq = np.float32(ROPE_THETA) ** (-np.arange(0, half, 2, dtype=np.float32) / np.float32(half))
    pos = np.arange(S)
    row = (pos // GRID_W).astype(np.float32)[:, None] * freq
    column = (pos % GRID_W).astype(np.float32)[:, None] * freq
    cos = np.concatenate([np.cos(row), np.cos(row), np.cos(column), np.cos(column)], 1)
    sin = np.concatenate([-np.sin(row), np.sin(row), -np.sin(column), np.sin(column)], 1)
    return np.ascontiguousarray(cos, np.float32), np.ascontiguousarray(sin, np.float32)


def kernel(**inputs):
    import concourse.bacc as _bacc
    from concourse.bass_utils import run_bass_kernel_spmd as _run

    nc = _bacc.Bacc("TRN2", target_bir_lowering=False, num_devices=1)
    arrays, tensors = {}, {}
    for name in NAMES:
        arrays[f"in_{name}"] = np.ascontiguousarray(inputs[name])
    arrays["in_rope_cos"], arrays["in_rope_sin"] = rope_tables()
    for name, a in arrays.items():
        tensors[name[3:]] = nc.dram_tensor(name, a.shape, mybir.dt.from_np(a.dtype), kind="ExternalInput").ap()
    out = nc.dram_tensor("out_0", (1, S, D), F32, kind="ExternalOutput").ap()
    encoder_block(nc, tensors, out)
    r = _run(nc, [arrays], core_ids=[0])
    return r.results[0]["out_0"]
```

```python
from contextlib import ExitStack

import concourse.bass as bass
import numpy as np
from concourse import mybir

F32 = mybir.dt.float32
F32R = mybir.dt.float32r
I32 = mybir.dt.int32
U32 = mybir.dt.uint32
ACT = mybir.ActivationFunctionType
ALU = mybir.AluOpType
AX = mybir.AxisListType

P = 128
BANK = 512
S, D = 2048, 1024
HEADS, KV_HEADS, HEAD = 8, 2, 64
GRID_W, ROPE_THETA = 64, 10000.0
CONV, TAPS = 512, 31
GROUPS, PER_GROUP, D_EXPERT = 4, 8, 512
EXPERTS = GROUPS * PER_GROUP
EPS = 1e-6

NT = S // P
KD = D // P
KC = CONV // P
KF = D_EXPERT // P
CH = 512
NC = S // CH
ATT = HEADS * HEAD
KV = KV_HEADS * HEAD
QK = ATT + KV
ROWS = 4 * D // BANK
HALF = S // 2
PAD = TAPS // 2
BLOCKS = 2 * S // P + EXPERTS
LOGITS = GROUPS + EXPERTS
COL_GLU, COL_QKV, COL_GATE = 0, 2 * CONV, 2 * CONV + ATT + 2 * KV
BIG = 1.0e30


class Arena:

    def __init__(self, tensor, size):
        self.tensor, self.size, self.at = tensor, size, 0

    def take(self, *shape):
        n = int(np.prod(shape))
        view = self.tensor[:, self.at:self.at + n]
        self.at += (n + 7) // 8 * 8
        assert self.at <= self.size, (self.at, self.size)
        if len(shape) > 1:
            names = "abcd"[:len(shape)]
            view = view.rearrange(f"p ({' '.join(names)}) -> p {' '.join(names)}",
                                  **{n: s for n, s in zip(names[1:], shape[1:])})
        return view


class Order:

    def __init__(self, eng, sem, turn=0, per=0, base=0):
        self.eng, self.sem, self.n = eng, sem, turn * per + base
        self.k = 0

    def link(self, ins):
        ins.then_inc(self.sem, 1)
        self.k += 1
        self.eng.wait_ge(self.sem, self.n + self.k)


def turns(eng, n):
    def run(body):
        body(0)
        with eng.Fori(1, n) as i:
            body(i)
    return run


def encoder_block(nc, t, out):
    ctx = ExitStack()
    with ctx:
        def dram(name, shape, dt=F32):
            return nc.dram_tensor(name, shape, dt, kind="Internal").ap()

        KEEP, FIXED = 5984, 24576
        kept = Arena(ctx.enter_context(nc.sbuf_tensor("kept", [P, KEEP], F32)), KEEP)
        banks = ctx.enter_context(nc.psum_tensor("banks", [P, 8, BANK], F32))
        keep = kept.take

        def wide(b, n):
            return banks[:, b:b + (n + BANK - 1) // BANK, :].rearrange("p a b -> p (a b)")[:, 0:n]

        qk_scr = dram("qk_scr", [NT, P, 2 * QK])
        q_scr = dram("q_scr", [NT + 1, P, 2 * HEADS * P])
        gate_scr = dram("gate_scr", [2 * KD, P, S])
        o_scr = dram("o_scr", [NT, P, ATT])
        x1_scr = dram("x1_scr", [S, D])
        h2_scr = dram("h2_scr", [S, D])
        y_scr = dram("y_scr", [BLOCKS * P, D])

        ident = keep(P)
        ones = keep(P)
        mean_w = keep(P)
        before = keep(P)
        eps_t = keep(1)
        c_col = keep(KD)
        c_silu = keep(KD)
        vec = keep(24)
        shift1 = keep(KD)
        scale1 = keep(KD)
        rbias = keep(LOGITS)
        logits = keep(NT, LOGITS)
        conv_g, conv_b, dw_b = keep(KC), keep(KC), keep(KC)
        dw_w = keep(KC, TAPS)
        rows = keep(4, D)

        mixing = ExitStack()
        arena = Arena(mixing.enter_context(nc.sbuf_tensor("arena", [P, FIXED], F32)), FIXED)
        hT = arena.take(KD, S)
        conv = arena.take(KC, S)
        arena.at = 0
        w_co = arena.take(KC, D)
        w_ao = arena.take(KC, D)
        w_o = arena.take(KD, D)

        keys_values = ExitStack()
        v_sb = keys_values.enter_context(nc.sbuf_tensor("v_sb", [P, NT * KV], F32))[:, :].rearrange(
            "p (t n) -> p t n", n=KV)
        kT = keys_values.enter_context(nc.sbuf_tensor("kT", [P, KV_HEADS * S], F32R))[:, :].rearrange(
            "p (g n) -> p g n", n=S)

        x_v = t["x"].rearrange("a (t p) d -> (a t) p d", p=P)
        w_ada_v = t["w_ada"].rearrange("l (k p) n -> p (l k) n", p=P)
        w_in_v = t["w_in"].rearrange("l (k p) n -> p (l k) n", p=P)
        out_v = out.rearrange("a (t p) d -> (a t) p d", p=P)

        def col(ap1d, n):
            return ap1d.rearrange("(k p) -> p k", p=P)

        def end_phase(sems):
            nc.clear_and_free_semaphores(sems)
            nc.all_engine_barrier()

        def project():
            sems = []
            with ExitStack() as own:
                def sem(name):
                    sems.append(nc.alloc_semaphore(name))
                    return sems[-1]

                arena.at = 0
                ada_w = [arena.take(KD, D) for _ in range(2)]
                arena.at = 0
                w_ada_row = [arena.take(KD, BANK) for _ in range(2)]
                gains = arena.take(3, D)
                arena.at = KD * S
                xt = [arena.take(D) for _ in range(2)]
                junk = arena.take(D)
                hs = [arena.take(KD, P) for _ in range(2)]
                sq = arena.take(QK)
                rot = arena.take(QK)
                gain = arena.take(QK)
                OWN = 12160
                buffers = Arena(own.enter_context(nc.sbuf_tensor("project_buffers", [P, OWN], F32)), OWN)
                take = buffers.take
                w_qkv = take(KD, ATT + 2 * KV)
                qk = [take(QK) for _ in range(2)]
                roped = [take(2 * QK) for _ in range(2)]
                cos_t, sin_t = take(NT, HEAD), take(NT, HEAD)
                st = [take(2) for _ in range(2)]
                hst = [take(2 * (HEADS + KV_HEADS)) for _ in range(2)]
                buffers.at = 0
                tin = [take(2 * QK) for _ in range(2)]
                qout = [own.enter_context(nc.sbuf_tensor(f"q_out{n}", [P, 2 * HEADS * P], F32R))[:, :].rearrange(
                    "p (h a n) -> p h a n", h=HEADS, a=2) for n in range(2)]
                buffers.at = 0
                wcol = [take(KD, P) for _ in range(2)]
                glu = take(S + 2 * PAD)
                sg = take(S)
                gate_out = [take(S) for _ in range(2)]
                c_wide = sg[:, 0:KD * P].rearrange("p (k n) -> p k n", n=P)

                s_const = sem("s_const")
                s_vec = sem("s_vec")
                s_convvec = sem("s_convvec")
                s_rows = sem("s_rows")
                s_csilu = sem("s_csilu")
                s_wada = [sem(f"s_wada{n}") for n in range(2)]
                s_ada_mm = sem("s_ada_mm")
                s_ada_col = sem("s_ada_col")
                s_x = [sem(f"s_x{s}") for s in range(2)]
                s_xss = [sem(f"s_xss{s}") for s in range(2)]
                s_xroot = [sem(f"s_xroot{s}") for s in range(2)]
                s_xn = [sem(f"s_xn{s}") for s in range(2)]
                s_xT = [sem(f"s_xT{s}") for s in range(2)]
                s_hs_a = [sem(f"s_hs_a{s}") for s in range(2)]
                s_hs_v = [sem(f"s_hs_v{s}") for s in range(2)]
                s_hT = [sem(f"s_hT{s}") for s in range(2)]
                s_qkv = [sem(f"s_qkv{s}") for s in range(2)]
                s_qkc = [sem(f"s_qkc{s}") for s in range(2)]
                s_hss = [sem(f"s_hss{s}") for s in range(2)]
                s_hroot = [sem(f"s_hroot{s}") for s in range(2)]
                s_rope = [sem(f"s_rope{s}") for s in range(2)]
                s_ropeout = [sem(f"s_ropeout{s}") for s in range(2)]
                s_wqkv = sem("s_wqkv")
                s_tab = sem("s_tab")
                o_gain = sem("o_gain")
                o_act1 = sem("o_act1")
                o_dve1 = sem("o_dve1")
                s_tin = [sem(f"s_tin{s}") for s in range(2)]
                s_tT = [sem(f"s_tT{s}") for s in range(2)]
                s_tq = [sem(f"s_tq{s}") for s in range(2)]
                s_tk = [sem(f"s_tk{s}") for s in range(2)]
                s_tq_hi = [sem(f"s_tq_hi{s}") for s in range(2)]
                s_tk_hi = [sem(f"s_tk_hi{s}") for s in range(2)]
                s_tout = [sem(f"s_tout{s}") for s in range(2)]
                s_wcol = [sem(f"s_wcol{s}") for s in range(2)]
                s_zT = [sem(f"s_zT{s}") for s in range(2)]
                s_sg = sem("s_sg")
                s_glu = sem("s_glu")
                s_pad = sem("s_pad")
                o_conv = sem("o_conv")
                s_conv = sem("s_conv")
                s_gateev = [sem(f"s_gateev{s}") for s in range(2)]
                s_gateout = [sem(f"s_gateout{s}") for s in range(2)]
                s_brow = sem("s_brow")
                s_gains = sem("s_gains")
                s_warow = [sem(f"s_warow{s}") for s in range(2)]
                s_cwide = sem("s_cwide")
                s_arow = [sem(f"s_arow{s}") for s in range(2)]
                s_rowadd = [sem(f"s_rowadd{s}") for s in range(2)]
                o_rows = sem("o_rows")
                block = own.enter_context(nc.Block())

                def by_head(s, first, n):
                    return wide(3 * s, 2 * QK)[:, first * P:(first + n) * P].rearrange("p (h n) -> p h n", n=P)

                @block.sync
                def _(sp):
                    with nc.allow_non_contiguous_dma(reason="short vectors as columns"):
                        sp.dma_start(c_col, col(t["c"][0], KD)).then_inc(s_vec, 16)
                        sp.dma_start(vec[:, 0:16], col(t["b_ada"][0, 0:2 * D], 16)).then_inc(s_vec, 16)
                        sp.dma_start(vec[:, 16:24], col(t["g_pre_mix"][0], KD)).then_inc(s_vec, 16)
                    for n in range(2):
                        sp.dma_start(ada_w[n], w_ada_v[:, :, n * D:(n + 1) * D]).then_inc(s_wada[n], 16)
                    sp.dma_start(gain[:, 0:HEAD], t["q_norm_g"][0:1, :].to_broadcast([P, HEAD])).then_inc(s_tab, 16)
                    sp.dma_start(gain[:, ATT:ATT + HEAD], t["k_norm_g"][0:1, :].to_broadcast([P, HEAD])).then_inc(s_tab, 16)
                    sp.dma_start(cos_t, t["rope_cos"].rearrange("(t p) n -> p t n", p=P)).then_inc(s_tab, 16)
                    sp.dma_start(sin_t, t["rope_sin"].rearrange("(t p) n -> p t n", p=P)).then_inc(s_tab, 16)
                    sp.dma_start(w_qkv, w_in_v[:, :, COL_QKV:COL_GATE]).then_inc(s_wqkv, 16)
                    with nc.allow_non_contiguous_dma(reason="short vectors as columns"):
                        sp.dma_start(dw_b, col(t["b_dw"][0], KC)).then_inc(s_convvec, 16)
                        sp.dma_start(conv_g, col(t["conv_ln_g"][0], KC)).then_inc(s_convvec, 16)
                        sp.dma_start(conv_b, col(t["conv_ln_b"][0], KC)).then_inc(s_convvec, 16)
                        for k in range(KC):
                            sp.dma_start(dw_w[:, k, :], t["w_dw"][0, :, k * P:(k + 1) * P].rearrange("j p -> p j")
                                         ).then_inc(s_convvec, 16)
                    @turns(sp, NT // 2)
                    def _(i):
                        for s in range(2):
                            sp.wait_ge(s_xT[s], i)
                            sp.dma_start(xt[s], x_v[2 * i + s]).then_inc(s_x[s], 16)
                        for s in range(2):
                            sp.wait_ge(s_hs_a[s], i + 1)
                            sp.wait_ge(s_hs_v[s], i + 1)
                            if s == 0:
                                sp.wait_ge(s_ada_mm, 16)
                            sp.dma_start(hT[:, :, bass.ts(2 * i + s, P)], hs[s]).then_inc(s_hT[s], 16)
                        for s in range(2):
                            sp.wait_ge(s_rope[s], i + 1)
                            sp.dma_start(qk_scr[2 * i + s], roped[s]).then_inc(s_ropeout[s], 16)
                    sp.wait_ge(s_ropeout[0], 16 * (NT // 2))
                    sp.wait_ge(s_ropeout[1], 16 * (NT // 2))
                    @turns(sp, NT // 2)
                    def _(i):
                        for s in range(2):
                            sp.wait_ge(s_tT[s], i)
                            sp.dma_start(tin[s], qk_scr[2 * i + s]).then_inc(s_tin[s], 16)
                        for s in range(2):
                            sp.wait_ge(s_tq[s], i + 1)
                            sp.dma_start(q_scr[2 * i + s], qout[s].rearrange("p h a n -> p (h a n)").bitcast(F32)).then_inc(s_tout[s], 16)
                    sp.dma_start(q_scr[NT], qout[1].rearrange("p h a n -> p (h a n)").bitcast(F32)).then_inc(s_tout[1], 16)
                    sp.wait_ge(s_hT[0], 16 * (NT // 2))
                    @turns(sp, KC)
                    def _(m):
                        for s in range(2):
                            sp.wait_ge(s_zT[s], m)
                            sp.dma_start(wcol[s], w_in_v[:, :, bass.ds(m * P + s * CONV, P)]).then_inc(s_wcol[s], 16)
                    @turns(sp, KD)
                    def _(m):
                        for s in range(2):
                            sp.wait_ge(s_zT[s], m + KC)
                            sp.dma_start(wcol[s], w_in_v[:, :, bass.ds(m * 2 * P + s * P + COL_GATE, P)]
                                         ).then_inc(s_wcol[s], 16)
                        for s in range(2):
                            sp.wait_ge(s_gateev[s], m + 1)
                            sp.dma_start(gate_scr[2 * m + s], gate_out[s]).then_inc(s_gateout[s], 16)

                    w_row_v = w_ada_v[:, :, 2 * D:6 * D]
                    sp.dma_start(rows.rearrange("p a b -> p (a b)"),
                                 t["b_ada"][0:1, 2 * D:6 * D].to_broadcast([P, 4 * D])).then_inc(s_brow, 16)
                    sp.wait_ge(s_zT[0], KC + KD)
                    sp.wait_ge(s_zT[1], KC + KD)
                    for n, name in enumerate(("g_post_mix", "g_pre_ffn", "g_post_ffn")):
                        sp.dma_start(gains[:, n, :], t[name][0:1, :].to_broadcast([P, D])).then_inc(s_gains, 16)
                    @turns(sp, ROWS // 2)
                    def _(i):
                        for s in range(2):
                            sp.wait_ge(s_arow[s], i)
                            sp.dma_start(w_ada_row[s], w_row_v[:, :, bass.ts(2 * i + s, BANK)]).then_inc(s_warow[s], 16)
                    sp.wait_ge(s_tout[0], 16 * (NT // 2))
                    sp.wait_ge(s_tout[1], 16 * (NT // 2) + 16)
                    for s in range(2):
                        sp.wait_ge(s_gateout[s], 16 * KD)

                @block.gpsimd
                def _(pool):
                    order = Order(pool, sem("o_pool"))
                    order.link(nc.gpsimd.memset(ident, 0.0))
                    nc.gpsimd.affine_select(out=ident, in_=ident, compare_op=ALU.not_equal, fill=1.0, base=0,
                                            pattern=[[-1, P]], channel_multiplier=1).then_inc(s_const, 1)
                    nc.gpsimd.memset(ones, 1.0).then_inc(s_const, 1)
                    nc.gpsimd.memset(mean_w, 1.0 / CONV).then_inc(s_const, 1)
                    nc.gpsimd.memset(eps_t, EPS).then_inc(s_const, 1)
                    order.link(nc.gpsimd.memset(before, 1.0))
                    nc.gpsimd.affine_select(out=before, in_=before, compare_op=ALU.is_gt, fill=0.0, base=0,
                                            pattern=[[1, P]], channel_multiplier=-1).then_inc(s_const, 1)

                @block.scalar
                def _(act):
                    act.wait_ge(s_vec, 48)
                    nc.scalar.activation(c_silu, c_col, ACT.Silu).then_inc(s_csilu, 1)
                    act.wait_ge(s_const, 5)
                    @turns(act, NT // 2)
                    def _(i):
                        order = Order(act, o_act1, i, 2)
                        for s in range(2):
                            act.wait_ge(s_x[s], 16 * i + 16)
                            order.link(nc.scalar.activation(junk, xt[s], ACT.Square, accum_out=st[s][:, 0:1]))
                            nc.scalar.activation(st[s][:, 1:2], st[s][:, 0:1], ACT.Sqrt, bias=eps_t, scale=1.0 / D
                                                 ).then_inc(s_xroot[s], 1)
                        for s in range(2):
                            act.wait_ge(s_xT[s], i + 1)
                            act.wait_ge(s_qkv[s], i)
                            act.wait_ge(s_hT[s], 16 * i)
                            for k in range(KD // 2):
                                ins = nc.scalar.activation(hs[s][:, k, :], wide(2 * s, D)[:, k * P:(k + 1) * P],
                                                           ACT.Identity, bias=shift1[:, k:k + 1], scale=scale1[:, k:k + 1])
                            ins.then_inc(s_hs_a[s], 1)
                        for s in range(2):
                            act.wait_ge(s_qkv[s], i + 1)
                            act.wait_ge(s_rope[s], i)
                            nc.scalar.activation(qk[s], wide(4 + 2 * s, QK), ACT.Copy).then_inc(s_qkc[s], 1)
                            nc.scalar.activation(v_sb[:, 2 * i + s, :], wide(4 + 2 * s, QK + KV)[:, QK:QK + KV], ACT.Copy
                                                 ).then_inc(s_qkc[s], 1)
                            if s == 1:
                                act.wait_ge(s_hss[0], i + 1)
                            else:
                                act.wait_ge(s_hss[1], i)
                            nc.scalar.activation(sq, wide(4 + 2 * s, QK), ACT.Square).then_inc(s_qkc[s], 1)
                            act.wait_ge(s_hss[s], i + 1)
                            nc.scalar.activation(hst[s][:, 10:20], hst[s][:, 0:10], ACT.Sqrt, bias=eps_t,
                                                 scale=1.0 / HEAD).then_inc(s_hroot[s], 1)
                    @turns(act, NT // 2)
                    def _(i):
                        for s in range(2):
                            act.wait_ge(s_tT[s], i + 1)
                            act.wait_ge(s_tout[s], 16 * i)
                            nc.scalar.activation(qout[s][:, :, 0, :], by_head(s, 0, HEADS), ACT.Copy).then_inc(s_tq_hi[s], 1)
                            nc.scalar.activation(kT[:, :, bass.ts(2 * i + s, P)], by_head(s, HEADS, KV_HEADS),
                                                 ACT.Copy).then_inc(s_tk_hi[s], 1)
                    @turns(act, KC)
                    def _(m):
                        act.wait_ge(s_zT[1], m + 1)
                        act.wait_ge(s_glu, m)
                        nc.scalar.activation(sg, wide(4, S), ACT.Sigmoid).then_inc(s_sg, 1)
                    @turns(act, KD)
                    def _(m):
                        for s in range(2):
                            act.wait_ge(s_zT[s], m + KC + 1)
                            act.wait_ge(s_gateout[s], 16 * m)
                            nc.scalar.activation(gate_out[s], wide(4 * s, S), ACT.Sigmoid).then_inc(s_gateev[s], 1)

                @block.vector
                def _(dve):
                    order = Order(dve, sem("o_dve0"))
                    dve.wait_ge(s_ada_mm, 16)
                    dve.wait_ge(s_vec, 48)
                    order.link(nc.vector.tensor_tensor(shift1, banks[:, 0, 0:KD], vec[:, 0:KD], ALU.add))
                    order.link(nc.vector.tensor_tensor(scale1, banks[:, 0, KD:2 * KD], vec[:, KD:2 * KD], ALU.add))
                    order.link(nc.vector.scalar_tensor_tensor(out=scale1, in0=scale1, scalar=1.0, in1=vec[:, 16:24],
                                                              op0=ALU.add, op1=ALU.mult))
                    dve.wait_ge(s_tab, 64)
                    order.link(nc.vector.tensor_scalar(gain[:, HEAD:2 * HEAD], gain[:, 0:HEAD], HEAD ** -0.5, None, ALU.mult))
                    order.link(nc.vector.tensor_copy(gain[:, 0:HEAD], gain[:, HEAD:2 * HEAD]))
                    for h in range(2, HEADS):
                        nc.vector.tensor_copy(gain[:, h * HEAD:(h + 1) * HEAD], gain[:, HEAD:2 * HEAD])
                    order.link(nc.vector.tensor_copy(gain[:, ATT + HEAD:ATT + 2 * HEAD], gain[:, ATT:ATT + HEAD]))

                    def heads(ap):
                        return ap.rearrange("p (h d) -> p h d", d=HEAD)

                    @turns(dve, NT // 2)
                    def _(i):
                        order = Order(dve, o_dve1, i, 14)
                        for s in range(2):
                            dve.wait_ge(s_xroot[s], i + 1)
                            order.link(nc.vector.reciprocal(st[s][:, 0:1], st[s][:, 1:2]))
                            nc.vector.tensor_scalar(xt[s], xt[s], st[s][:, 0:1], None, ALU.mult).then_inc(s_xn[s], 1)
                        for s in range(2):
                            dve.wait_ge(s_xT[s], i + 1)
                            dve.wait_ge(s_qkv[s], i)
                            dve.wait_ge(s_hT[s], 16 * i)
                            for k in range(KD // 2, KD):
                                ins = nc.vector.tensor_scalar(hs[s][:, k, :], wide(2 * s, D)[:, k * P:(k + 1) * P],
                                                              scale1[:, k:k + 1], shift1[:, k:k + 1], ALU.mult, ALU.add)
                            ins.then_inc(s_hs_v[s], 1)
                        for s in range(2):
                            dve.wait_ge(s_qkc[s], 3 * i + 3)
                            nc.vector.tensor_reduce(hst[s][:, 0:10], heads(sq), AX.X, ALU.add).then_inc(s_hss[s], 1)
                            dve.wait_ge(s_hroot[s], i + 1)
                            order.link(nc.vector.reciprocal(hst[s][:, 0:10], hst[s][:, 10:20]))
                            order.link(nc.vector.tensor_tensor(
                                heads(qk[s]), heads(qk[s]),
                                hst[s][:, 0:10].rearrange("p (h o) -> p h o", o=1).to_broadcast([P, 10, HEAD]), ALU.mult))
                            order.link(nc.vector.tensor_tensor(qk[s], qk[s], gain, ALU.mult))
                            pairs = qk[s].rearrange("p (h a b n) -> p h a b n", h=10, a=2, b=2)
                            turned = rot.rearrange("p (h a b n) -> p h a b n", h=10, a=2, b=2)
                            sins = sin_t[:, 2 * i + s, :].rearrange("p (o a b n) -> p o a b n", o=1, a=2, b=2)
                            for b in range(2):
                                order.link(nc.vector.tensor_tensor(turned[:, :, :, b, :], pairs[:, :, :, 1 - b, :],
                                                                   sins[:, :, :, b, :].to_broadcast([P, 10, 2, 16]), ALU.mult))
                            cosb = cos_t[:, 2 * i + s, :].rearrange("p (o d) -> p o d", o=1)
                            order.link(nc.vector.tensor_tensor(heads(qk[s]), heads(qk[s]), cosb.to_broadcast([P, 10, HEAD]),
                                                               ALU.mult))
                            dve.wait_ge(s_ropeout[s], 16 * i)
                            twice = [a.rearrange("p (g o d) -> p g o d", o=1, d=HEAD).to_broadcast(
                                [P, HEADS + KV_HEADS, 2, HEAD]) for a in (qk[s], rot)]
                            nc.vector.tensor_tensor(roped[s].rearrange("p (g o d) -> p g o d", o=2, d=HEAD),
                                                    twice[0], twice[1], ALU.add).then_inc(s_rope[s], 1)
                            dve.wait_ge(s_rope[s], i + 1)
                    @turns(dve, NT // 2)
                    def _(i):
                        for s in range(2):
                            dve.wait_ge(s_tq_hi[s], i + 1)
                            nc.vector.tensor_tensor(qout[s][:, :, 1, :], by_head(s, 0, HEADS),
                                                    qout[s][:, :, 0, :].bitcast(F32), ALU.subtract).then_inc(s_tq[s], 1)
                            dve.wait_ge(s_tk_hi[s], i + 1)
                            upper = kT[HEAD:, :, bass.ts(2 * i + s, P)]
                            nc.vector.tensor_tensor(upper, by_head(s, HEADS, KV_HEADS)[HEAD:], upper.bitcast(F32), ALU.subtract
                                                    ).then_inc(s_tk[s], 1)
                    nc.vector.memset(glu[:, 0:PAD], 0.0).then_inc(s_pad, 1)
                    nc.vector.memset(glu[:, PAD + S:], 0.0).then_inc(s_pad, 1)
                    dve.wait_ge(s_pad, 2)
                    dve.wait_ge(s_convvec, 16 * (3 + KC))
                    @turns(dve, KC)
                    def _(m):
                        order = Order(dve, o_conv, m, TAPS)
                        dve.wait_ge(s_sg, m + 1)
                        dve.wait_ge(s_zT[0], m + 1)
                        nc.vector.tensor_tensor(glu[:, PAD:PAD + S], wide(0, S), sg, ALU.mult).then_inc(s_glu, 1)
                        dve.wait_ge(s_glu, m + 1)
                        order.link(nc.vector.tensor_scalar(conv[:, m, :], glu[:, 0:S], dw_w[:, m, 0:1], dw_b[:, bass.ds(m, 1)],
                                                           ALU.mult, ALU.add))
                        for j in range(1, TAPS):
                            order.link(nc.vector.scalar_tensor_tensor(
                                out=conv[:, m, :], in0=glu[:, j:j + S], scalar=dw_w[:, m, j:j + 1], in1=conv[:, m, :],
                                op0=ALU.mult, op1=ALU.add))

                    for k in range(KD):
                        ins = nc.vector.tensor_scalar(c_wide[:, k, :], ones, c_silu[:, k:k + 1], None, ALU.mult)
                    ins.then_inc(s_cwide, 1)
                    row_banks = rows.rearrange("p a (b n) -> p (a b) n", n=BANK)
                    dve.wait_ge(s_brow, 16)
                    @turns(dve, ROWS // 2)
                    def _(i):
                        for s in range(2):
                            dve.wait_ge(s_arow[s], i + 1)
                            nc.vector.tensor_tensor(row_banks[:, 2 * i + s, :], banks[:, s, :], row_banks[:, 2 * i + s, :],
                                                    ALU.add).then_inc(s_rowadd[s], 1)
                    order = Order(dve, o_rows)
                    dve.wait_ge(s_gains, 48)
                    for s in range(2):
                        dve.wait_ge(s_rowadd[s], ROWS // 2)
                    order.link(nc.vector.tensor_tensor(rows[:, 0, :], rows[:, 0, :], gains[:, 0, :], ALU.mult))
                    order.link(nc.vector.scalar_tensor_tensor(out=rows[:, 2, :], in0=rows[:, 2, :], scalar=1.0,
                                                              in1=gains[:, 1, :], op0=ALU.add, op1=ALU.mult))
                    order.link(nc.vector.tensor_tensor(rows[:, 3, :], rows[:, 3, :], gains[:, 2, :], ALU.mult))

                @block.tensor
                def _(pe):
                    pe.wait_ge(s_csilu, 1)
                    for n in range(16):
                        if n % KD == 0:
                            pe.wait_ge(s_wada[n // KD], 16)
                        for k in range(KD):
                            ins = nc.tensor.matmul(banks[:, 0, n:n + 1], ada_w[n // KD][:, k, (n % KD) * P:(n % KD + 1) * P],
                                                   c_silu[:, k:k + 1], start=(k == 0), stop=(k == KD - 1))
                        ins.then_inc(s_ada_mm, 1)
                    pe.wait_ge(s_const, 5)
                    pe.wait_ge(s_wqkv, 16)
                    @turns(pe, NT // 2)
                    def _(i):
                        for s in range(2):
                            pe.wait_ge(s_xn[s], i + 1)
                            pe.wait_ge(s_hs_a[s], i)
                            pe.wait_ge(s_hs_v[s], i)
                            for k in range(KD):
                                ins = nc.tensor.transpose(wide(2 * s, D)[:, k * P:(k + 1) * P], xt[s][:, k * P:(k + 1) * P],
                                                          ident)
                            ins.then_inc(s_xT[s], 1)
                        for s in range(2):
                            pe.wait_ge(s_hs_a[s], i + 1)
                            pe.wait_ge(s_hs_v[s], i + 1)
                            pe.wait_ge(s_qkc[s], 3 * i)
                            for k in range(KD):
                                nc.tensor.matmul(banks[:, 4 + 2 * s, :], hs[s][:, k, :], w_qkv[:, k, 0:ATT],
                                                 start=(k == 0), stop=(k == KD - 1))
                            for k in range(KD):
                                ins = nc.tensor.matmul(banks[:, 5 + 2 * s, 0:2 * KV], hs[s][:, k, :],
                                                       w_qkv[:, k, ATT:ATT + 2 * KV], start=(k == 0), stop=(k == KD - 1))
                            ins.then_inc(s_qkv[s], 1)
                    @turns(pe, NT // 2)
                    def _(i):
                        for s in range(2):
                            pe.wait_ge(s_tin[s], 16 * i + 16)
                            pe.wait_ge(s_tq[s], i)
                            pe.wait_ge(s_tk[s], i)
                            for j in range(HEADS + KV_HEADS):
                                ins = nc.tensor.transpose(wide(3 * s, 2 * QK)[:, j * P:(j + 1) * P],
                                                          tin[s][:, j * P:(j + 1) * P], ident)
                            ins.then_inc(s_tT[s], 1)
                    pe.wait_ge(s_hT[0], 16 * (NT // 2))
                    pe.wait_ge(s_hT[1], 16 * (NT // 2))
                    for s in range(2):
                        pe.wait_ge(s_tq[s], NT // 2)
                        pe.wait_ge(s_tk[s], NT // 2)

                    def project(s, turn):
                        pe.wait_ge(s_wcol[s], 16 * turn + 16)
                        for k in range(KD):
                            for n in range(S // BANK):
                                ins = nc.tensor.matmul(banks[:, 4 * s + n, :], wcol[s][:, k, :],
                                                       hT[:, k, n * BANK:(n + 1) * BANK], start=(k == 0), stop=(k == KD - 1))
                        ins.then_inc(s_zT[s], 1)

                    @turns(pe, KC)
                    def _(m):
                        for s in range(2):
                            pe.wait_ge(s_glu, m)
                            project(s, m)
                    @turns(pe, KD)
                    def _(m):
                        for s in range(2):
                            pe.wait_ge(s_glu, KC)
                            pe.wait_ge(s_gateev[s], m)
                            project(s, m + KC)
                    pe.wait_ge(s_cwide, 1)
                    for s in range(2):
                        pe.wait_ge(s_gateev[s], KD)
                    @turns(pe, ROWS // 2)
                    def _(i):
                        for s in range(2):
                            pe.wait_ge(s_warow[s], 16 * i + 16)
                            pe.wait_ge(s_rowadd[s], i)
                            for k in range(KD):
                                ins = nc.tensor.matmul(banks[:, s, :], c_wide[:, k, :], w_ada_row[s][:, k, :],
                                                       start=(k == 0), stop=(k == KD - 1))
                            ins.then_inc(s_arow[s], 1)
                    for s in range(2):
                        pe.wait_ge(s_rowadd[s], ROWS // 2)

            end_phase(sems)

        def attend():
            sems = []
            with ExitStack() as own:
                def sem(name):
                    sems.append(nc.alloc_semaphore(name))
                    return sems[-1]

                UNITS = 2 * HEADS
                qb = [own.enter_context(nc.sbuf_tensor(f"q_pair{p}", [P, 4 * P], F32R))[:, :] for p in range(4)]
                OWN = 5300
                take = Arena(own.enter_context(nc.sbuf_tensor("attend_buffers", [P, OWN], F32)), OWN).take
                prob = [take(HALF) for _ in range(2)]
                probT = [take(BANK) for _ in range(2)]
                neg_max, total = take(UNITS), take(UNITS)
                neg_top, fade, mass, norm, share = take(4), take(8), take(8), take(4), take(8)
                o_parts = take(8, HEAD)
                o_out = take(2, 4, HEAD)
                blank = take(D)

                def first(i):
                    return isinstance(i, int)

                s_q = [sem(f"s_q{p}") for p in range(4)]
                s_qk = [sem(f"s_qk{s}") for s in range(2)]
                s_max = [sem(f"s_max{s}") for s in range(2)]
                s_exp = [sem(f"s_exp{s}") for s in range(2)]
                s_pT = [sem(f"s_pT{g}") for g in range(2)]
                s_pTe = [sem(f"s_pTe{g}") for g in range(2)]
                s_pv = [sem(f"s_pv{g}") for g in range(2)]
                s_fade = [sem(f"s_fade{g}") for g in range(2)]
                s_faded = [sem(f"s_faded{g}") for g in range(2)]
                s_oread = [sem(f"s_oread{g}") for g in range(2)]
                s_osum = [sem(f"s_osum{g}") for g in range(2)]
                s_oout = [sem(f"s_oout{g}") for g in range(2)]
                o_join = [sem(f"o_join{g}") for g in range(2)]
                s_wmerge = sem("s_wmerge")
                s_blank, s_yblank = sem("s_blank"), sem("s_yblank")
                block = own.enter_context(nc.Block())

                @block.sync
                def _(sp):
                    for p in range(4):
                        sp.dma_start(qb[p].bitcast(F32), q_scr[0][:, p * 4 * P:(p + 1) * 4 * P]).then_inc(s_q[p], 16)
                    sp.wait_ge(s_blank, 1)
                    sp.dma_start(y_scr[2 * S:, :].rearrange("(b p) n -> p b n", p=P),
                                 blank.rearrange("p (o n) -> p o n", o=1).to_broadcast([P, BLOCKS - 2 * S // P, D])
                                 ).then_inc(s_yblank, 16)
                    for w, name in ((w_co, "w_conv_out"), (w_ao, "w_attn_out"), (w_o, "w_out")):
                        sp.dma_start(w, t[name].rearrange("l (k p) n -> p (l k) n", p=P)).then_inc(s_wmerge, 16)

                    def send(i, g):
                        sp.wait_ge(s_osum[g], i + 1)
                        sp.dma_start(o_scr[i][:, g * 4 * HEAD:(g + 1) * 4 * HEAD],
                                     o_out[:, g].rearrange("p a b -> p (a b)")).then_inc(s_oout[g], 16)

                    @turns(sp, NT)
                    def _(i):
                        for p in range(4):
                            sp.wait_ge(s_qk[1], 8 * i + 2 * p + 2)
                            sp.dma_start(qb[p].bitcast(F32), q_scr[i + 1][:, p * 4 * P:(p + 1) * 4 * P]).then_inc(s_q[p], 16)
                            if p == 1 and not first(i):
                                send(i - 1, 1)
                        send(i, 0)
                    send(NT - 1, 1)
                    for p in range(4):
                        sp.wait_ge(s_q[p], 16 * NT + 16)
                    for g in range(2):
                        sp.wait_ge(s_oout[g], 16 * NT)
                    sp.wait_ge(s_wmerge, 48)
                    sp.wait_ge(s_yblank, 16)

                @block.scalar
                def _(act):
                    def fade_group(i, g):
                        act.wait_ge(s_fade[g], i + 1)
                        nc.scalar.activation(fade, fade, ACT.Exp).then_inc(s_faded[g], 1)

                    def exp(s, turn, u):
                        act.wait_ge(s_max[s], turn)
                        nc.scalar.activation(prob[s], wide(2 * s, HALF), ACT.Exp, bias=neg_max[:, u:u + 1],
                                             accum_out=total[:, u:u + 1]).then_inc(s_exp[s], 1)

                    exp(0, 1, 0)
                    @turns(act, NT)
                    def _(i):
                        for u in range(UNITS):
                            act.wait_ge(s_pT[0], UNITS * i + u + 1)
                            nc.scalar.activation(probT[0], banks[:, 4, :], ACT.Copy).then_inc(s_pTe[0], 1)
                            if u + 1 < UNITS:
                                exp((u + 1) % 2, 8 * i + (u + 1) // 2 + 1, u + 1)
                            else:
                                exp(0, 8 * i + 9, 0)
                            if u == 9:
                                fade_group(i, 0)
                            if u == 1 and not first(i):
                                fade_group(i - 1, 1)
                    fade_group(NT - 1, 1)

                @block.vector
                def _(dve):
                    JOIN = range(5)
                    nc.vector.memset(blank, 0.0).then_inc(s_blank, 1)

                    def unit_max(s, turn, u):
                        dve.wait_ge(s_qk[s], turn)
                        nc.vector.tensor_reduce(neg_max[:, u:u + 1], wide(2 * s, HALF), AX.X, ALU.max, negate=True
                                                ).then_inc(s_max[s], 1)

                    halves = lambda a: a.rearrange("p (h o) -> p h o", o=2)
                    one = lambda a: a.rearrange("p (h o) -> p h o", o=1)

                    def join_halves(step, i, g):
                        order = Order(dve, o_join[g], i, 5, (0, 1, 3, 5, 5)[step])
                        nm = halves(neg_max[:, 8 * g:8 * g + 8])
                        if step == 0:
                            order.link(nc.vector.tensor_reduce(neg_top, nm, AX.X, ALU.min))
                            nc.vector.tensor_tensor(halves(fade), one(neg_top).to_broadcast([P, 4, 2]), nm, ALU.subtract
                                                    ).then_inc(s_fade[g], 1)
                        elif step == 1:
                            dve.wait_ge(s_faded[g], i + 1)
                            order.link(nc.vector.tensor_tensor(mass, fade, total[:, 8 * g:8 * g + 8], ALU.mult))
                            order.link(nc.vector.tensor_reduce(norm, halves(mass), AX.X, ALU.add))
                        elif step == 2:
                            order.link(nc.vector.reciprocal(norm, norm))
                            order.link(nc.vector.tensor_tensor(halves(share), halves(fade),
                                                               one(norm).to_broadcast([P, 4, 2]), ALU.mult))
                        elif step == 3:
                            dve.wait_ge(s_pv[1], UNITS * i + 8 * g + 8)
                            nc.vector.tensor_tensor(o_parts, banks[:, 6 + g, :].rearrange("p (u d) -> p u d", d=HEAD),
                                                    one(share).to_broadcast([P, 8, HEAD]), ALU.mult).then_inc(s_oread[g], 1)
                        else:
                            dve.wait_ge(s_oread[g], i + 1)
                            dve.wait_ge(s_oout[g], 16 * i)
                            parts = o_parts.rearrange("p (h o) d -> p h o d", o=2)
                            nc.vector.tensor_tensor(o_out[:, g], parts[:, :, 0, :], parts[:, :, 1, :], ALU.add
                                                    ).then_inc(s_osum[g], 1)

                    unit_max(0, 1, 0)
                    @turns(dve, NT)
                    def _(i):
                        for u in range(UNITS):
                            if u + 1 < UNITS:
                                unit_max((u + 1) % 2, 8 * i + (u + 1) // 2 + 1, u + 1)
                            else:
                                unit_max(0, 8 * i + 9, 0)
                            dve.wait_ge(s_pT[1], UNITS * i + u + 1)
                            nc.vector.tensor_copy(probT[1], banks[:, 5, :]).then_inc(s_pTe[1], 1)
                            if 8 <= u < 13:
                                join_halves(JOIN[u - 8], i, 0)
                            if u < 5 and not first(i):
                                join_halves(JOIN[u], i - 1, 1)
                    for step in JOIN:
                        join_halves(step, NT - 1, 1)

                @block.tensor
                def _(pe):
                    def q_of(h, part):
                        at = (2 * (h % 2) + part) * P
                        return qb[h // 2][:, at:at + P]

                    def scores(u, turn_q, turn_exp):
                        h, half = u // 2, u % 2
                        pe.wait_ge(s_q[h // 2], turn_q)
                        pe.wait_ge(s_exp[u % 2], turn_exp)
                        for n in range(HALF // BANK):
                            key = half * HALF + n * BANK
                            for part in range(2):
                                ins = nc.tensor.matmul(banks[:, 2 * (u % 2) + n, :], q_of(h, part),
                                                       kT[:, h // 4, key:key + BANK], start=(part == 0), stop=(part == 1))
                        ins.then_inc(s_qk[u % 2], 1)

                    def turn_probs(i, u, g):
                        pe.wait_ge(s_exp[u % 2], 8 * i + u // 2 + 1)
                        pe.wait_ge(s_pTe[g], UNITS * i + u)
                        for j in range(4):
                            ins = nc.tensor.transpose(banks[:, 4 + g, j * P:(j + 1) * P],
                                                      prob[u % 2][:, (4 * g + j) * P:(4 * g + j + 1) * P], ident)
                        ins.then_inc(s_pT[g], 1)

                    def values(i, u, g):
                        kv, half = u // 8, u % 2
                        pe.wait_ge(s_pTe[g], UNITS * i + u + 1)
                        if u % 8 == 0 and g == 0:
                            pe.wait_ge(s_oread[kv], i)
                        for j in range(4):
                            ins = nc.tensor.matmul(banks[:, 6 + kv, (u % 8) * HEAD:(u % 8 + 1) * HEAD],
                                                   probT[g][:, j * P:(j + 1) * P],
                                                   v_sb[:, half * 8 + 4 * g + j, kv * HEAD:(kv + 1) * HEAD],
                                                   start=(g == 0 and j == 0), stop=(g == 1 and j == 3))
                        ins.then_inc(s_pv[g], 1)

                    scores(0, 16, 0)
                    @turns(pe, NT)
                    def _(i):
                        for u in range(UNITS):
                            if u + 1 < UNITS:
                                scores(u + 1, 16 * i + 16, 8 * i + (u + 1) // 2)
                            else:
                                scores(0, 16 * i + 32, 8 * i + 8)
                            turn_probs(i, u, 0)
                            if u:
                                values(i, u - 1, 1)
                            turn_probs(i, u, 1)
                            values(i, u, 0)
                        values(i, UNITS - 1, 1)

                    pe.wait_ge(s_oread[0], NT)
                    pe.wait_ge(s_oread[1], NT)
                    pe.wait_ge(s_max[0], 8 * NT + 1)

            end_phase(sems)

        def merge():
            sems = []
            with ExitStack() as own:
                def sem(name):
                    sems.append(nc.alloc_semaphore(name))
                    return sems[-1]

                OWN = 20400
                take = Arena(own.enter_context(nc.sbuf_tensor("merge_buffers", [P, OWN], F32)), OWN).take
                o_in = take(CH // P, ATT)
                squares = o_in.rearrange("p a b -> p (a b)").rearrange("p (k n) -> p k n", n=CH)
                oT = take(KC, CH)
                cT = take(KC, CH)
                gate_a = take(KD, CH)
                gate_c = take(KD, CH)
                inv_dev = take(CH)
                xm = [take(D) for _ in range(2)]
                ym = [take(D) for _ in range(2)]
                h2T = take(KD, P)
                w_r = take(KD, LOGITS)
                mst = [take(4) for _ in range(2)]

                s_rb = sem("s_rb")
                s_oin = sem("s_oin")
                s_ga, s_gc = sem("s_ga"), sem("s_gc")
                s_mu, s_centred, s_sq, s_var, s_dev = sem("s_mu"), sem("s_centred"), sem("s_sq"), sem("s_var"), sem("s_dev")
                s_cnorm, s_cT = sem("s_cnorm"), sem("s_cT")
                s_oT = sem("s_oT")
                s_oTa, s_oTv = sem("s_oTa"), sem("s_oTv")
                s_branch = [sem(f"s_branch{b}") for b in range(2)]
                s_used = [sem(f"s_used{b}") for b in range(2)]
                s_merged = sem("s_merged")
                s_wout = [sem(f"s_wout{b}") for b in range(2)]
                s_xm = [sem(f"s_xm{b}") for b in range(2)]
                s_ydev = [sem(f"s_ydev{b}") for b in range(2)]
                s_x1 = [sem(f"s_x1{b}") for b in range(2)]
                s_x1out = [sem(f"s_x1out{b}") for b in range(2)]
                s_x1dev = [sem(f"s_x1dev{b}") for b in range(2)]
                s_h2 = [sem(f"s_h2{b}") for b in range(2)]
                s_h2out = [sem(f"s_h2out{b}") for b in range(2)]
                s_h2T, s_h2Ta, s_h2Tv = sem("s_h2T"), sem("s_h2Ta"), sem("s_h2Tv")
                s_logit, s_logitc = sem("s_logit"), sem("s_logitc")
                o_merge, o_mact = sem("o_merge"), sem("o_mact")
                block = own.enter_context(nc.Block())

                @block.sync
                def _(sp):
                    with nc.allow_non_contiguous_dma(reason="36 columns of two matrices"):
                        sp.dma_start(w_r[:, :, 0:GROUPS], t["w_group"].rearrange("l (k p) n -> p (l k) n", p=P)
                                     ).then_inc(s_rb, 16)
                        sp.dma_start(w_r[:, :, GROUPS:], t["w_router"].rearrange("l (k p) n -> p (l k) n", p=P)
                                     ).then_inc(s_rb, 16)
                    sp.dma_start(rbias[:, 0:GROUPS], t["b_group"][0:1, :].to_broadcast([P, GROUPS])).then_inc(s_rb, 16)
                    sp.dma_start(rbias[:, GROUPS:], t["b_router"][0:1, :].to_broadcast([P, EXPERTS])).then_inc(s_rb, 16)
                    @turns(sp, NC)
                    def _(i):
                        sp.wait_ge(s_var, i)
                        sp.dma_start(o_in, o_scr.rearrange("(c t) p n -> c p t n", c=NC)[i]).then_inc(s_oin, 16)
                        for b in range(2):
                            sp.wait_ge(s_wout[b], 2 * i)
                        for gate, sm, first_tile in ((gate_a, s_ga, KD), (gate_c, s_gc, 0)):
                            sp.dma_start(gate, gate_scr[first_tile:first_tile + KD, :, bass.ts(i, CH)]
                                         .rearrange("k p n -> p k n")).then_inc(sm, 16)
                        for j in range(CH // P):
                            b, n = j % 2, 2 * i + j // 2
                            sp.wait_ge(s_x1out[b], 16 * n)
                            sp.dma_start(xm[b], x_v[4 * i + j]).then_inc(s_xm[b], 16)
                            if j % 2:
                                for b in range(2):
                                    sp.wait_ge(s_x1[b], n + 1)
                                    sp.dma_start(x1_scr[bass.ds(i * CH + (j - 1 + b) * P, P), :], xm[b]
                                                 ).then_inc(s_x1out[b], 16)
                                    sp.wait_ge(s_h2[b], n + 1)
                                    sp.dma_start(h2_scr[bass.ds(i * CH + (j - 1 + b) * P, P), :], ym[b]
                                                 ).then_inc(s_h2out[b], 16)
                    for b in range(2):
                        sp.wait_ge(s_x1out[b], 16 * (NT // 2))
                        sp.wait_ge(s_h2out[b], 16 * (NT // 2))

                @block.scalar
                def _(act):
                    @turns(act, NC)
                    def _(i):
                        order = Order(act, o_mact, i, 2 * (CH // P))
                        act.wait_ge(s_oT, i + 1)
                        for j in range(2):
                            ins = nc.scalar.activation(oT[:, j, :], banks[:, 1 + j, :], ACT.Copy)
                        ins.then_inc(s_oTa, 1)
                        act.wait_ge(s_centred, i + 1)
                        nc.scalar.activation(squares, cT, ACT.Square).then_inc(s_sq, 1)
                        act.wait_ge(s_var, i + 1)
                        nc.scalar.activation(inv_dev, banks[:, 0, :], ACT.Sqrt, bias=eps_t).then_inc(s_dev, 1)
                        act.wait_ge(s_cnorm, i + 1)
                        for k in range(KC):
                            ins = nc.scalar.activation(cT[:, k, :], cT[:, k, :], ACT.Silu, bias=conv_b[:, k:k + 1],
                                                       scale=conv_g[:, k:k + 1])
                        ins.then_inc(s_cT, 1)

                        def h2T_out(n):
                            act.wait_ge(s_h2T, n + 1)
                            nc.scalar.activation(h2T[:, 0:4, :], banks[:, 5, :].rearrange("p (k n) -> p k n", n=P), ACT.Copy
                                                 ).then_inc(s_h2Ta, 1)

                        for j in range(CH // P):
                            b, n = j % 2, 2 * i + j // 2
                            y = wide(1 + 2 * b, D)
                            act.wait_ge(s_wout[b], n + 1)
                            act.wait_ge(s_h2out[b], 16 * n)
                            act.wait_ge(s_h2Tv, 4 * i + j - 1 if j else 4 * i)
                            order.link(nc.scalar.activation(ym[b], y, ACT.Square, accum_out=mst[b][:, 0:1]))
                            nc.scalar.activation(mst[b][:, 1:2], mst[b][:, 0:1], ACT.Sqrt, bias=eps_t, scale=1.0 / D
                                                 ).then_inc(s_ydev[b], 1)
                            act.wait_ge(s_x1[b], n + 1)
                            order.link(nc.scalar.activation(ym[b], xm[b], ACT.Square, accum_out=mst[b][:, 2:3]))
                            nc.scalar.activation(mst[b][:, 3:4], mst[b][:, 2:3], ACT.Sqrt, bias=eps_t, scale=1.0 / D
                                                 ).then_inc(s_x1dev[b], 1)
                            if j:
                                h2T_out(4 * i + j - 1)
                        h2T_out(4 * i + 3)

                @block.vector
                def _(dve):
                    @turns(dve, NC)
                    def _(i):
                        order = Order(dve, o_merge, i, 1 + 4 * (CH // P))
                        dve.wait_ge(s_oT, i + 1)
                        for j in range(2, 4):
                            ins = nc.vector.tensor_copy(oT[:, j, :], banks[:, 1 + j, :])
                        ins.then_inc(s_oTv, 1)
                        dve.wait_ge(s_mu, i + 1)
                        one = banks[:, 0, :].rearrange("p (o n) -> p o n", o=1).to_broadcast([P, KC, CH])
                        nc.vector.tensor_tensor(cT, conv[:, :, bass.ts(i, CH)], one, ALU.subtract).then_inc(s_centred, 1)
                        dve.wait_ge(s_ga, 16 * i + 16)

                        def branch(d, gate, fold):
                            n = 8 * i + (KD + d if fold else d) // 2 + 1
                            dve.wait_ge(s_branch[d % 2], n)
                            ins = nc.vector.tensor_tensor(gate[:, d, :], banks[:, 5 + d % 2, :], gate[:, d, :], ALU.mult)
                            ins.then_inc(s_used[d % 2], 1)
                            if fold:
                                dve.wait_ge(s_used[d % 2], n)
                                nc.vector.tensor_tensor(gate_a[:, d, :], gate_a[:, d, :], gate_c[:, d, :], ALU.add
                                                        ).then_inc(s_merged, 1)

                        for d in range(2):
                            branch(d, gate_a, False)
                        dve.wait_ge(s_dev, i + 1)
                        order.link(nc.vector.reciprocal(inv_dev, inv_dev))
                        nc.vector.tensor_tensor(cT, cT, inv_dev.rearrange("p (o n) -> p o n", o=1).to_broadcast([P, KC, CH]),
                                                ALU.mult).then_inc(s_cnorm, 1)
                        for d in range(2, KD):
                            branch(d, gate_a, False)
                        dve.wait_ge(s_gc, 16 * i + 16)
                        for d in range(KD):
                            branch(d, gate_c, True)

                        def h2T_out(n):
                            dve.wait_ge(s_h2T, n + 1)
                            nc.vector.tensor_copy(h2T[:, 4:8, :], banks[:, 6, :].rearrange("p (k n) -> p k n", n=P)
                                                  ).then_inc(s_h2Tv, 1)
                            dve.wait_ge(s_logit, n + 1)
                            nc.vector.tensor_copy(logits[:, bass.ds(n, 1), :].rearrange("p a b -> p (a b)"),
                                                  banks[:, 7, 0:LOGITS]).then_inc(s_logitc, 1)

                        for j in range(CH // P):
                            b, n = j % 2, 2 * i + j // 2
                            y = wide(1 + 2 * b, D)
                            dve.wait_ge(s_ydev[b], n + 1)
                            order.link(nc.vector.reciprocal(mst[b][:, 0:1], mst[b][:, 1:2]))
                            order.link(nc.vector.scalar_tensor_tensor(out=ym[b], in0=y, scalar=mst[b][:, 0:1],
                                                                      in1=rows[:, 0, :], op0=ALU.mult, op1=ALU.mult))
                            dve.wait_ge(s_xm[b], 16 * n + 16)
                            nc.vector.tensor_tensor(xm[b], xm[b], ym[b], ALU.add).then_inc(s_x1[b], 1)
                            dve.wait_ge(s_x1dev[b], n + 1)
                            order.link(nc.vector.reciprocal(mst[b][:, 2:3], mst[b][:, 3:4]))
                            order.link(nc.vector.scalar_tensor_tensor(out=ym[b], in0=xm[b], scalar=mst[b][:, 2:3],
                                                                      in1=rows[:, 2, :], op0=ALU.mult, op1=ALU.mult))
                            nc.vector.tensor_tensor(ym[b], ym[b], rows[:, 1, :], ALU.add).then_inc(s_h2[b], 1)
                            if j:
                                h2T_out(4 * i + j - 1)
                        h2T_out(4 * i + 3)

                @block.tensor
                def _(pe):
                    pe.wait_ge(s_rb, 64)
                    @turns(pe, NC)
                    def _(i):
                        pe.wait_ge(s_dev, i)
                        for k in range(KC):
                            ins = nc.tensor.matmul(banks[:, 0, :], mean_w, conv[:, k, bass.ts(i, CH)],
                                                   start=(k == 0), stop=(k == KC - 1))
                        ins.then_inc(s_mu, 1)
                        pe.wait_ge(s_oin, 16 * i + 16)
                        for b in range(2):
                            pe.wait_ge(s_h2[b], 2 * i)
                        for j in range(KC):
                            for n in range(CH // P):
                                ins = nc.tensor.transpose(banks[:, 1 + j, n * P:(n + 1) * P], o_in[:, n, j * P:(j + 1) * P],
                                                          ident)
                        ins.then_inc(s_oT, 1)
                        pe.wait_ge(s_oTa, i + 1)
                        pe.wait_ge(s_oTv, i + 1)
                        pe.wait_ge(s_logitc, 4 * i)

                        def branch(d, w, src, turn):
                            pe.wait_ge(s_used[d % 2], turn)
                            for k in range(KC):
                                ins = nc.tensor.matmul(banks[:, 5 + d % 2, :], w[:, k, d * P:(d + 1) * P], src[:, k, :],
                                                       start=(k == 0), stop=(k == KC - 1))
                            ins.then_inc(s_branch[d % 2], 1)

                        for d in range(KD):
                            branch(d, w_ao, oT, 8 * i + d // 2)
                            if d == 1:
                                pe.wait_ge(s_sq, i + 1)
                                for k in range(KC):
                                    ins = nc.tensor.matmul(banks[:, 0, :], mean_w, squares[:, k, :],
                                                           start=(k == 0), stop=(k == KC - 1))
                                ins.then_inc(s_var, 1)
                        pe.wait_ge(s_cT, i + 1)
                        for d in range(KD):
                            branch(d, w_co, cT, 8 * i + 4 + d // 2)
                        pe.wait_ge(s_merged, KD * i + KD)

                        def route_logits(n, b, turn):
                            pe.wait_ge(s_h2[b], turn + 1)
                            pe.wait_ge(s_h2Ta, n)
                            pe.wait_ge(s_h2Tv, n)
                            for k in range(KD):
                                ins = nc.tensor.transpose(banks[:, 5 + k // 4, (k % 4) * P:(k % 4 + 1) * P],
                                                          ym[b][:, k * P:(k + 1) * P], ident)
                            ins.then_inc(s_h2T, 1)
                            pe.wait_ge(s_h2Ta, n + 1)
                            pe.wait_ge(s_h2Tv, n + 1)
                            pe.wait_ge(s_logitc, n)
                            for k in range(KD):
                                ins = nc.tensor.matmul(banks[:, 7, 0:LOGITS], h2T[:, k, :], w_r[:, k, :],
                                                       start=(k == 0), stop=(k == KD - 1))
                            ins.then_inc(s_logit, 1)

                        for j in range(CH // P):
                            b, n = j % 2, 2 * i + j // 2
                            pe.wait_ge(s_h2[b], n)
                            for o in range(2):
                                for k in range(KD):
                                    ins = nc.tensor.matmul(banks[:, 1 + 2 * b + o, :], gate_a[:, k, j * P:(j + 1) * P],
                                                           w_o[:, k, o * BANK:(o + 1) * BANK],
                                                           start=(k == 0), stop=(k == KD - 1))
                            ins.then_inc(s_wout[b], 1)
                            if j:
                                route_logits(4 * i + j - 1, 1 - b, 2 * i + (j - 1) // 2)
                        route_logits(4 * i + 3, 1, 2 * i + 1)

            end_phase(sems)

        def experts():
            sems = []
            with ExitStack() as own:
                def sem(name):
                    sems.append(nc.alloc_semaphore(name))
                    return sems[-1]

                def tensor(name, size, dt=F32):
                    return own.enter_context(nc.sbuf_tensor(name, [P, size], dt))

                def halves(name, a, n):
                    return [tensor(f"{name}_{part}", a * n, F32R)[:, :].rearrange("p (k n) -> p k n", n=n)
                            for part in ("hi", "lo")]

                lists = Arena(tensor("lists", 1500), 1500)
                iota = lists.take(P)
                iota_i = lists.take(P).bitcast(I32)
                token = lists.take(NT)
                token_i = lists.take(NT).bitcast(I32)
                slots_of = lists.take(2, NT)
                slots_i = lists.take(2, NT).bitcast(I32)
                slots_hi = lists.take(2, NT)
                slots_lo = lists.take(2, NT)
                weights = lists.take(2, NT)
                block_expert = lists.take(BLOCKS)
                block_expert_i = lists.take(BLOCKS).bitcast(I32)
                load = lists.take(BLOCKS + 1)
                load_i = lists.take(BLOCKS + 1).bitcast(I32)
                y_count, y_count_i = lists.take(2), lists.take(2).bitcast(I32)
                slot_token = lists.take(BLOCKS).bitcast(I32)
                zeros = lists.take(P)

                stage = [tensor(f"stage_{n}", KD * D_EXPERT)[:, :] for n in ("gate", "up", "down")]
                w_g = halves("w_gate", KD, D_EXPERT)
                w_u = halves("w_up", KD, D_EXPERT)
                w_d = halves("w_down", KF, D)
                xT = halves("x_T", KD, P)
                actT = halves("act_T", KF, P)
                xg = [tensor(f"x_rows{n}", D)[:, :] for n in range(2)]
                act_g = tensor("act_gate", D_EXPERT)[:, :]
                act_u = tensor("act_up", D_EXPERT)[:, :]
                ys = [tensor(f"y_rows{n}", D)[:, :] for n in range(2)]

                tables = [Arena(s, KD * D_EXPERT) for s in stage]
                take = tables[0].take
                in_block = [take(P) for _ in range(2)]
                of_block = [take(BLOCKS) for _ in range(2)]
                top_g, sum_g, exp_g = take(NT), take(NT), take(NT, GROUPS)
                hot_g, cand_g, first_g = take(NT, GROUPS), take(NT, GROUPS), take(NT)
                masked = take(NT, EXPERTS)
                cand = take(NT, EXPERTS)
                hot = [take(NT, EXPERTS) for _ in range(2)]
                picked = take(NT, EXPERTS)
                top, first = [take(NT) for _ in range(2)], take(NT)
                ratio = take(NT)
                base = tables[1].take(NT + 1, EXPERTS)
                blocks_of = tables[1].take(EXPERTS, NT)
                run = [tables[1].take(EXPERTS) for _ in range(2)]
                counts = tables[1].take(EXPERTS)
                used = tables[1].take(EXPERTS)
                exists = tables[1].take(BLOCKS)
                reached = tables[2].take(BLOCKS, EXPERTS)

                yj = [[stage[n][:, a * D:(a + 1) * D] for a in range(2)] for n in range(2)]
                xj = [stage[2][:, n * D:(n + 1) * D] for n in range(2)]
                jjunk = stage[2][:, 2 * D:3 * D]
                jst = [stage[2][:, 3 * D + 2 * n:3 * D + 2 * n + 2] for n in range(2)]

                o_route = sem("o_route")
                s_iota = sem("s_iota")
                s_gdiff, s_gexp, s_ediff, s_eexp = sem("s_gdiff"), sem("s_gexp"), sem("s_ediff"), sem("s_eexp")
                s_picked, s_rank = sem("s_picked"), sem("s_rank")
                s_onehot = [sem(f"s_onehot{a}") for a in range(2)]
                s_list = [sem(f"s_list{a}") for a in range(2)]
                s_blocks, s_lists = sem("s_blocks"), sem("s_lists")
                s_w = [sem(f"s_w_{n}") for n in ("gate", "up", "down")]
                s_hi = [sem(f"s_hi_{n}") for n in ("gate", "up", "down")]
                s_lo = [sem(f"s_lo_{n}") for n in ("gate", "up", "down")]
                s_xg = [sem(f"s_xg{s}") for s in range(2)]
                s_xgT, s_xT_hi, s_xT_lo = sem("s_xgT"), sem("s_xT_hi"), sem("s_xT_lo")
                s_gate, s_up, s_down = sem("s_gate"), sem("s_up"), sem("s_down")
                s_silu, s_act, s_actT = sem("s_silu"), sem("s_act"), sem("s_actT")
                s_actT_hi, s_actT_lo = sem("s_actT_hi"), sem("s_actT_lo")
                s_ya, s_yv = sem("s_ya"), sem("s_yv")
                s_yout = [sem(f"s_yout{s}") for s in range(2)]
                s_y = sem("s_y")
                s_yj = [sem(f"s_yj{s}") for s in range(2)]
                s_xj = [sem(f"s_xj{s}") for s in range(2)]
                s_jsum = [sem(f"s_jsum{s}") for s in range(2)]
                s_jdev = [sem(f"s_jdev{s}") for s in range(2)]
                s_jout = [sem(f"s_jout{s}") for s in range(2)]
                s_out = [sem(f"s_out{s}") for s in range(2)]
                o_jdve, o_jact = sem("o_jdve"), sem("o_jact")
                block = own.enter_context(nc.Block())
                flat = lambda a: a.rearrange("p a b -> p (a b)")

                def load_of(eng, j):
                    at = load_i[0:1, j:j + 1] if isinstance(j, int) else load_i[0:1, bass.ds(j, 1)]
                    return eng.value_load(at, min_val=0, max_val=EXPERTS)

                def loads_of(eng, j):
                    return load_of(eng, j), load_of(eng, j + 1)

                def blocks(eng):
                    def run(body):
                        def block_pair(i):
                            for s in range(2):
                                j = 2 * i + s
                                this = load_of(eng, j)
                                with eng.If(this > 0):
                                    after = load_of(eng, j + 1)

                                    def more(step):
                                        with eng.If(after > 0):
                                            step()

                                    def new(step):
                                        with eng.If(after > this):
                                            step(after)

                                    body(j, s, i, more, new)
                        block_pair(0)
                        with eng.Fori(1, BLOCKS // 2) as i:
                            block_pair(i)
                    return run

                @block.sync
                def _(sp):
                    names = ("w_e_gate", "w_e_up", "w_e_down")

                    def fetch(j, before):
                        e = sp.value_load(block_expert_i[0:1, j:j + 1] if isinstance(j, int)
                                          else block_expert_i[0:1, bass.ds(j, 1)], min_val=0, max_val=EXPERTS - 1)
                        for n in range(3):
                            if before is not None:
                                sp.wait_ge(s_hi[n], before)
                                sp.wait_ge(s_lo[n], before)
                            sp.dma_start(stage[n].rearrange("p (k n) -> p k n", n=(D_EXPERT, D_EXPERT, D)[n]),
                                         t[names[n]][0, bass.ds(e, 1)].rearrange("e (k p) n -> p (e k) n", p=P)
                                         ).then_inc(s_w[n], 16)

                    sp.wait_ge(s_blocks, 1)
                    sp.wait_ge(s_lists, 1)
                    fetch(0, None)
                    with sp.Fori(1, BLOCKS) as j:
                        last, this = loads_of(sp, j - 1)
                        with sp.If(this > last):
                            fetch(j, last)
                    sp.wait_ge(s_y, 1)
                    @turns(sp, NT // 2)
                    def _(i):
                        for s in range(2):
                            sp.wait_ge(s_out[s], 16 * i)
                            sp.dma_start(xj[s], x1_scr[bass.ts(2 * i + s, P), :]).then_inc(s_xj[s], 16)
                        for s in range(2):
                            sp.wait_ge(s_jout[s], i + 1)
                            sp.dma_start(out_v[2 * i + s], xj[s]).then_inc(s_out[s], 16)
                    for s in range(2):
                        sp.wait_ge(s_out[s], 16 * (NT // 2))

                @block.gpsimd
                def _(pool):
                    nc.gpsimd.iota(iota_i, [[1, P]], base=0, channel_multiplier=0).then_inc(s_iota, 1)
                    nc.gpsimd.iota(token_i, [[P, NT]], base=0, channel_multiplier=1).then_inc(s_iota, 1)
                    pool.wait_ge(s_lists, 1)
                    for j in range(BLOCKS):
                        s = j % 2

                        def gather(j=j, s=s):
                            if j >= 2:
                                pool.wait_ge(s_xgT, j - 1)
                            nc.gpsimd.indirect_dma_start(out=xg[s], out_offset=None, in_=h2_scr[:, :],
                                                         in_offset=bass.IndirectOffsetOnAxis(
                                                             ap=slot_token[:, j:j + 1], axis=0)).then_inc(s_xg[s], 16)

                        if j < 2 * S // P:
                            gather()
                        else:
                            this = pool.value_load(load_i[0:1, j:j + 1], min_val=0, max_val=EXPERTS)
                            with pool.If(this > 0):
                                gather()
                    pool.wait_ge(s_y, 1)
                    for n in range(NT):
                        s = n % 2
                        pool.wait_ge(s_jout[s], n // 2)
                        for a in range(2):
                            nc.gpsimd.indirect_dma_start(out=yj[s][a], out_offset=None, in_=y_scr[:, :],
                                                         in_offset=bass.IndirectOffsetOnAxis(
                                                             ap=slots_i[:, a, n:n + 1], axis=0)).then_inc(s_yj[s], 16)

                @block.scalar
                def _(act):
                    act.wait_ge(s_gdiff, 1)
                    nc.scalar.activation(exp_g, exp_g, ACT.Exp).then_inc(s_gexp, 1)
                    act.wait_ge(s_ediff, 1)
                    nc.scalar.activation(ratio, ratio, ACT.Exp).then_inc(s_eexp, 1)
                    def split(n, w, this):
                        act.wait_ge(s_w[n], 16 * this)
                        nc.scalar.activation(flat(w[0]), stage[n], ACT.Copy).then_inc(s_hi[n], 1)

                    def xT_out(turn):
                        act.wait_ge(s_xgT, turn)
                        nc.scalar.activation(flat(xT[0]), wide(2, D), ACT.Copy).then_inc(s_xT_hi, 1)

                    act.wait_ge(s_lists, 1)
                    for n, w in enumerate((w_g, w_u, w_d)):
                        split(n, w, 1)
                    xT_out(1)
                    @blocks(act)
                    def _(j, s, i, more, new):
                        act.wait_ge(s_gate, j + 1)
                        nc.scalar.activation(act_g, banks[:, 0, :], ACT.Silu).then_inc(s_silu, 1)
                        new(lambda this: split(0, w_g, this))
                        act.wait_ge(s_actT, j + 1)
                        nc.scalar.activation(flat(actT[0]), banks[:, 4, :], ACT.Copy).then_inc(s_actT_hi, 1)
                        more(lambda: xT_out(j + 2))
                        new(lambda this: split(1, w_u, this))
                        act.wait_ge(s_down, j + 1)
                        act.wait_ge(s_yout[s], 16 * i)
                        nc.scalar.activation(ys[s][:, 0:BANK], banks[:, 5, :], ACT.Copy).then_inc(s_ya, 1)
                        act.wait_ge(s_ya, j + 1)
                        act.wait_ge(s_yv, j + 1)
                        act.dma_start(y_scr[bass.ds(j * P, P), :], ys[s]).then_inc(s_yout[s], 16)
                        new(lambda this: split(2, w_d, this))
                    sent = [act.value_load(y_count_i[0:1, s:s + 1], min_val=16, max_val=16 * BLOCKS) for s in range(2)]
                    for s in range(2):
                        act.wait_ge(s_yout[s], sent[s])
                    nc.scalar.activation(act_g, act_g, ACT.Copy).then_inc(s_y, 1)
                    @turns(act, NT // 2)
                    def _(i):
                        order = Order(act, o_jact, i, 2)
                        for s in range(2):
                            act.wait_ge(s_jsum[s], i + 1)
                            order.link(nc.scalar.activation(jjunk, yj[s][0], ACT.Square, accum_out=jst[s][:, 0:1]))
                            nc.scalar.activation(jst[s][:, 1:2], jst[s][:, 0:1], ACT.Sqrt, bias=eps_t, scale=1.0 / D
                                                 ).then_inc(s_jdev[s], 1)

                @block.vector
                def _(dve):
                    order = Order(dve, o_route)
                    L = order.link
                    tt, ts = nc.vector.tensor_tensor, nc.vector.tensor_scalar

                    def over(ap, n):
                        return ap.rearrange("p (a o) -> p a o", o=1).to_broadcast([P, ap.shape[1], n])

                    def along(ap, n):
                        return ap.rearrange("p (o a) -> p o a", o=1).to_broadcast([P, n, ap.shape[1]])

                    dve.wait_ge(s_iota, 2)
                    L(nc.vector.tensor_copy(iota, iota_i))
                    L(nc.vector.tensor_copy(token, token_i))
                    L(nc.vector.memset(zeros, 0.0))
                    L(tt(logits, logits, along(rbias, NT), ALU.add))
                    lg, le = logits[:, :, 0:GROUPS], logits[:, :, GROUPS:]
                    L(nc.vector.tensor_reduce(top_g, lg, AX.X, ALU.max))
                    tt(exp_g, lg, over(top_g, GROUPS), ALU.subtract).then_inc(s_gdiff, 1)

                    def first_of(scores, best, n, cand, low, hot):
                        L(tt(cand, scores, over(best, n), ALU.is_equal))
                        L(nc.vector.scalar_tensor_tensor(out=cand, in0=cand, scalar=-64.0, in1=along(iota[:, 0:n], NT),
                                                         op0=ALU.mult, op1=ALU.add))
                        L(nc.vector.tensor_reduce(low, cand, AX.X, ALU.min))
                        L(tt(hot, cand, over(low, n), ALU.is_equal))

                    first_of(lg, top_g, GROUPS, cand_g, first_g, hot_g)
                    hot_wide = over(hot_g.rearrange("p t g -> p (t g)"), PER_GROUP)
                    by_group = lambda a: a.rearrange("p t (g e) -> p (t g) e", e=PER_GROUP)
                    L(nc.vector.tensor_copy(picked, le))
                    L(tt(by_group(masked), by_group(picked), hot_wide, ALU.mult))
                    L(ts(cand_g, hot_g, BIG, -BIG, ALU.mult, ALU.add))
                    L(tt(by_group(masked), by_group(masked), over(cand_g.rearrange("p t g -> p (t g)"), PER_GROUP), ALU.add))
                    L(nc.vector.tensor_reduce(top[0], masked, AX.X, ALU.max))
                    first_of(masked, top[0], EXPERTS, cand, first, hot[0])
                    L(nc.vector.scalar_tensor_tensor(out=masked, in0=hot[0], scalar=-4.0 * BIG, in1=masked,
                                                     op0=ALU.mult, op1=ALU.add))
                    L(nc.vector.tensor_reduce(top[1], masked, AX.X, ALU.max))
                    first_of(masked, top[1], EXPERTS, cand, first, hot[1])
                    tt(picked, hot[0], hot[1], ALU.add).then_inc(s_picked, 1)
                    tt(ratio, top[1], top[0], ALU.subtract).then_inc(s_ediff, 1)
                    dve.wait_ge(s_gexp, 1)
                    L(nc.vector.tensor_reduce(sum_g, exp_g, AX.X, ALU.add))
                    dve.wait_ge(s_eexp, 1)
                    L(nc.vector.scalar_tensor_tensor(out=sum_g, in0=ratio, scalar=1.0, in1=sum_g, op0=ALU.add, op1=ALU.mult))
                    L(nc.vector.reciprocal(weights[:, 0, :], sum_g))
                    L(tt(weights[:, 1, :], weights[:, 0, :], ratio, ALU.mult))
                    dve.wait_ge(s_rank, 1)
                    L(nc.vector.memset(base[:, 0, :], 0.0))
                    totals = banks[:, 1, :].rearrange("p (t e) -> p t e", e=EXPERTS)
                    for n in range(NT):
                        L(tt(base[:, n + 1, :], base[:, n, :], totals[:, n, :], ALU.add))
                    L(ts(blocks_of.rearrange("p e n -> p (e n)")[:, 0:NT], iota[:, 0:NT], float(P), None, ALU.mult))
                    L(nc.vector.tensor_copy(run[1][:, 0:NT], blocks_of.rearrange("p e n -> p (e n)")[:, 0:NT]))
                    L(tt(blocks_of, over(base[:, NT, :], NT), along(run[1][:, 0:NT], EXPERTS), ALU.is_gt))
                    L(nc.vector.tensor_reduce(counts, blocks_of, AX.X, ALU.add))
                    L(nc.vector.tensor_copy(run[0], counts))
                    side = 0
                    for step in (1, 2, 4, 8, 16):
                        L(nc.vector.tensor_copy(run[1 - side][:, 0:step], run[side][:, 0:step]))
                        L(tt(run[1 - side][:, step:], run[side][:, step:], run[side][:, 0:EXPERTS - step], ALU.add))
                        side = 1 - side
                    ends = run[side]
                    L(tt(reached, over(iota[:, 0:BLOCKS], EXPERTS), along(ends, BLOCKS), ALU.is_ge))
                    L(nc.vector.tensor_reduce(block_expert, reached, AX.X, ALU.add))
                    L(ts(block_expert, block_expert, float(EXPERTS - 1), None, ALU.min))
                    L(nc.vector.tensor_copy(block_expert_i, block_expert))
                    L(tt(run[1 - side], ends, counts, ALU.subtract))
                    L(ts(used, counts, 0.0, None, ALU.is_gt))
                    L(tt(reached, over(iota[:, 0:BLOCKS], EXPERTS), along(run[1 - side], BLOCKS), ALU.is_ge))
                    L(tt(reached, reached, along(used, BLOCKS), ALU.mult))
                    L(nc.vector.memset(load, 0.0))
                    L(nc.vector.tensor_reduce(load[:, 0:BLOCKS], reached, AX.X, ALU.add))
                    L(ts(exists, iota[:, 0:BLOCKS], ends[:, EXPERTS - 1:EXPERTS], None, ALU.is_lt))
                    L(tt(load[:, 0:BLOCKS], load[:, 0:BLOCKS], exists, ALU.mult))
                    L(nc.vector.tensor_reduce(y_count, exists.rearrange("p (i s) -> p s i", s=2), AX.X, ALU.add))
                    L(ts(y_count, y_count, 16.0, None, ALU.mult))
                    L(nc.vector.tensor_copy(y_count_i, y_count))
                    nc.vector.tensor_copy(load_i, load).then_inc(s_blocks, 1)
                    L(ts(run[1 - side], run[1 - side], float(P), None, ALU.mult))
                    slot = cand
                    L(tt(slot, banks[:, 0, :].rearrange("p (t e) -> p t e", e=EXPERTS), base[:, 0:NT, :], ALU.add))
                    L(tt(slot, slot, along(run[1 - side], NT), ALU.add))
                    for a in range(2):
                        L(tt(masked, slot, hot[a], ALU.mult))
                        L(nc.vector.tensor_reduce(slots_of[:, a, :], masked, AX.X, ALU.add))
                    L(nc.vector.tensor_copy(slots_i, slots_of))
                    hi_i, lo_i = picked.rearrange("p a b -> p (a b)")[:, 0:2 * NT].bitcast(I32), cand.rearrange(
                        "p a b -> p (a b)")[:, 0:2 * NT].bitcast(I32)
                    L(ts(hi_i, flat(slots_i), 7, None, ALU.logical_shift_right))
                    L(ts(lo_i, flat(slots_i), P - 1, None, ALU.bitwise_and))
                    L(nc.vector.tensor_copy(flat(slots_hi), hi_i))
                    L(nc.vector.tensor_copy(flat(slots_lo), lo_i))
                    @turns(dve, NT)
                    def _(i):
                        for a in range(2):
                            dve.wait_ge(s_list[a], i)
                            ts(in_block[a], iota, slots_lo[:, a, bass.ds(i, 1)], None, ALU.is_equal).then_inc(s_onehot[a], 1)
                            ts(of_block[a], iota[:, 0:BLOCKS], slots_hi[:, a, bass.ds(i, 1)], token[:, bass.ds(i, 1)],
                               ALU.is_equal, ALU.mult).then_inc(s_onehot[a], 1)
                    dve.wait_ge(s_list[1], NT + 1)
                    nc.vector.tensor_copy(slot_token, banks[:, 2, 0:BLOCKS]).then_inc(s_lists, 1)

                    def rest(out, whole, high):
                        return tt(flat(out), whole, flat(high).bitcast(F32), ALU.subtract)

                    def split(n, w, this):
                        dve.wait_ge(s_hi[n], this)
                        rest(w[1], stage[n], w[0]).then_inc(s_lo[n], 1)

                    def xT_out(turn):
                        dve.wait_ge(s_xT_hi, turn)
                        rest(xT[1], wide(2, D), xT[0]).then_inc(s_xT_lo, 1)

                    for n, w in enumerate((w_g, w_u, w_d)):
                        split(n, w, 1)
                    xT_out(1)
                    @blocks(dve)
                    def _(j, s, i, more, new):
                        dve.wait_ge(s_silu, j + 1)
                        dve.wait_ge(s_up, j + 1)
                        tt(act_u, act_g, banks[:, 1, :], ALU.mult).then_inc(s_act, 1)
                        dve.wait_ge(s_actT_hi, j + 1)
                        rest(actT[1], banks[:, 4, :], actT[0]).then_inc(s_actT_lo, 1)
                        new(lambda this: split(0, w_g, this))
                        more(lambda: xT_out(j + 2))
                        new(lambda this: split(1, w_u, this))
                        dve.wait_ge(s_down, j + 1)
                        dve.wait_ge(s_yout[s], 16 * i)
                        nc.vector.tensor_copy(ys[s][:, BANK:], banks[:, 6, :]).then_inc(s_yv, 1)
                        new(lambda this: split(2, w_d, this))
                    @turns(dve, NT // 2)
                    def _(i):
                        order = Order(dve, o_jdve, i, 6)
                        for s in range(2):
                            dve.wait_ge(s_yj[s], 32 * i + 32)
                            order.link(ts(yj[s][0], yj[s][0], weights[:, 0, bass.ds(2 * i + s, 1)], None, ALU.mult))
                            nc.vector.scalar_tensor_tensor(
                                out=yj[s][0], in0=yj[s][1], scalar=weights[:, 1, bass.ds(2 * i + s, 1)], in1=yj[s][0],
                                op0=ALU.mult, op1=ALU.add).then_inc(s_jsum[s], 1)
                            dve.wait_ge(s_jdev[s], i + 1)
                            order.link(nc.vector.reciprocal(jst[s][:, 0:1], jst[s][:, 1:2]))
                            order.link(nc.vector.scalar_tensor_tensor(out=yj[s][1], in0=yj[s][0], scalar=jst[s][:, 0:1],
                                                                      in1=rows[:, 3, :], op0=ALU.mult, op1=ALU.mult))
                            dve.wait_ge(s_xj[s], 16 * i + 16)
                            nc.vector.tensor_tensor(xj[s], xj[s], yj[s][1], ALU.add).then_inc(s_jout[s], 1)

                @block.tensor
                def _(pe):
                    pe.wait_ge(s_picked, 1)
                    flat_picked = picked.rearrange("p t e -> p (t e)")
                    nc.tensor.matmul(banks[:, 0, :], before, flat_picked, start=True, stop=True)
                    nc.tensor.matmul(banks[:, 1, :], ones, flat_picked, start=True, stop=True).then_inc(s_rank, 1)
                    pe.wait_ge(s_onehot[0], 2)
                    nc.tensor.matmul(banks[:, 2, 0:BLOCKS], zeros, of_block[0], start=True, stop=False)
                    @turns(pe, NT)
                    def _(i):
                        for a in range(2):
                            pe.wait_ge(s_onehot[a], 2 * i + 2)
                            nc.tensor.matmul(banks[:, 2, 0:BLOCKS], in_block[a], of_block[a], start=False, stop=False
                                             ).then_inc(s_list[a], 1)
                    nc.tensor.matmul(banks[:, 2, 0:BLOCKS], zeros, of_block[0], start=False, stop=True
                                     ).then_inc(s_list[1], 1)
                    pe.wait_ge(s_lists, 1)

                    def turn_tokens(s, turn, half):
                        if not half:
                            pe.wait_ge(s_xg[s], 16 * turn)
                        for k in range(4 * half, 4 * half + 4):
                            ins = nc.tensor.transpose(wide(2, D)[:, k * P:(k + 1) * P], xg[s][:, k * P:(k + 1) * P], ident)
                        if half:
                            ins.then_inc(s_xgT, 1)

                    def product(bank, xs, hi_ready, lo_ready, w, chunks, columns=slice(0, BANK)):
                        parts = ((0, 0), (0, 1), (1, 0))
                        for n, (a, b) in enumerate(parts):
                            if n == 0 and hi_ready:
                                hi_ready()
                            if n == 1 and lo_ready:
                                lo_ready()
                            for k in range(chunks):
                                ins = nc.tensor.matmul(banks[:, bank, :], xs[a][:, k, :], w[b][:, k, columns],
                                                       start=(n == 0 and k == 0), stop=(n == 2 and k == chunks - 1))
                        return ins

                    for half in range(2):
                        turn_tokens(0, 1, half)
                    @blocks(pe)
                    def _(j, s, i, more, new):
                        this = load_of(pe, j)

                        def hi(n, x_ready, turn):
                            pe.wait_ge(x_ready, turn)
                            pe.wait_ge(s_hi[n], this)

                        def lo(n, x_ready, turn):
                            pe.wait_ge(x_ready, turn)
                            pe.wait_ge(s_lo[n], this)

                        pe.wait_ge(s_act, j)
                        product(0, xT, lambda: hi(0, s_xT_hi, j + 1), lambda: lo(0, s_xT_lo, j + 1), w_g, KD
                                ).then_inc(s_gate, 1)
                        product(1, xT, lambda: hi(1, s_xT_hi, j + 1), lambda: lo(1, s_xT_lo, j + 1), w_u, KD
                                ).then_inc(s_up, 1)
                        more(lambda: turn_tokens(1 - s, i + 1 + s, 0))
                        pe.wait_ge(s_act, j + 1)
                        for k in range(KF):
                            ins = nc.tensor.transpose(banks[:, 4, k * P:(k + 1) * P], act_u[:, k * P:(k + 1) * P], ident)
                        ins.then_inc(s_actT, 1)
                        more(lambda: turn_tokens(1 - s, i + 1 + s, 1))
                        pe.wait_ge(s_ya, j)
                        pe.wait_ge(s_yv, j)
                        product(5, actT, lambda: hi(2, s_actT_hi, j + 1), lambda: lo(2, s_actT_lo, j + 1), w_d, KF)
                        product(6, actT, None, None, w_d, KF, slice(BANK, D)).then_inc(s_down, 1)

        project()
        attend()
        keys_values.close()
        merge()
        mixing.close()
        experts()


NAMES = ["x", "c", "w_ada", "b_ada", "g_pre_mix", "g_post_mix", "w_in", "w_dw", "b_dw", "conv_ln_g", "conv_ln_b",
         "w_conv_out", "q_norm_g", "k_norm_g", "w_attn_out", "w_out", "g_pre_ffn", "g_post_ffn", "w_group",
         "b_group", "w_router", "b_router", "w_e_gate", "w_e_up", "w_e_down"]


def rope_tables():
    half = HEAD // 2
    freq = np.float32(ROPE_THETA) ** (-np.arange(0, half, 2, dtype=np.float32) / np.float32(half))
    pos = np.arange(S)
    row = (pos // GRID_W).astype(np.float32)[:, None] * freq
    column = (pos % GRID_W).astype(np.float32)[:, None] * freq
    cos = np.concatenate([np.cos(row), np.cos(row), np.cos(column), np.cos(column)], 1)
    sin = np.concatenate([-np.sin(row), np.sin(row), -np.sin(column), np.sin(column)], 1)
    return np.ascontiguousarray(cos, np.float32), np.ascontiguousarray(sin, np.float32)


def kernel(**inputs):
    import concourse.bacc as _bacc
    from concourse.bass_utils import run_bass_kernel_spmd as _run

    nc = _bacc.Bacc("TRN2", target_bir_lowering=False, num_devices=1)
    arrays, tensors = {}, {}
    for name in NAMES:
        arrays[f"in_{name}"] = np.ascontiguousarray(inputs[name])
    arrays["in_rope_cos"], arrays["in_rope_sin"] = rope_tables()
    for name, a in arrays.items():
        tensors[name[3:]] = nc.dram_tensor(name, a.shape, mybir.dt.from_np(a.dtype), kind="ExternalInput").ap()
    out = nc.dram_tensor("out_0", (1, S, D), F32, kind="ExternalOutput").ap()
    encoder_block(nc, tensors, out)
    r = _run(nc, [arrays], core_ids=[0])
    return r.results[0]["out_0"]
```

```python
from contextlib import ExitStack

import concourse.bass as bass
import numpy as np
from concourse import mybir

F32 = mybir.dt.float32
F32R = mybir.dt.float32r
I32 = mybir.dt.int32
U32 = mybir.dt.uint32
ACT = mybir.ActivationFunctionType
ALU = mybir.AluOpType
AX = mybir.AxisListType

P = 128
BANK = 512
S, D = 2048, 1024
HEADS, KV_HEADS, HEAD = 8, 2, 64
GRID_W, ROPE_THETA = 64, 10000.0
CONV, TAPS = 512, 31
GROUPS, PER_GROUP, D_EXPERT = 4, 8, 512
EXPERTS = GROUPS * PER_GROUP
EPS = 1e-6

NT = S // P
KD = D // P
KC = CONV // P
KF = D_EXPERT // P
CH = 512
NC = S // CH
ATT = HEADS * HEAD
KV = KV_HEADS * HEAD
QK = ATT + KV
HALF = S // 2
PAD = TAPS // 2
BLOCKS = 2 * S // P + EXPERTS
LOGITS = GROUPS + EXPERTS
COL_GLU, COL_QKV, COL_GATE = 0, 2 * CONV, 2 * CONV + ATT + 2 * KV
BIG = 1.0e30


class Arena:

    def __init__(self, tensor, size):
        self.tensor, self.size, self.at = tensor, size, 0

    def take(self, *shape):
        n = int(np.prod(shape))
        view = self.tensor[:, self.at:self.at + n]
        self.at += (n + 7) // 8 * 8
        assert self.at <= self.size, (self.at, self.size)
        if len(shape) > 1:
            names = "abcd"[:len(shape)]
            view = view.rearrange(f"p ({' '.join(names)}) -> p {' '.join(names)}",
                                  **{n: s for n, s in zip(names[1:], shape[1:])})
        return view


class Order:

    def __init__(self, eng, sem, turn=0, per=0, base=0):
        self.eng, self.sem, self.n = eng, sem, turn * per + base
        self.k = 0

    def link(self, ins):
        ins.then_inc(self.sem, 1)
        self.k += 1
        self.eng.wait_ge(self.sem, self.n + self.k)


def turns(eng, n, last=False):
    def run(body):
        body(0)
        with eng.Fori(1, n - 1 if last else n) as i:
            body(i)
        if last:
            body(n - 1)
    return run


def is_last(i, n):
    return isinstance(i, int) and i == n - 1


def encoder_block(nc, t, out):
    ctx = ExitStack()
    with ctx:
        def dram(name, shape, dt=F32):
            return nc.dram_tensor(name, shape, dt, kind="Internal").ap()

        KEEP = 5984
        kept = Arena(ctx.enter_context(nc.sbuf_tensor("kept", [P, KEEP], F32)), KEEP)
        banks = ctx.enter_context(nc.psum_tensor("banks", [P, 8, BANK], F32))
        keep = kept.take

        def wide(b, n):
            return banks[:, b:b + (n + BANK - 1) // BANK, :].rearrange("p a b -> p (a b)")[:, 0:n]

        q_scr = dram("q_scr", [QK // P, P, S + P])
        v_scr = dram("v_scr", [P, NT, KV])
        row_scr = dram("row_scr", [1, 4 * D])
        gate_scr = dram("gate_scr", [2 * KD, P, S])
        o_scr = dram("o_scr", [NT, P, ATT])
        m_scr = dram("m_scr", [KD, P, S])
        x1_scr = dram("x1_scr", [S, D])
        h2_scr = dram("h2_scr", [S, D])
        y_scr = dram("y_scr", [BLOCKS * P, D])

        ident = keep(P)
        ones = keep(P)
        mean_w = keep(P)
        before = keep(P)
        eps_t = keep(1)
        c_col = keep(KD)
        c_silu = keep(KD)
        vec = keep(24)
        shift1 = keep(KD)
        scale1 = keep(KD)
        rbias = keep(LOGITS)
        logits = keep(NT, LOGITS)
        conv_g, conv_b, dw_b = keep(KC), keep(KC), keep(KC)
        dw_w = keep(KC, TAPS)
        rows = keep(4, D)

        mixing = ExitStack()
        conv_arena = Arena(mixing.enter_context(nc.sbuf_tensor("conv", [P, KC * S], F32)), KC * S)
        conv = conv_arena.take(KC, S)
        rows_flat = rows.rearrange("p a b -> p (a b)")

        x_v = t["x"].rearrange("a (t p) d -> (a t) p d", p=P)
        w_ada_v = t["w_ada"].rearrange("l (k p) n -> p (l k) n", p=P)
        w_in_v = t["w_in"].rearrange("l (k p) n -> p (l k) n", p=P)
        out_v = out.rearrange("a (t p) d -> (a t) p d", p=P)

        def col(ap1d, n):
            return ap1d.rearrange("(k p) -> p k", p=P)

        def end_phase(sems):
            nc.clear_and_free_semaphores(sems)
            nc.all_engine_barrier()

        def project():
            sems = []
            with ExitStack() as own:
                def sem(name):
                    sems.append(nc.alloc_semaphore(name))
                    return sems[-1]

                def overlay(name, *shapes):
                    with nc.sbuf_tensor(name, [P, sum(int(np.prod(s)) for s in shapes)], F32) as tensor:
                        region = Arena(tensor, sum(int(np.prod(s)) for s in shapes))
                        return [region.take(*s) for s in shapes]

                QKV_TILES = (ATT + 2 * KV) // P
                QK_TILES = QK // P
                REST = KD - KC
                FIRST_REST = QKV_TILES + 4 * KC

                ada_w = overlay("ada_w", (KD, D), (KD, D))
                hT = [own.enter_context(nc.sbuf_tensor(f"hT_{part}", [P, KD * S], F32R))[:, :].rearrange(
                    "p (k n) -> p k n", n=S) for part in ("hi", "lo")]
                wraw = own.enter_context(nc.sbuf_tensor("w_raw", [P, D], F32))[:, :]
                PIECE = BANK // 2
                PIECES = 4 * D // PIECE
                w_ada_row = overlay("ada_row_w", (KD, PIECE), (KD, PIECE))
                wcol = [[own.enter_context(nc.sbuf_tensor(f"w_{part}{n}", [P, D], F32R))[:, :].rearrange(
                    "p (k n) -> p k n", n=P) for part in ("hi", "lo")] for n in range(2)]
                spare = own.enter_context(nc.sbuf_tensor("spare", [P, 1056], F32))
                HALF_S = S // 2
                early = Arena(conv_arena.tensor, KC * S)
                xt = [early.take(D) for _ in range(2)]
                junk = early.take(D)
                hsum = [early.take(D) for _ in range(2)]
                first_ada = early.take(2 * D)[0:1, :]
                early.at = 0
                cosT, sinT = early.take(S), early.take(S)
                zg = [early.take(HALF_S) for _ in range(2)]
                square, dev = early.take(HALF_S), early.take(HALF_S)
                ada_rows = rows_flat[0:1, :]
                early = Arena(rows_flat, 4 * D)
                turned = [early.take(HALF_S) for _ in range(2)]
                swap = early.take(P)
                mean_head = early.take(P)
                early.at = 0
                glu = early.take(S + 2 * PAD)
                gate_out = [early.take(HALF_S), spare[:, 0:HALF_S]]
                early = Arena(spare, 1056)
                early.at = 1024
                st = [early.take(2) for _ in range(2)]
                gain = early.take(QK_TILES)
                gain_in = early.take(2)

                s_const = sem("s_const")
                s_vec = sem("s_vec")
                s_convvec = sem("s_convvec")
                s_csilu = sem("s_csilu")
                s_wada = [sem(f"s_wada{n}") for n in range(2)]
                s_ada_row, s_ada_rowout, s_ada_mm = sem("s_ada_row"), sem("s_ada_rowout"), sem("s_ada_mm")
                s_ada_col = sem("s_ada_col")
                s_x = [sem(f"s_x{s}") for s in range(2)]
                s_xroot = [sem(f"s_xroot{s}") for s in range(2)]
                s_xn = [sem(f"s_xn{s}") for s in range(2)]
                s_xT = [sem(f"s_xT{s}") for s in range(2)]
                s_h_a = [sem(f"s_h_a{s}") for s in range(2)]
                s_h_v = [sem(f"s_h_v{s}") for s in range(2)]
                s_h_hi = [sem(f"s_h_hi{s}") for s in range(2)]
                s_h_lo = [sem(f"s_h_lo{s}") for s in range(2)]
                o_norm_a, o_norm_v = sem("o_norm_a"), sem("o_norm_v")
                s_tab, s_gain = sem("s_tab"), sem("s_gain")
                s_raw = sem("s_raw")
                s_whi, s_wlo = sem("s_whi"), sem("s_wlo")
                s_z = [sem(f"s_z{e}") for e in range(2)]
                s_zg = [sem(f"s_zg{e}") for e in range(2)]
                s_zsq, s_zmean, s_zdev = sem("s_zsq"), sem("s_zmean"), sem("s_zdev")
                s_zswap, s_zturn = sem("s_zswap"), sem("s_zturn")
                s_rope = [sem(f"s_rope{e}") for e in range(2)]
                s_ropeout = [sem(f"s_ropeout{e}") for e in range(2)]
                o_rope = sem("o_rope")
                o_ada = sem("o_ada")
                s_vT, s_v, s_vout = sem("s_vT"), sem("s_v"), sem("s_vout")
                s_zT = [sem(f"s_zT{s}") for s in range(2)]
                s_sg, s_glu, s_pad = sem("s_sg"), sem("s_glu"), sem("s_pad")
                o_conv = sem("o_conv")
                s_gateev = [sem(f"s_gateev{s}") for s in range(2)]
                s_gateout = [sem(f"s_gateout{e}") for e in range(2)]
                s_brow = sem("s_brow")
                s_rowout = sem("s_rowout")
                s_warow = [sem(f"s_warow{s}") for s in range(2)]
                s_arow = [sem(f"s_arow{s}") for s in range(2)]
                s_rowadd = [sem(f"s_rowadd{s}") for s in range(2)]
                o_pool = sem("o_pool")
                block = own.enter_context(nc.Block())

                def flat(a):
                    return a.rearrange("p k n -> p (k n)")

                def by_chunk(a):
                    return a.rearrange("p (k n) -> p k n", n=P)

                @block.sync
                def _(sp):
                    with nc.allow_non_contiguous_dma(reason="short vectors as columns"):
                        sp.dma_start(c_col, col(t["c"][0], KD)).then_inc(s_vec, 16)
                        sp.dma_start(vec[:, 0:16], col(t["b_ada"][0, 0:2 * D], 16)).then_inc(s_vec, 16)
                        sp.dma_start(vec[:, 16:24], col(t["g_pre_mix"][0], KD)).then_inc(s_vec, 16)
                    for s in range(2):
                        sp.dma_start(xt[s], x_v[s]).then_inc(s_x[s], 16)
                    for n in range(2):
                        sp.dma_start(ada_w[n], w_ada_v[:, :, n * D:(n + 1) * D]).then_inc(s_wada[n], 16)
                    sp.dma_start(by_chunk(wraw), w_in_v[:, :, COL_QKV:COL_QKV + P]).then_inc(s_raw, 16)
                    with nc.allow_non_contiguous_dma(reason="short vectors as columns"):
                        for n in range(2):
                            for g, name in enumerate(("q_norm_g", "k_norm_g")):
                                sp.dma_start(gain_in[n * HEAD:(n + 1) * HEAD, g:g + 1], t[name].rearrange("l d -> d l")
                                             ).then_inc(s_tab, 16)
                        sp.dma_start(dw_b, col(t["b_dw"][0], KC)).then_inc(s_convvec, 16)
                        sp.dma_start(conv_g, col(t["conv_ln_g"][0], KC)).then_inc(s_convvec, 16)
                        sp.dma_start(conv_b, col(t["conv_ln_b"][0], KC)).then_inc(s_convvec, 16)
                        for k in range(KC):
                            sp.dma_start(dw_w[:, k, :], t["w_dw"][0, :, k * P:(k + 1) * P].rearrange("j p -> p j")
                                         ).then_inc(s_convvec, 16)
                    sp.dma_start(ada_rows, t["b_ada"][0:1, 2 * D:6 * D]).then_inc(s_brow, 16)

                    def fetch_piece(i, s):
                        sp.wait_ge(s_arow[s], i)
                        sp.dma_start(w_ada_row[s], w_ada_v[:, :, bass.ds((2 * i + s) * PIECE + 2 * D, PIECE)]
                                     ).then_inc(s_warow[s], 16)

                    @turns(sp, NT // 2 - 1)
                    def _(i):
                        for s in range(2):
                            fetch_piece(i, s)
                            sp.wait_ge(s_xT[s], i + 1)
                            sp.dma_start(xt[s], x_v[2 * i + 2 + s]).then_inc(s_x[s], 16)
                    for s in range(2):
                        fetch_piece(NT // 2 - 1, s)
                    for s in range(2):
                        sp.wait_ge(s_h_lo[s], NT // 2)
                    sp.dma_start(cosT, t["rope_cos"]).then_inc(s_tab, 16)
                    sp.dma_start(sinT, t["rope_sin"]).then_inc(s_tab, 16)
                    for s in range(2):
                        sp.wait_ge(s_rowadd[s], PIECES // 2)
                    sp.dma_start(row_scr[:, :], ada_rows).then_inc(s_rowout, 16)
                    sp.wait_ge(s_rowout, 16)
                    sp.dma_start(swap, t["rope_swap"]).then_inc(s_tab, 16)
                    sp.dma_start(mean_head, t["head_mean"]).then_inc(s_tab, 16)

                    def fetch(n, column):
                        sp.wait_ge(s_whi, n)
                        sp.wait_ge(s_wlo, n)
                        sp.dma_start(by_chunk(wraw), w_in_v[:, :, bass.ds(column, P)]).then_inc(s_raw, 16)

                    @turns(sp, QK_TILES)
                    def _(c):
                        fetch(c + 1, c * P + COL_QKV + P)
                        for e in range(2):
                            sp.wait_ge(s_rope[e], c + 1)
                            sp.dma_start(q_scr[c][:, e * HALF_S:(e + 1) * HALF_S], turned[e]).then_inc(s_ropeout[e], 16)
                        sp.dma_start(q_scr[c][:, S:], turned[1][:, 0:P]).then_inc(s_ropeout[1], 16)
                    fetch(QKV_TILES, 0)
                    for e in range(2):
                        sp.wait_ge(s_v, e + 1)
                        sp.dma_start(v_scr[:, e * (NT // 2):(e + 1) * (NT // 2), :].rearrange("p t n -> p (t n)"), turned[e]
                                     ).then_inc(s_vout, 16)

                    def send(m, s):
                        for e in range(2):
                            sp.wait_ge(s_gateev[e], 2 * m + s + 1)
                            sp.dma_start(gate_scr[2 * m + s][:, e * HALF_S:(e + 1) * HALF_S], gate_out[e]
                                         ).then_inc(s_gateout[e], 16)

                    @turns(sp, KC, last=True)
                    def _(m):
                        fetch(4 * m + QKV_TILES + 1, m * P + CONV)
                        for s in range(2):
                            fetch(4 * m + QKV_TILES + 2 + s, m * 2 * P + s * P + COL_GATE)
                        if is_last(m, KC):
                            fetch(FIRST_REST, KC * 2 * P + COL_GATE)
                        else:
                            fetch(4 * m + QKV_TILES + 4, m * P + P)
                        send(m, 0)
                        send(m, 1)
                    @turns(sp, REST, last=True)
                    def _(j):
                        fetch(2 * j + FIRST_REST + 1, j * 2 * P + KC * 2 * P + P + COL_GATE)
                        if not is_last(j, REST):
                            fetch(2 * j + FIRST_REST + 2, j * 2 * P + KC * 2 * P + 2 * P + COL_GATE)
                        send(j + KC, 0)
                        send(j + KC, 1)

                    sp.wait_ge(s_ropeout[0], 16 * QK_TILES)
                    sp.wait_ge(s_ropeout[1], 32 * QK_TILES)
                    sp.wait_ge(s_vout, 32)
                    for e in range(2):
                        sp.wait_ge(s_gateout[e], 16 * 2 * KD)

                @block.gpsimd
                def _(pool):
                    order = Order(pool, o_pool)
                    order.link(nc.gpsimd.memset(ident, 0.0))
                    nc.gpsimd.affine_select(out=ident, in_=ident, compare_op=ALU.not_equal, fill=1.0, base=0,
                                            pattern=[[-1, P]], channel_multiplier=1).then_inc(s_const, 1)
                    nc.gpsimd.memset(ones, 1.0).then_inc(s_const, 1)
                    nc.gpsimd.memset(mean_w, 1.0 / CONV).then_inc(s_const, 1)
                    nc.gpsimd.memset(eps_t, EPS).then_inc(s_const, 1)
                    order.link(nc.gpsimd.memset(before, 1.0))
                    nc.gpsimd.affine_select(out=before, in_=before, compare_op=ALU.is_gt, fill=0.0, base=0,
                                            pattern=[[1, P]], channel_multiplier=-1).then_inc(s_const, 1)

                    def split(n, s):
                        pool.wait_ge(s_whi, n + 1)
                        nc.gpsimd.tensor_tensor(flat(wcol[s][1]), wraw, flat(wcol[s][0]).bitcast(F32), ALU.subtract
                                                ).then_inc(s_wlo, 1)

                    @turns(pool, QKV_TILES)
                    def _(c):
                        split(c, 0)
                    @turns(pool, 2 * KC + REST)
                    def _(m):
                        for s in range(2):
                            split(2 * m + s + QKV_TILES, s)

                @block.scalar
                def _(act):
                    act.wait_ge(s_vec, 48)
                    nc.scalar.activation(c_silu, c_col, ACT.Silu).then_inc(s_csilu, 1)
                    act.wait_ge(s_const, 5)

                    def root(s, turn, i):
                        order = Order(act, o_norm_a, i, 2, s)
                        act.wait_ge(s_x[s], 16 * turn)
                        order.link(nc.scalar.activation(junk, xt[s], ACT.Square, accum_out=st[s][:, 0:1]))
                        nc.scalar.activation(st[s][:, 1:2], st[s][:, 0:1], ACT.Sqrt, bias=eps_t, scale=1.0 / D
                                             ).then_inc(s_xroot[s], 1)

                    root(0, 1, 0)
                    act.wait_ge(s_ada_col, 1)
                    @turns(act, NT // 2, last=True)
                    def _(i):
                        for s in range(2):
                            act.wait_ge(s_xT[s], i + 1)
                            act.wait_ge(s_h_lo[s], i)
                            for k in range(KD // 2):
                                ins = nc.scalar.activation(hsum[s][:, k * P:(k + 1) * P], wide(2 * s, D)[:, k * P:(k + 1) * P],
                                                           ACT.Identity, bias=shift1[:, k:k + 1], scale=scale1[:, k:k + 1])
                            ins.then_inc(s_h_a[s], 1)
                            act.wait_ge(s_h_a[s], i + 1)
                            act.wait_ge(s_h_v[s], i + 1)
                            if s == 0:
                                root(1, i + 1, i)
                            elif not is_last(i, NT // 2):
                                root(0, i + 2, i + 1)
                            nc.scalar.activation(hT[0][:, :, bass.ds((2 * i + s) * P, P)], by_chunk(hsum[s]), ACT.Copy
                                                 ).then_inc(s_h_hi[s], 1)

                    def split(n, s):
                        act.wait_ge(s_raw, 16 * n + 16)
                        nc.scalar.activation(flat(wcol[s][0]), wraw, ACT.Copy).then_inc(s_whi, 1)

                    def deviation(unit, ready, last_used):
                        act.wait_ge(s_zmean, unit + 1)
                        act.wait_ge(last_used, ready)
                        nc.scalar.activation(dev, wide(4, HALF_S), ACT.Sqrt, bias=eps_t).then_inc(s_zdev, 1)

                    for s in range(2):
                        act.wait_ge(s_arow[s], PIECES // 2)
                    split(0, 0)
                    act.wait_ge(s_gain, 2)
                    @turns(act, QK_TILES)
                    def _(c):
                        for e in range(2):
                            act.wait_ge(s_z[e], c + 1)
                            act.wait_ge(s_rope[e], c)
                            act.wait_ge(s_zmean, 2 * c + e)
                            nc.scalar.activation(square, wide(2 * e, HALF_S), ACT.Square).then_inc(s_zsq, 1)
                            nc.scalar.activation(zg[e], wide(2 * e, HALF_S), ACT.Identity, scale=gain[:, bass.ds(c, 1)]
                                                 ).then_inc(s_zg[e], 1)
                            if e == 0:
                                if not isinstance(c, int):
                                    deviation(2 * c - 1, c, s_rope[0])
                            else:
                                split(c + 1, 0)
                                deviation(2 * c, c, s_rope[1])
                    for e in range(2):
                        act.wait_ge(s_z[e], QKV_TILES)
                        act.wait_ge(s_rope[e], QK_TILES)
                        nc.scalar.activation(zg[e], wide(2 * e, HALF_S), ACT.Copy).then_inc(s_zg[e], 1)
                        if e == 0:
                            deviation(2 * QK_TILES - 1, QK_TILES, s_rope[0])
                    split(QKV_TILES, 0)

                    def gate(m, s, turn):
                        act.wait_ge(s_zT[s], turn)
                        for e in range(2):
                            act.wait_ge(s_gateout[e], 32 * m + 16 * s)
                            nc.scalar.activation(gate_out[e], wide(4 * s + 2 * e, HALF_S), ACT.Sigmoid).then_inc(s_gateev[e], 1)

                    act.wait_ge(s_pad, 2)
                    @turns(act, KC)
                    def _(m):
                        n = 4 * m + QKV_TILES
                        act.wait_ge(s_zT[1], 2 * m)
                        split(n + 1, 1)
                        act.wait_ge(s_zT[0], 2 * m + 1)
                        split(n + 2, 0)
                        act.wait_ge(s_zT[1], 2 * m + 1)
                        act.wait_ge(o_conv, TAPS * m)
                        nc.scalar.activation(glu[:, PAD:PAD + S], wide(4, S), ACT.Sigmoid).then_inc(s_sg, 1)
                        split(n + 3, 1)
                        gate(m, 0, 2 * m + 2)
                        split(n + 4, 0)
                        gate(m, 1, 2 * m + 2)
                    @turns(act, REST, last=True)
                    def _(j):
                        n = 2 * j + FIRST_REST
                        act.wait_ge(s_zT[1], j + 2 * KC)
                        split(n + 1, 1)
                        gate(j + KC, 0, j + 2 * KC + 1)
                        if not is_last(j, REST):
                            split(n + 2, 0)
                        gate(j + KC, 1, j + 2 * KC + 1)

                @block.vector
                def _(dve):
                    order = Order(dve, o_ada)

                    def normed(s, turn, i):
                        order = Order(dve, o_norm_v, i, 2, s)
                        dve.wait_ge(s_xroot[s], turn)
                        order.link(nc.vector.reciprocal(st[s][:, 0:1], st[s][:, 1:2]))
                        nc.vector.tensor_scalar(xt[s], xt[s], st[s][:, 0:1], None, ALU.mult).then_inc(s_xn[s], 1)

                    dve.wait_ge(s_brow, 16)
                    normed(0, 1, 0)
                    for n in range(4):
                        dve.wait_ge(s_ada_row, n + 1)
                        nc.vector.tensor_copy(first_ada[:, n * BANK:(n + 1) * BANK], banks[0:1, 4 + n, :]
                                              ).then_inc(s_ada_rowout, 1)
                    dve.wait_ge(s_ada_mm, 1)
                    dve.wait_ge(s_vec, 48)
                    order.link(nc.vector.tensor_tensor(shift1, banks[:, 4, 0:KD], vec[:, 0:KD], ALU.add))
                    order.link(nc.vector.tensor_tensor(scale1, banks[:, 4, KD:2 * KD], vec[:, KD:2 * KD], ALU.add))
                    nc.vector.scalar_tensor_tensor(out=scale1, in0=scale1, scalar=1.0, in1=vec[:, 16:24],
                                                   op0=ALU.add, op1=ALU.mult).then_inc(s_ada_col, 1)
                    dve.wait_ge(s_ada_col, 1)
                    dve.wait_ge(s_tab, 64)
                    nc.vector.tensor_scalar(gain[:, 0:QK_TILES - 1], gain_in[:, 0:1].to_broadcast([P, QK_TILES - 1]),
                                            HEAD ** -0.5, None, ALU.mult).then_inc(s_gain, 1)
                    nc.vector.tensor_copy(gain[:, QK_TILES - 1:QK_TILES], gain_in[:, 1:2]).then_inc(s_gain, 1)
                    @turns(dve, NT // 2, last=True)
                    def _(i):
                        for s in range(2):
                            dve.wait_ge(s_xT[s], i + 1)
                            dve.wait_ge(s_h_lo[s], i)
                            for k in range(KD // 2, KD):
                                ins = nc.vector.tensor_scalar(hsum[s][:, k * P:(k + 1) * P], wide(2 * s, D)[:, k * P:(k + 1) * P],
                                                              scale1[:, k:k + 1], shift1[:, k:k + 1], ALU.mult, ALU.add)
                            ins.then_inc(s_h_v[s], 1)
                            if s == 0:
                                normed(1, i + 1, i)
                            elif not is_last(i, NT // 2):
                                normed(0, i + 2, i + 1)
                            dve.wait_ge(s_h_hi[s], i + 1)
                            at = bass.ds((2 * i + s) * P, P)
                            nc.vector.tensor_tensor(hT[1][:, :, at], by_chunk(hsum[s]), hT[0][:, :, at].bitcast(F32),
                                                    ALU.subtract).then_inc(s_h_lo[s], 1)
                            dve.wait_ge(s_arow[s], i + 1)
                            piece = ada_rows[:, bass.ds((2 * i + s) * PIECE, PIECE)]
                            nc.vector.tensor_tensor(piece, banks[0:1, 5 + s, 0:PIECE], piece, ALU.add).then_inc(s_rowadd[s], 1)

                    dve.wait_ge(s_tab, 128)
                    @turns(dve, QK_TILES)
                    def _(c):
                        order = Order(dve, o_rope, c, 6)
                        for e in range(2):
                            tokens = slice(e * HALF_S, (e + 1) * HALF_S)
                            dve.wait_ge(s_zg[e], c + 1)
                            dve.wait_ge(s_ropeout[e], (16 + 16 * e) * c)
                            order.link(nc.vector.tensor_tensor(turned[e], zg[e], cosT[:, tokens], ALU.mult))
                            dve.wait_ge(s_zswap, 2 * c + e + 1)
                            nc.vector.tensor_tensor(zg[e], wide(6, HALF_S), sinT[:, tokens], ALU.mult).then_inc(s_zturn, 1)
                            dve.wait_ge(s_zturn, 2 * c + e + 1)
                            order.link(nc.vector.tensor_tensor(turned[e], turned[e], zg[e], ALU.add))
                            dve.wait_ge(s_zdev, 2 * c + e + 1)
                            order.link(nc.vector.reciprocal(dev, dev))
                            nc.vector.tensor_tensor(turned[e], turned[e], dev, ALU.mult).then_inc(s_rope[e], 1)
                    for e in range(2):
                        dve.wait_ge(s_vT, e + 1)
                        dve.wait_ge(s_ropeout[e], (16 + 16 * e) * QK_TILES)
                        nc.vector.tensor_copy(turned[e], wide(6, HALF_S)).then_inc(s_v, 1)
                    dve.wait_ge(s_vout, 32)
                    nc.vector.memset(glu[:, 0:PAD], 0.0).then_inc(s_pad, 1)
                    nc.vector.memset(glu[:, PAD + S:], 0.0).then_inc(s_pad, 1)
                    dve.wait_ge(s_pad, 2)
                    dve.wait_ge(s_convvec, 16 * (3 + KC))
                    @turns(dve, KC)
                    def _(m):
                        order = Order(dve, o_conv, m, TAPS)
                        dve.wait_ge(s_sg, m + 1)
                        dve.wait_ge(s_zT[0], 2 * m + 1)
                        middle = glu[:, PAD:PAD + S]
                        nc.vector.tensor_tensor(middle, wide(0, S), middle, ALU.mult).then_inc(s_glu, 1)
                        dve.wait_ge(s_glu, m + 1)
                        order.link(nc.vector.tensor_scalar(conv[:, m, :], glu[:, 0:S], dw_w[:, m, 0:1], dw_b[:, bass.ds(m, 1)],
                                                           ALU.mult, ALU.add))
                        for j in range(1, TAPS):
                            order.link(nc.vector.scalar_tensor_tensor(
                                out=conv[:, m, :], in0=glu[:, j:j + S], scalar=dw_w[:, m, j:j + 1], in1=conv[:, m, :],
                                op0=ALU.mult, op1=ALU.add))


                @block.tensor
                def _(pe):
                    pe.wait_ge(s_csilu, 1)
                    for n in range(4):
                        pe.wait_ge(s_wada[n // 2], 16)
                        for k in range(KD):
                            ins = nc.tensor.matmul(banks[0:1, 4 + n, :], c_silu[:, k:k + 1],
                                                   ada_w[n // 2][:, k, (n % 2) * BANK:(n % 2 + 1) * BANK],
                                                   start=(k == 0), stop=(k == KD - 1))
                        ins.then_inc(s_ada_row, 1)
                    pe.wait_ge(s_const, 5)
                    pe.wait_ge(s_ada_rowout, 4)
                    for n in range(16):
                        ins = nc.tensor.matmul(banks[:, 4, n:n + 1], first_ada[:, n * P:(n + 1) * P], ones[0:1, 0:1],
                                               start=True, stop=True)
                    ins.then_inc(s_ada_mm, 1)
                    pe.wait_ge(s_const, 5)
                    @turns(pe, NT // 2)
                    def _(i):
                        for s in range(2):
                            pe.wait_ge(s_xn[s], i + 1)
                            pe.wait_ge(s_h_a[s], i)
                            pe.wait_ge(s_h_v[s], i)
                            for k in range(KD):
                                ins = nc.tensor.transpose(wide(2 * s, D)[:, k * P:(k + 1) * P], xt[s][:, k * P:(k + 1) * P],
                                                          ident)
                            ins.then_inc(s_xT[s], 1)
                            pe.wait_ge(s_warow[s], 16 * i + 16)
                            pe.wait_ge(s_rowadd[s], i)
                            for k in range(KD):
                                ins = nc.tensor.matmul(banks[0:1, 5 + s, 0:PIECE], c_silu[:, k:k + 1], w_ada_row[s][:, k, :],
                                                       start=(k == 0), stop=(k == KD - 1))
                            ins.then_inc(s_arow[s], 1)
                    for s in range(2):
                        pe.wait_ge(s_h_lo[s], NT // 2)
                        pe.wait_ge(s_rowadd[s], PIECES // 2)

                    def product(s, bank, first_token, n_banks, tile):
                        for part, (a, b) in enumerate(((0, 0), (0, 1), (1, 0))):
                            if part == 0:
                                pe.wait_ge(s_whi, tile + 1)
                            if part == 2:
                                pe.wait_ge(s_wlo, tile + 1)
                            for k in range(KD):
                                for n in range(n_banks):
                                    at = first_token + n * BANK
                                    ins = nc.tensor.matmul(banks[:, bank + n, :], wcol[s][a][:, k, :], hT[b][:, k, at:at + BANK],
                                                           start=(part == 0 and k == 0), stop=(part == 2 and k == KD - 1))
                        return ins

                    def mean_and_swap(unit, e, turn):
                        pe.wait_ge(s_zsq, unit + 1)
                        at_most(unit, s_zdev)
                        for n in range(2):
                            ins = nc.tensor.matmul(banks[:, 4 + n, :], mean_head, square[:, n * BANK:(n + 1) * BANK],
                                                   start=True, stop=True)
                        ins.then_inc(s_zmean, 1)
                        pe.wait_ge(s_zg[e], turn)
                        at_most(unit, s_zturn)
                        for n in range(2):
                            ins = nc.tensor.matmul(banks[:, 6 + n, :], swap, zg[e][:, n * BANK:(n + 1) * BANK],
                                                   start=True, stop=True)
                        ins.then_inc(s_zswap, 1)

                    def at_most(unit, used):
                        if not isinstance(unit, int) or unit:
                            pe.wait_ge(used, unit)

                    def turn_values(e):
                        pe.wait_ge(s_zg[e], QKV_TILES)
                        if e:
                            pe.wait_ge(s_v, 1)
                        else:
                            pe.wait_ge(s_zturn, 2 * QK_TILES)
                        for k in range(NT // 2):
                            ins = nc.tensor.transpose(wide(6, HALF_S)[:, k * P:(k + 1) * P], zg[e][:, k * P:(k + 1) * P], ident)
                        ins.then_inc(s_vT, 1)

                    pe.wait_ge(s_tab, 128)
                    @turns(pe, QK_TILES)
                    def _(c):
                        for e in range(2):
                            pe.wait_ge(s_zg[e], c)
                            product(0, 2 * e, e * HALF_S, 2, c).then_inc(s_z[e], 1)
                            if e:
                                mean_and_swap(2 * c, 0, c + 1)
                            elif not isinstance(c, int):
                                mean_and_swap(2 * c - 1, 1, c)
                    for e in range(2):
                        pe.wait_ge(s_zg[e], QK_TILES)
                        product(0, 2 * e, e * HALF_S, 2, QK_TILES).then_inc(s_z[e], 1)
                        if e == 0:
                            mean_and_swap(2 * QK_TILES - 1, 1, QK_TILES)
                        else:
                            turn_values(0)
                    turn_values(1)
                    pe.wait_ge(s_v, 2)
                    pe.wait_ge(s_zdev, 2 * QK_TILES)

                    @turns(pe, KC)
                    def _(m):
                        n = 4 * m + QKV_TILES
                        if not isinstance(m, int):
                            pe.wait_ge(s_gateev[1], 2 * m - 1)
                        product(0, 0, 0, 4, n).then_inc(s_zT[0], 1)
                        pe.wait_ge(s_gateev[1], 2 * m)
                        product(1, 4, 0, 4, n + 1).then_inc(s_zT[1], 1)
                        pe.wait_ge(s_glu, m + 1)
                        product(0, 0, 0, 4, n + 2).then_inc(s_zT[0], 1)
                        pe.wait_ge(s_sg, m + 1)
                        product(1, 4, 0, 4, n + 3).then_inc(s_zT[1], 1)
                    @turns(pe, REST)
                    def _(j):
                        for s in range(2):
                            pe.wait_ge(s_gateev[1], 2 * (j + KC) + s - 1)
                            product(s, 4 * s, 0, 4, 2 * j + FIRST_REST + s).then_inc(s_zT[s], 1)
                    pe.wait_ge(s_gateev[1], 2 * KD)

            end_phase(sems)

        def attend():
            sems = []
            with ExitStack() as own:
                def sem(name):
                    sems.append(nc.alloc_semaphore(name))
                    return sems[-1]

                UNITS = 2 * HEADS
                kT = own.enter_context(nc.sbuf_tensor("kT", [P, KV_HEADS * S], F32R))[:, :].rearrange(
                    "p (g n) -> p g n", n=S)
                qb = [own.enter_context(nc.sbuf_tensor(f"q_pair{p}", [P, 4 * P], F32R))[:, :].rearrange(
                    "p (h a n) -> p h a n", h=2, a=2) for p in range(4)]
                OWN = 11472
                take = Arena(own.enter_context(nc.sbuf_tensor("attend_buffers", [P, OWN], F32)), OWN).take
                v_sb = take(NT, KV)
                q_in = take(HEADS, P)
                k_in = w_co.rearrange("p (g n) -> p g n", n=S)
                prob = [take(HALF) for _ in range(2)]
                probT = [take(BANK) for _ in range(2)]
                neg_max, total = take(UNITS), take(UNITS)
                neg_top, fade, mass, norm, share = take(4), take(8), take(8), take(4), take(8)
                o_parts = take(8, HEAD)
                o_out = take(2, 4, HEAD)
                blank = take(D)
                gains = take(3, D)

                def first(i):
                    return isinstance(i, int)

                s_rows, o_rows = sem("s_rows"), sem("o_rows")
                s_k, s_kv, s_qin = sem("s_k"), sem("s_kv"), sem("s_qin")
                s_k_hi, s_k_lo = sem("s_k_hi"), sem("s_k_lo")
                s_q_hi = [sem(f"s_q_hi{p}") for p in range(4)]
                s_q_lo = [sem(f"s_q_lo{p}") for p in range(4)]
                s_qk = [sem(f"s_qk{s}") for s in range(2)]
                s_max = [sem(f"s_max{s}") for s in range(2)]
                s_exp = [sem(f"s_exp{s}") for s in range(2)]
                s_pT = [sem(f"s_pT{g}") for g in range(2)]
                s_pTe = [sem(f"s_pTe{g}") for g in range(2)]
                s_pv = [sem(f"s_pv{g}") for g in range(2)]
                s_fade = [sem(f"s_fade{g}") for g in range(2)]
                s_faded = [sem(f"s_faded{g}") for g in range(2)]
                s_oread = [sem(f"s_oread{g}") for g in range(2)]
                s_osum = [sem(f"s_osum{g}") for g in range(2)]
                s_oout = [sem(f"s_oout{g}") for g in range(2)]
                o_join = [sem(f"o_join{g}") for g in range(2)]
                s_wmerge = sem("s_wmerge")
                s_blank, s_yblank = sem("s_blank"), sem("s_yblank")
                block = own.enter_context(nc.Block())

                @block.sync
                def _(sp):
                    def fetch(i):
                        for half in range(2):
                            sp.dma_start(q_in[half * HEAD:(half + 1) * HEAD],
                                         q_scr[0:ATT // P, :, bass.ds(i * P, P)].rearrange("c (h d) n -> d (c h) n", d=HEAD)
                                         ).then_inc(s_qin, 16)

                    for half in range(2):
                        sp.dma_start(k_in[half * HEAD:(half + 1) * HEAD],
                                     q_scr[ATT // P, :, 0:S].rearrange("(g d) n -> d g n", d=HEAD)).then_inc(s_k, 16)
                    fetch(0)
                    sp.dma_start(v_sb, v_scr[:, :, :]).then_inc(s_kv, 16)
                    def fetch_merge():
                        sp.dma_start(rows_flat, row_scr[:, :].to_broadcast([P, 4 * D])).then_inc(s_rows, 16)
                        for n, name in enumerate(("g_post_mix", "g_pre_ffn", "g_post_ffn")):
                            sp.dma_start(gains[:, n, :], t[name][0:1, :].to_broadcast([P, D])).then_inc(s_rows, 16)
                        sp.wait_ge(s_k_lo, KV_HEADS)
                        for w, name in ((w_co, "w_conv_out"), (w_ao, "w_attn_out")):
                            sp.dma_start(w.rearrange("p (k n) -> p k n", n=D), t[name].rearrange("l (k p) n -> p (l k) n", p=P)).then_inc(s_wmerge, 16)

                    BLANK = (BLOCKS - 2 * S // P) // NT
                    sp.wait_ge(s_blank, 1)

                    def send(i, g):
                        sp.wait_ge(s_osum[g], i + 1)
                        sp.dma_start(o_scr[i][:, g * 4 * HEAD:(g + 1) * 4 * HEAD],
                                     o_out[:, g].rearrange("p a b -> p (a b)")).then_inc(s_oout[g], 16)

                    @turns(sp, NT)
                    def _(i):
                        for p in range(4):
                            sp.wait_ge(s_q_lo[p], i + 1)
                        fetch(i + 1)
                        if first(i):
                            fetch_merge()
                        sp.dma_start(y_scr[bass.ds(i * BLANK * P + 2 * S, BLANK * P), :].rearrange("(b p) n -> p b n", p=P),
                                     blank.rearrange("p (o n) -> p o n", o=1).to_broadcast([P, BLANK, D])
                                     ).then_inc(s_yblank, 16)
                        if not first(i):
                            send(i - 1, 1)
                        send(i, 0)
                    send(NT - 1, 1)
                    sp.wait_ge(s_qin, 32 * NT + 32)
                    for g in range(2):
                        sp.wait_ge(s_oout[g], 16 * NT)
                    sp.wait_ge(s_wmerge, 32)
                    sp.wait_ge(s_yblank, 16 * NT)

                @block.gpsimd
                def _(pool):
                    order = Order(pool, o_rows)
                    pool.wait_ge(s_rows, 64)
                    order.link(nc.gpsimd.tensor_tensor(rows[:, 0, :], rows[:, 0, :], gains[:, 0, :], ALU.mult))
                    order.link(nc.gpsimd.tensor_scalar(rows[:, 2, :], rows[:, 2, :], 1.0, None, ALU.add))
                    order.link(nc.gpsimd.tensor_tensor(rows[:, 2, :], rows[:, 2, :], gains[:, 1, :], ALU.mult))
                    order.link(nc.gpsimd.tensor_tensor(rows[:, 3, :], rows[:, 3, :], gains[:, 2, :], ALU.mult))

                @block.scalar
                def _(act):
                    def fade_group(i, g):
                        act.wait_ge(s_fade[g], i + 1)
                        nc.scalar.activation(fade, fade, ACT.Exp).then_inc(s_faded[g], 1)

                    def exp(s, turn, u):
                        act.wait_ge(s_max[s], turn)
                        nc.scalar.activation(prob[s], wide(2 * s, HALF), ACT.Exp, bias=neg_max[:, u:u + 1],
                                             accum_out=total[:, u:u + 1]).then_inc(s_exp[s], 1)

                    def q_high(i, p):
                        act.wait_ge(s_qin, 32 * i + 32)
                        if not first(i) or i:
                            act.wait_ge(s_qk[1], 8 * i + 2 * p - 6)
                        nc.scalar.activation(qb[p][:, :, 0, :], q_in[:, 2 * p:2 * p + 2, :], ACT.Copy).then_inc(s_q_hi[p], 1)

                    act.wait_ge(s_k, 32)
                    for g in range(KV_HEADS):
                        nc.scalar.activation(kT[:, g, :], k_in[:, g, :], ACT.Copy).then_inc(s_k_hi, 1)
                    for p in range(4):
                        q_high(0, p)
                    exp(0, 1, 0)
                    @turns(act, NT)
                    def _(i):
                        for u in range(UNITS):
                            act.wait_ge(s_pT[0], UNITS * i + u + 1)
                            nc.scalar.activation(probT[0], banks[:, 4, :], ACT.Copy).then_inc(s_pTe[0], 1)
                            if u + 1 < UNITS:
                                exp((u + 1) % 2, 8 * i + (u + 1) // 2 + 1, u + 1)
                            else:
                                exp(0, 8 * i + 9, 0)
                            if u % 4 == 3:
                                q_high(i + 1, u // 4)
                            if u == 9:
                                fade_group(i, 0)
                            if u == 1 and not first(i):
                                fade_group(i - 1, 1)
                    fade_group(NT - 1, 1)

                @block.vector
                def _(dve):
                    JOIN = range(5)
                    nc.vector.memset(blank, 0.0).then_inc(s_blank, 1)

                    def unit_max(s, turn, u):
                        dve.wait_ge(s_qk[s], turn)
                        nc.vector.tensor_reduce(neg_max[:, u:u + 1], wide(2 * s, HALF), AX.X, ALU.max, negate=True
                                                ).then_inc(s_max[s], 1)

                    halves = lambda a: a.rearrange("p (h o) -> p h o", o=2)
                    one = lambda a: a.rearrange("p (h o) -> p h o", o=1)

                    def join_halves(step, i, g):
                        order = Order(dve, o_join[g], i, 5, (0, 1, 3, 5, 5)[step])
                        nm = halves(neg_max[:, 8 * g:8 * g + 8])
                        if step == 0:
                            order.link(nc.vector.tensor_reduce(neg_top, nm, AX.X, ALU.min))
                            nc.vector.tensor_tensor(halves(fade), one(neg_top).to_broadcast([P, 4, 2]), nm, ALU.subtract
                                                    ).then_inc(s_fade[g], 1)
                        elif step == 1:
                            dve.wait_ge(s_faded[g], i + 1)
                            order.link(nc.vector.tensor_tensor(mass, fade, total[:, 8 * g:8 * g + 8], ALU.mult))
                            order.link(nc.vector.tensor_reduce(norm, halves(mass), AX.X, ALU.add))
                        elif step == 2:
                            order.link(nc.vector.reciprocal(norm, norm))
                            order.link(nc.vector.tensor_tensor(halves(share), halves(fade),
                                                               one(norm).to_broadcast([P, 4, 2]), ALU.mult))
                        elif step == 3:
                            dve.wait_ge(s_pv[1], UNITS * i + 8 * g + 8)
                            nc.vector.tensor_tensor(o_parts, banks[:, 6 + g, :].rearrange("p (u d) -> p u d", d=HEAD),
                                                    one(share).to_broadcast([P, 8, HEAD]), ALU.mult).then_inc(s_oread[g], 1)
                        else:
                            dve.wait_ge(s_oread[g], i + 1)
                            dve.wait_ge(s_oout[g], 16 * i)
                            parts = o_parts.rearrange("p (h o) d -> p h o d", o=2)
                            nc.vector.tensor_tensor(o_out[:, g], parts[:, :, 0, :], parts[:, :, 1, :], ALU.add
                                                    ).then_inc(s_osum[g], 1)

                    def q_low(i, p):
                        dve.wait_ge(s_q_hi[p], i + 1)
                        nc.vector.tensor_tensor(qb[p][:, :, 1, :], q_in[:, 2 * p:2 * p + 2, :],
                                                qb[p][:, :, 0, :].bitcast(F32), ALU.subtract).then_inc(s_q_lo[p], 1)

                    for g in range(KV_HEADS):
                        dve.wait_ge(s_k_hi, g + 1)
                        nc.vector.tensor_tensor(kT[HEAD:, g, :], k_in[HEAD:, g, :], kT[HEAD:, g, :].bitcast(F32), ALU.subtract
                                                ).then_inc(s_k_lo, 1)
                    for p in range(3):
                        q_low(0, p)
                    unit_max(0, 1, 0)
                    @turns(dve, NT)
                    def _(i):
                        for u in range(UNITS):
                            if u + 1 < UNITS:
                                unit_max((u + 1) % 2, 8 * i + (u + 1) // 2 + 1, u + 1)
                            else:
                                unit_max(0, 8 * i + 9, 0)
                            dve.wait_ge(s_pT[1], UNITS * i + u + 1)
                            nc.vector.tensor_copy(probT[1], banks[:, 5, :]).then_inc(s_pTe[1], 1)
                            if u == 0:
                                q_low(i, 3)
                            elif u % 4 == 0:
                                q_low(i + 1, u // 4 - 1)
                            if 8 <= u < 13:
                                join_halves(JOIN[u - 8], i, 0)
                            if u < 5 and not first(i):
                                join_halves(JOIN[u], i - 1, 1)
                    for step in JOIN:
                        join_halves(step, NT - 1, 1)

                @block.tensor
                def _(pe):
                    def q_of(h, part):
                        return qb[h // 2][:, h % 2, part, :]

                    def scores(u, turn_q, turn_exp):
                        h, half = u // 2, u % 2
                        pe.wait_ge(s_q_lo[h // 2], turn_q)
                        pe.wait_ge(s_exp[u % 2], turn_exp)
                        for n in range(HALF // BANK):
                            key = half * HALF + n * BANK
                            for part in range(2):
                                ins = nc.tensor.matmul(banks[:, 2 * (u % 2) + n, :], q_of(h, part),
                                                       kT[:, h // 4, key:key + BANK], start=(part == 0), stop=(part == 1))
                        ins.then_inc(s_qk[u % 2], 1)

                    def turn_probs(i, u, g):
                        pe.wait_ge(s_exp[u % 2], 8 * i + u // 2 + 1)
                        pe.wait_ge(s_pTe[g], UNITS * i + u)
                        for j in range(4):
                            ins = nc.tensor.transpose(banks[:, 4 + g, j * P:(j + 1) * P],
                                                      prob[u % 2][:, (4 * g + j) * P:(4 * g + j + 1) * P], ident)
                        ins.then_inc(s_pT[g], 1)

                    def values(i, u, g):
                        kv, half = u // 8, u % 2
                        pe.wait_ge(s_pTe[g], UNITS * i + u + 1)
                        if u % 8 == 0 and g == 0:
                            pe.wait_ge(s_oread[kv], i)
                        for j in range(4):
                            ins = nc.tensor.matmul(banks[:, 6 + kv, (u % 8) * HEAD:(u % 8 + 1) * HEAD],
                                                   probT[g][:, j * P:(j + 1) * P],
                                                   v_sb[:, half * 8 + 4 * g + j, kv * HEAD:(kv + 1) * HEAD],
                                                   start=(g == 0 and j == 0), stop=(g == 1 and j == 3))
                        ins.then_inc(s_pv[g], 1)

                    pe.wait_ge(s_k_lo, KV_HEADS)
                    pe.wait_ge(s_kv, 16)
                    scores(0, 1, 0)
                    @turns(pe, NT)
                    def _(i):
                        for u in range(UNITS):
                            if u + 1 < UNITS:
                                scores(u + 1, i + 1, 8 * i + (u + 1) // 2)
                            else:
                                scores(0, i + 2, 8 * i + 8)
                            turn_probs(i, u, 0)
                            if u:
                                values(i, u - 1, 1)
                            turn_probs(i, u, 1)
                            values(i, u, 0)
                        values(i, UNITS - 1, 1)

                    pe.wait_ge(s_oread[0], NT)
                    pe.wait_ge(s_oread[1], NT)
                    pe.wait_ge(s_max[0], 8 * NT + 1)

            end_phase(sems)

        def branches():
            sems = []
            with ExitStack() as own:
                def sem(name):
                    sems.append(nc.alloc_semaphore(name))
                    return sems[-1]

                def halves(name, a, n):
                    return [own.enter_context(nc.sbuf_tensor(f"{name}_{part}", [P, a * n], F32R))[:, :].rearrange(
                        "p (k n) -> p k n", n=n) for part in ("hi", "lo")]

                w_ao2, w_co2 = halves("w_ao", KC, D), halves("w_co", KC, D)
                oT, cT2 = halves("oT", KC, CH), halves("cT", KC, CH)
                OWN = 4608
                take = Arena(own.enter_context(nc.sbuf_tensor("branch_buffers", [P, OWN], F32)), OWN).take
                o_in = take(CH // P, ATT)
                squares = o_in.rearrange("p a b -> p (a b)").rearrange("p (k n) -> p k n", n=CH)
                cT = take(KC, CH)
                inv_dev = take(CH)
                gate_a, gate_c = (w.rearrange("p (k n) -> p k n", n=CH) for w in (w_ao, w_co))
                QUAD = KD // 2

                s_w_hi, s_w_lo = sem("s_branch_w_hi"), sem("s_branch_w_lo")
                s_oin = sem("s_oin")
                s_ga = [sem(f"s_ga{q}") for q in range(2)]
                s_gc = [sem(f"s_gc{q}") for q in range(2)]
                s_mout = [sem(f"s_mout{q}") for q in range(2)]
                s_mu, s_centred, s_sq, s_var, s_dev = sem("s_mu"), sem("s_centred"), sem("s_sq"), sem("s_var"), sem("s_dev")
                s_cnorm, s_silu, s_cT_hi, s_cT_lo = sem("s_cnorm"), sem("s_conv_silu"), sem("s_cT_hi"), sem("s_cT_lo")
                s_oT, s_oT_hi, s_oT_lo = sem("s_oT"), sem("s_oT_hi"), sem("s_oT_lo")
                s_branch = [sem(f"s_branch{b}") for b in range(2)]
                s_used = [sem(f"s_used{b}") for b in range(2)]
                s_merged = sem("s_merged")
                s_wo = sem("s_wo")
                o_dev = sem("o_dev")
                block = own.enter_context(nc.Block())

                def flat(a):
                    return a.rearrange("p k n -> p (k n)")

                @block.sync
                def _(sp):
                    def fetch_o(i):
                        sp.dma_start(o_in, o_scr.rearrange("(c t) p n -> c p t n", c=NC)[i]).then_inc(s_oin, 16)

                    def fetch_gates(i, q):
                        for gate, sm, first_tile in ((gate_a, s_ga[q], KD), (gate_c, s_gc[q], 0)):
                            at = first_tile + q * QUAD
                            sp.dma_start(gate[:, q * QUAD:(q + 1) * QUAD],
                                         gate_scr[at:at + QUAD, :, bass.ds(i * CH, CH)].rearrange("k p n -> p k n")
                                         ).then_inc(sm, 16)

                    fetch_o(0)
                    sp.wait_ge(s_w_lo, 2)
                    for q in range(2):
                        fetch_gates(0, q)

                    @turns(sp, NC, last=True)
                    def _(i):
                        if not is_last(i, NC):
                            sp.wait_ge(s_var, i + 1)
                            fetch_o(i + 1)
                        else:
                            sp.wait_ge(s_centred, NC)
                            sp.dma_start(conv[:, :, :].rearrange("p a b -> p (a b)").rearrange("p (k n) -> p k n", n=D),
                                         t["w_out"].rearrange("l (k p) n -> p (l k) n", p=P)).then_inc(s_wo, 16)
                        for q in range(2):
                            sp.wait_ge(s_merged, KD * i + (q + 1) * QUAD)
                            sp.dma_start(m_scr[q * QUAD:(q + 1) * QUAD, :, bass.ds(i * CH, CH)].rearrange("k p n -> p k n"),
                                         gate_a[:, q * QUAD:(q + 1) * QUAD]).then_inc(s_mout[q], 16)
                            if not is_last(i, NC):
                                sp.wait_ge(s_mout[q], 16 * i + 16)
                                fetch_gates(i + 1, q)
                    sp.wait_ge(s_wo, 16)
                    for q in range(2):
                        sp.wait_ge(s_mout[q], 16 * NC)

                @block.scalar
                def _(act):
                    for raw, w in ((w_ao, w_ao2), (w_co, w_co2)):
                        nc.scalar.activation(flat(w[0]), raw, ACT.Copy).then_inc(s_w_hi, 1)
                    @turns(act, NC)
                    def _(i):
                        act.wait_ge(s_oT, i + 1)
                        nc.scalar.activation(flat(oT[0]), wide(1, KC * CH), ACT.Copy).then_inc(s_oT_hi, 1)
                        act.wait_ge(s_centred, i + 1)
                        nc.scalar.activation(squares, cT, ACT.Square).then_inc(s_sq, 1)
                        act.wait_ge(s_var, i + 1)
                        nc.scalar.activation(inv_dev, banks[:, 0, :], ACT.Sqrt, bias=eps_t).then_inc(s_dev, 1)
                        act.wait_ge(s_cnorm, i + 1)
                        for k in range(KC):
                            ins = nc.scalar.activation(cT[:, k, :], cT[:, k, :], ACT.Silu, bias=conv_b[:, k:k + 1],
                                                       scale=conv_g[:, k:k + 1])
                        ins.then_inc(s_silu, 1)
                        act.wait_ge(s_silu, i + 1)
                        nc.scalar.activation(flat(cT2[0]), flat(cT), ACT.Copy).then_inc(s_cT_hi, 1)

                @block.vector
                def _(dve):
                    def rest(out, whole, high):
                        return nc.vector.tensor_tensor(flat(out), whole, flat(high).bitcast(F32), ALU.subtract)

                    for n, (raw, w) in enumerate(((w_ao, w_ao2), (w_co, w_co2))):
                        dve.wait_ge(s_w_hi, n + 1)
                        rest(w[1], raw, w[0]).then_inc(s_w_lo, 1)
                    @turns(dve, NC)
                    def _(i):
                        order = Order(dve, o_dev, i, 1)
                        dve.wait_ge(s_oT_hi, i + 1)
                        rest(oT[1], wide(1, KC * CH), oT[0]).then_inc(s_oT_lo, 1)
                        dve.wait_ge(s_mu, i + 1)
                        one = banks[:, 0, :].rearrange("p (o n) -> p o n", o=1).to_broadcast([P, KC, CH])
                        nc.vector.tensor_tensor(cT, conv[:, :, bass.ts(i, CH)], one, ALU.subtract).then_inc(s_centred, 1)

                        def branch(d, gate, ready, fold):
                            n = 8 * i + (KD + d if fold else d) // 2 + 1
                            if d % QUAD == 0:
                                dve.wait_ge(ready[d // QUAD], 16 * i + 16)
                            dve.wait_ge(s_branch[d % 2], n)
                            nc.vector.tensor_tensor(gate[:, d, :], banks[:, 5 + d % 2, :], gate[:, d, :], ALU.mult
                                                    ).then_inc(s_used[d % 2], 1)
                            if fold:
                                dve.wait_ge(s_used[d % 2], n)
                                nc.vector.tensor_tensor(gate_a[:, d, :], gate_a[:, d, :], gate_c[:, d, :], ALU.add
                                                        ).then_inc(s_merged, 1)

                        for d in range(2):
                            branch(d, gate_a, s_ga, False)
                        dve.wait_ge(s_dev, i + 1)
                        order.link(nc.vector.reciprocal(inv_dev, inv_dev))
                        nc.vector.tensor_tensor(cT, cT, inv_dev.rearrange("p (o n) -> p o n", o=1).to_broadcast([P, KC, CH]),
                                                ALU.mult).then_inc(s_cnorm, 1)
                        for d in range(2, KD):
                            branch(d, gate_a, s_ga, False)
                        dve.wait_ge(s_cT_hi, i + 1)
                        rest(cT2[1], flat(cT), cT2[0]).then_inc(s_cT_lo, 1)
                        for d in range(KD):
                            branch(d, gate_c, s_gc, True)

                @block.tensor
                def _(pe):
                    def mean(i):
                        pe.wait_ge(s_dev, i)
                        for k in range(KC):
                            ins = nc.tensor.matmul(banks[:, 0, :], mean_w, conv[:, k, bass.ts(i, CH)],
                                                   start=(k == 0), stop=(k == KC - 1))
                        ins.then_inc(s_mu, 1)

                    @turns(pe, NC)
                    def _(i):
                        mean(i)
                        pe.wait_ge(s_oin, 16 * i + 16)
                        pe.wait_ge(s_oT_lo, i)
                        for j in range(KC):
                            for n in range(CH // P):
                                ins = nc.tensor.transpose(banks[:, 1 + j, n * P:(n + 1) * P], o_in[:, n, j * P:(j + 1) * P],
                                                          ident)
                        ins.then_inc(s_oT, 1)

                        def branch(d, w, src, turn, hi_ready, lo_ready, w_ready):
                            pe.wait_ge(s_used[d % 2], turn)
                            for part, (a, b) in enumerate(((0, 0), (1, 0), (0, 1))):
                                if d == 0 and part == 0:
                                    pe.wait_ge(s_w_hi, w_ready)
                                    pe.wait_ge(hi_ready, i + 1)
                                if d == 0 and part == 1:
                                    pe.wait_ge(s_w_lo, w_ready)
                                if d == 0 and part == 2:
                                    pe.wait_ge(lo_ready, i + 1)
                                for k in range(KC):
                                    ins = nc.tensor.matmul(banks[:, 5 + d % 2, :], w[a][:, k, d * P:(d + 1) * P], src[b][:, k, :],
                                                           start=(part == 0 and k == 0), stop=(part == 2 and k == KC - 1))
                            ins.then_inc(s_branch[d % 2], 1)

                        for d in range(KD):
                            branch(d, w_ao2, oT, 8 * i + d // 2, s_oT_hi, s_oT_lo, 1)
                            if d == 1:
                                pe.wait_ge(s_sq, i + 1)
                                for k in range(KC):
                                    ins = nc.tensor.matmul(banks[:, 0, :], mean_w, squares[:, k, :],
                                                           start=(k == 0), stop=(k == KC - 1))
                                ins.then_inc(s_var, 1)
                        for d in range(KD):
                            branch(d, w_co2, cT2, 8 * i + 4 + d // 2, s_cT_hi, s_cT_lo, 2)
                    for b in range(2):
                        pe.wait_ge(s_used[b], 8 * NC)
                    pe.wait_ge(s_dev, NC)

            end_phase(sems)

        def merge():
            sems = []
            with ExitStack() as own:
                def sem(name):
                    sems.append(nc.alloc_semaphore(name))
                    return sems[-1]

                def halves(name, a, n):
                    return [own.enter_context(nc.sbuf_tensor(f"{name}_{part}", [P, a * n], F32R))[:, :].rearrange(
                        "p (k n) -> p k n", n=n) for part in ("hi", "lo")]

                w_o = halves("w_out", KD, D)
                merged = [halves(f"merged{b}", KD, P) for b in range(2)]
                raw_w = conv.rearrange("p a b -> p (a b)")
                OWN = 7500
                take = Arena(own.enter_context(nc.sbuf_tensor("merge_buffers", [P, OWN], F32)), OWN).take
                m_in = [take(KD, P) for _ in range(2)]
                xm = [take(D) for _ in range(2)]
                ym = [take(D) for _ in range(2)]
                h2T = take(KD, P)
                w_r = take(KD, LOGITS)
                mst = [take(4) for _ in range(2)]

                s_rb = sem("s_rb")
                s_w_hi, s_w_lo = sem("s_w_out_hi"), sem("s_w_out_lo")
                s_min = [sem(f"s_min{b}") for b in range(2)]
                s_m_hi = [sem(f"s_m_hi{b}") for b in range(2)]
                s_m_lo = [sem(f"s_m_lo{b}") for b in range(2)]
                s_wout = [sem(f"s_wout{b}") for b in range(2)]
                s_xm = [sem(f"s_xm{b}") for b in range(2)]
                s_ydev = [sem(f"s_ydev{b}") for b in range(2)]
                s_x1 = [sem(f"s_x1{b}") for b in range(2)]
                s_x1out = [sem(f"s_x1out{b}") for b in range(2)]
                s_x1dev = [sem(f"s_x1dev{b}") for b in range(2)]
                s_h2 = [sem(f"s_h2{b}") for b in range(2)]
                s_h2out = [sem(f"s_h2out{b}") for b in range(2)]
                s_h2T, s_h2Ta, s_h2Tv = sem("s_h2T"), sem("s_h2Ta"), sem("s_h2Tv")
                s_logit, s_logitc = sem("s_logit"), sem("s_logitc")
                o_merge, o_mact = sem("o_merge"), sem("o_mact")
                block = own.enter_context(nc.Block())

                def flat(a):
                    return a.rearrange("p k n -> p (k n)")

                HALF_W = KD * D // 2
                TURNS = NT // 2

                def very_first(i, b):
                    return isinstance(i, int) and i == 0 and b == 0

                @block.sync
                def _(sp):
                    def fetch_merged(i, b):
                        sp.wait_ge(s_m_lo[b], i)
                        sp.dma_start(m_in[b], m_scr[:, :, bass.ds((2 * i + b) * P, P)].rearrange("k p n -> p k n")
                                     ).then_inc(s_min[b], 16)

                    def fetch_x(i, b):
                        sp.wait_ge(s_x1out[b], 16 * i)
                        sp.dma_start(xm[b], x_v[2 * i + b]).then_inc(s_xm[b], 16)

                    for b in range(2):
                        fetch_merged(0, b)
                    for b in range(2):
                        fetch_x(0, b)
                    with nc.allow_non_contiguous_dma(reason="36 columns of two matrices"):
                        sp.dma_start(w_r[:, :, 0:GROUPS], t["w_group"].rearrange("l (k p) n -> p (l k) n", p=P)
                                     ).then_inc(s_rb, 16)
                        sp.dma_start(w_r[:, :, GROUPS:], t["w_router"].rearrange("l (k p) n -> p (l k) n", p=P)
                                     ).then_inc(s_rb, 16)
                    sp.dma_start(rbias[:, 0:GROUPS], t["b_group"][0:1, :].to_broadcast([P, GROUPS])).then_inc(s_rb, 16)
                    sp.dma_start(rbias[:, GROUPS:], t["b_router"][0:1, :].to_broadcast([P, EXPERTS])).then_inc(s_rb, 16)
                    @turns(sp, TURNS, last=True)
                    def _(i):
                        for b in range(2):
                            if not is_last(i, TURNS):
                                fetch_merged(i + 1, b)
                            sp.wait_ge(s_x1[b], i + 1)
                            sp.dma_start(x1_scr[bass.ds((2 * i + b) * P, P), :], xm[b]).then_inc(s_x1out[b], 16)
                            sp.wait_ge(s_h2[b], i + 1)
                            sp.dma_start(h2_scr[bass.ds((2 * i + b) * P, P), :], ym[b]).then_inc(s_h2out[b], 16)
                            if not is_last(i, TURNS):
                                fetch_x(i + 1, b)
                    for b in range(2):
                        sp.wait_ge(s_x1out[b], 16 * TURNS)
                        sp.wait_ge(s_h2out[b], 16 * TURNS)

                @block.scalar
                def _(act):
                    def high(i, b):
                        act.wait_ge(s_min[b], 16 * i + 16)
                        act.wait_ge(s_wout[b], i)
                        nc.scalar.activation(flat(merged[b][0]), flat(m_in[b]), ACT.Copy).then_inc(s_m_hi[b], 1)

                    def h2T_out(n):
                        act.wait_ge(s_h2T, n + 1)
                        nc.scalar.activation(h2T[:, 0:4, :], banks[:, 5, :].rearrange("p (k n) -> p k n", n=P), ACT.Copy
                                             ).then_inc(s_h2Ta, 1)

                    for n in range(2):
                        part = slice(n * HALF_W, (n + 1) * HALF_W)
                        nc.scalar.activation(flat(w_o[0])[:, part], raw_w[:, part], ACT.Copy).then_inc(s_w_hi, 1)
                        if n == 0:
                            high(0, 0)
                    @turns(act, TURNS, last=True)
                    def _(i):
                        order = Order(act, o_mact, i, 4)
                        for b in range(2):
                            if b == 0:
                                high(i, 1)
                            elif not is_last(i, TURNS):
                                high(i + 1, 0)
                            if not very_first(i, b):
                                h2T_out(2 * i + b - 1)
                            y = wide(1 + 2 * b, D)
                            act.wait_ge(s_wout[b], i + 1)
                            act.wait_ge(s_h2out[b], 16 * i)
                            order.link(nc.scalar.activation(ym[b], y, ACT.Square, accum_out=mst[b][:, 0:1]))
                            nc.scalar.activation(mst[b][:, 1:2], mst[b][:, 0:1], ACT.Sqrt, bias=eps_t, scale=1.0 / D
                                                 ).then_inc(s_ydev[b], 1)
                            act.wait_ge(s_x1[b], i + 1)
                            order.link(nc.scalar.activation(ym[b], xm[b], ACT.Square, accum_out=mst[b][:, 2:3]))
                            nc.scalar.activation(mst[b][:, 3:4], mst[b][:, 2:3], ACT.Sqrt, bias=eps_t, scale=1.0 / D
                                                 ).then_inc(s_x1dev[b], 1)
                    h2T_out(NT - 1)

                @block.vector
                def _(dve):
                    def low(i, b):
                        dve.wait_ge(s_m_hi[b], i + 1)
                        nc.vector.tensor_tensor(flat(merged[b][1]), flat(m_in[b]), flat(merged[b][0]).bitcast(F32), ALU.subtract
                                                ).then_inc(s_m_lo[b], 1)

                    def h2T_out(n):
                        dve.wait_ge(s_h2T, n + 1)
                        nc.vector.tensor_copy(h2T[:, 4:8, :], banks[:, 6, :].rearrange("p (k n) -> p k n", n=P)
                                              ).then_inc(s_h2Tv, 1)

                    def logits_out(n):
                        dve.wait_ge(s_logit, n + 1)
                        nc.vector.tensor_copy(logits[:, bass.ds(n, 1), :].rearrange("p a b -> p (a b)"),
                                              banks[:, 7, 0:LOGITS]).then_inc(s_logitc, 1)

                    for n in range(2):
                        part = slice(n * HALF_W, (n + 1) * HALF_W)
                        if n:
                            low(0, 0)
                        dve.wait_ge(s_w_hi, n + 1)
                        nc.vector.tensor_tensor(flat(w_o[1])[:, part], raw_w[:, part], flat(w_o[0])[:, part].bitcast(F32),
                                                ALU.subtract).then_inc(s_w_lo, 1)
                    @turns(dve, TURNS, last=True)
                    def _(i):
                        order = Order(dve, o_merge, i, 8)
                        for b in range(2):
                            if b == 0:
                                low(i, 1)
                            elif not is_last(i, TURNS):
                                low(i + 1, 0)
                            if not very_first(i, b):
                                h2T_out(2 * i + b - 1)
                            y = wide(1 + 2 * b, D)
                            dve.wait_ge(s_ydev[b], i + 1)
                            order.link(nc.vector.reciprocal(mst[b][:, 0:1], mst[b][:, 1:2]))
                            order.link(nc.vector.scalar_tensor_tensor(out=ym[b], in0=y, scalar=mst[b][:, 0:1],
                                                                      in1=rows[:, 0, :], op0=ALU.mult, op1=ALU.mult))
                            dve.wait_ge(s_xm[b], 16 * i + 16)
                            nc.vector.tensor_tensor(xm[b], xm[b], ym[b], ALU.add).then_inc(s_x1[b], 1)
                            dve.wait_ge(s_x1dev[b], i + 1)
                            order.link(nc.vector.reciprocal(mst[b][:, 2:3], mst[b][:, 3:4]))
                            order.link(nc.vector.scalar_tensor_tensor(out=ym[b], in0=xm[b], scalar=mst[b][:, 2:3],
                                                                      in1=rows[:, 2, :], op0=ALU.mult, op1=ALU.mult))
                            nc.vector.tensor_tensor(ym[b], ym[b], rows[:, 1, :], ALU.add).then_inc(s_h2[b], 1)
                            if not very_first(i, b):
                                logits_out(2 * i + b - 1)
                    h2T_out(NT - 1)
                    logits_out(NT - 1)

                @block.tensor
                def _(pe):
                    def route_logits(n, b, turn):
                        pe.wait_ge(s_h2[b], turn)
                        pe.wait_ge(s_h2Ta, n)
                        pe.wait_ge(s_h2Tv, n)
                        for k in range(KD):
                            ins = nc.tensor.transpose(banks[:, 5 + k // 4, (k % 4) * P:(k % 4 + 1) * P],
                                                      ym[b][:, k * P:(k + 1) * P], ident)
                        ins.then_inc(s_h2T, 1)
                        pe.wait_ge(s_h2Ta, n + 1)
                        pe.wait_ge(s_h2Tv, n + 1)
                        pe.wait_ge(s_logitc, n)
                        for k in range(KD):
                            ins = nc.tensor.matmul(banks[:, 7, 0:LOGITS], h2T[:, k, :], w_r[:, k, :],
                                                   start=(k == 0), stop=(k == KD - 1))
                        ins.then_inc(s_logit, 1)

                    pe.wait_ge(s_rb, 64)
                    pe.wait_ge(s_w_hi, 2)
                    @turns(pe, TURNS)
                    def _(i):
                        for b in range(2):
                            pe.wait_ge(s_h2[b], i)
                            for o in range(2):
                                for part, (a, c) in enumerate(((0, 0), (1, 0), (0, 1))):
                                    if o == 0 and part == 0:
                                        pe.wait_ge(s_m_hi[b], i + 1)
                                    if o == 0 and part == 1:
                                        pe.wait_ge(s_m_lo[b], i + 1)
                                    if o == 0 and part == 2:
                                        pe.wait_ge(s_w_lo, 2)
                                    for k in range(KD):
                                        ins = nc.tensor.matmul(banks[:, 1 + 2 * b + o, :], merged[b][a][:, k, :],
                                                               w_o[c][:, k, o * BANK:(o + 1) * BANK],
                                                               start=(part == 0 and k == 0), stop=(part == 2 and k == KD - 1))
                            ins.then_inc(s_wout[b], 1)
                            if b:
                                route_logits(2 * i, 0, i + 1)
                            elif not isinstance(i, int):
                                route_logits(2 * i - 1, 1, i)
                    route_logits(NT - 1, 1, TURNS)

            end_phase(sems)

        def experts():
            sems = []
            with ExitStack() as own:
                def sem(name):
                    sems.append(nc.alloc_semaphore(name))
                    return sems[-1]

                def tensor(name, size, dt=F32):
                    return own.enter_context(nc.sbuf_tensor(name, [P, size], dt))

                def halves(name, a, n):
                    return [tensor(f"{name}_{part}", a * n, F32R)[:, :].rearrange("p (k n) -> p k n", n=n)
                            for part in ("hi", "lo")]

                lists = Arena(tensor("lists", 1500), 1500)
                iota = lists.take(P)
                iota_i = lists.take(P).bitcast(I32)
                token = lists.take(NT)
                token_i = lists.take(NT).bitcast(I32)
                slots_of = lists.take(2, NT)
                slots_i = lists.take(2, NT).bitcast(I32)
                slots_hi = lists.take(2, NT)
                slots_lo = lists.take(2, NT)
                weights = lists.take(2, NT)
                block_expert = lists.take(BLOCKS)
                block_expert_i = lists.take(BLOCKS).bitcast(I32)
                load = lists.take(BLOCKS + 1)
                load_i = lists.take(BLOCKS + 1).bitcast(I32)
                y_count, y_count_i = lists.take(2), lists.take(2).bitcast(I32)
                slot_token = lists.take(BLOCKS).bitcast(I32)

                stage = [tensor(f"stage_{n}", KD * D_EXPERT)[:, :] for n in ("gate", "up", "down")]
                w_g = halves("w_gate", KD, D_EXPERT)
                w_u = halves("w_up", KD, D_EXPERT)
                w_d = halves("w_down", KF, D)
                xT = halves("x_T", KD, P)
                actT = halves("act_T", KF, P)
                OWN = 4 * D + 2 * D_EXPERT
                buffers = Arena(tensor("expert_buffers", OWN), OWN)
                take = buffers.take
                xg = [take(D) for _ in range(2)]
                act_g = take(D_EXPERT)
                act_u = take(D_EXPERT)
                ys = [take(D) for _ in range(2)]

                buffers.at = 0
                top_g, sum_g, exp_g = take(NT), take(NT), take(NT, GROUPS)
                hot_g, cand_g, first_g = take(NT, GROUPS), take(NT, GROUPS), take(NT)
                masked = take(NT, EXPERTS)
                cand = take(NT, EXPERTS)
                hot = [take(NT, EXPERTS) for _ in range(2)]
                picked = take(NT, EXPERTS)
                top, first = [take(NT) for _ in range(2)], take(NT)
                ratio = take(NT)
                base = take(NT + 1, EXPERTS)
                blocks_of = take(EXPERTS, NT)
                run = [take(EXPERTS) for _ in range(2)]
                counts = take(EXPERTS)
                used = take(EXPERTS)
                exists = take(BLOCKS)
                take = Arena(stage[1], KD * D_EXPERT).take
                reached = take(BLOCKS, EXPERTS)
                of_block = [take(NT, BLOCKS) for _ in range(2)]
                take = Arena(stage[2], KD * D_EXPERT).take
                in_block = [take(NT, P) for _ in range(2)]

                SLOTS = 4
                yj = [[stage[n // 2][:, (2 * (n % 2) + a) * D:(2 * (n % 2) + a + 1) * D] for a in range(2)]
                      for n in range(SLOTS)]
                xj = [stage[2][:, n * D:(n + 1) * D] for n in range(SLOTS)]
                jjunk = xg[0]
                jst = [xg[1][:, 2 * n:2 * n + 2] for n in range(SLOTS)]

                o_route = sem("o_route")
                s_iota = sem("s_iota")
                s_gdiff, s_gexp, s_ediff, s_eexp = sem("s_gdiff"), sem("s_gexp"), sem("s_ediff"), sem("s_eexp")
                s_picked, s_rank = sem("s_picked"), sem("s_rank")
                s_onehot, s_list = sem("s_onehot"), sem("s_list")
                s_blocks, s_lists = sem("s_blocks"), sem("s_lists")
                s_w = [sem(f"s_w_{n}") for n in ("gate", "up", "down")]
                s_hi = [sem(f"s_hi_{n}") for n in ("gate", "up", "down")]
                s_lo = [sem(f"s_lo_{n}") for n in ("gate", "up", "down")]
                s_lo_pool = sem("s_lo_pool")
                s_xg = [sem(f"s_xg{s}") for s in range(2)]
                s_xgT, s_xT_hi, s_xT_lo = sem("s_xgT"), sem("s_xT_hi"), sem("s_xT_lo")
                s_gate, s_up, s_down = sem("s_gate"), sem("s_up"), sem("s_down")
                s_silu, s_act, s_actT = sem("s_silu"), sem("s_act"), sem("s_actT")
                s_actT_hi, s_actT_lo = sem("s_actT_hi"), sem("s_actT_lo")
                s_ya, s_yv = sem("s_ya"), sem("s_yv")
                s_yout = [sem(f"s_yout{s}") for s in range(2)]
                s_y = sem("s_y")
                s_yj = [sem(f"s_yj{s}") for s in range(SLOTS)]
                s_xj = [sem(f"s_xj{s}") for s in range(SLOTS)]
                s_jsum = [sem(f"s_jsum{s}") for s in range(SLOTS)]
                s_jdev = [sem(f"s_jdev{s}") for s in range(SLOTS)]
                s_jout = [sem(f"s_jout{s}") for s in range(SLOTS)]
                s_out = [sem(f"s_out{s}") for s in range(SLOTS)]
                o_jsum, o_jdve, o_jact = sem("o_jsum"), sem("o_jdve"), sem("o_jact")
                block = own.enter_context(nc.Block())
                flat = lambda a: a.rearrange("p a b -> p (a b)")
                SHARE = KF * D // 2

                def load_of(eng, j):
                    at = load_i[0:1, j:j + 1] if isinstance(j, int) else load_i[0:1, bass.ds(j, 1)]
                    return eng.value_load(at, min_val=0, max_val=EXPERTS)

                def loads_of(eng, j):
                    return load_of(eng, j), load_of(eng, j + 1)

                def blocks(eng):
                    def run(body):
                        def block_pair(i):
                            for s in range(2):
                                j = 2 * i + s
                                this = load_of(eng, j)
                                with eng.If(this > 0):
                                    after = load_of(eng, j + 1)

                                    def more(step):
                                        with eng.If(after > 0):
                                            step()

                                    def new(step):
                                        with eng.If(after > this):
                                            step(after)

                                    body(j, s, i, more, new)
                        block_pair(0)
                        with eng.Fori(1, BLOCKS // 2) as i:
                            block_pair(i)
                    return run

                @block.sync
                def _(sp):
                    names = ("w_e_gate", "w_e_up", "w_e_down")

                    def fetch(j, before):
                        e = sp.value_load(block_expert_i[0:1, j:j + 1] if isinstance(j, int)
                                          else block_expert_i[0:1, bass.ds(j, 1)], min_val=0, max_val=EXPERTS - 1)
                        for n in range(3):
                            if before is not None:
                                sp.wait_ge(s_hi[n], before)
                                sp.wait_ge(s_lo[n], before)
                                if n == 2:
                                    sp.wait_ge(s_lo_pool, before)
                            elif n == 1:
                                sp.wait_ge(s_lists, 1)
                            sp.dma_start(stage[n].rearrange("p (k n) -> p k n", n=(D_EXPERT, D_EXPERT, D)[n]),
                                         t[names[n]][0, bass.ds(e, 1)].rearrange("e (k p) n -> p (e k) n", p=P)
                                         ).then_inc(s_w[n], 16)

                    sp.wait_ge(s_blocks, 1)
                    fetch(0, None)
                    with sp.Fori(1, BLOCKS) as j:
                        last, this = loads_of(sp, j - 1)
                        with sp.If(this > last):
                            fetch(j, last)
                    sp.wait_ge(s_y, 1)
                    @turns(sp, NT // SLOTS)
                    def _(i):
                        for s in range(SLOTS):
                            sp.wait_ge(s_out[s], 16 * i)
                            sp.dma_start(xj[s], x1_scr[bass.ts(SLOTS * i + s, P), :]).then_inc(s_xj[s], 16)
                        for s in range(SLOTS):
                            sp.wait_ge(s_jout[s], i + 1)
                            sp.dma_start(out_v[SLOTS * i + s], xj[s]).then_inc(s_out[s], 16)
                    for s in range(SLOTS):
                        sp.wait_ge(s_out[s], 16 * (NT // SLOTS))

                @block.gpsimd
                def _(pool):
                    nc.gpsimd.iota(iota_i, [[1, P]], base=0, channel_multiplier=0).then_inc(s_iota, 1)
                    nc.gpsimd.iota(token_i, [[P, NT]], base=0, channel_multiplier=1).then_inc(s_iota, 1)
                    pool.wait_ge(s_lists, 1)
                    def gather(j):
                        if j >= 2:
                            pool.wait_ge(s_xgT, j - 1)
                        nc.gpsimd.indirect_dma_start(out=xg[j % 2], out_offset=None, in_=h2_scr[:, :],
                                                     in_offset=bass.IndirectOffsetOnAxis(
                                                         ap=slot_token[:, j:j + 1], axis=0)).then_inc(s_xg[j % 2], 16)

                    def split(this):
                        pool.wait_ge(s_hi[2], this)
                        nc.gpsimd.tensor_tensor(flat(w_d[1])[:, SHARE:], stage[2][:, SHARE:],
                                                flat(w_d[0])[:, SHARE:].bitcast(F32), ALU.subtract).then_inc(s_lo_pool, 1)

                    gather(0)
                    gather(1)
                    split(1)
                    this = load_of(pool, 0)
                    for j in range(1, BLOCKS):
                        last, this = this, load_of(pool, j)
                        if j + 1 < 2 * S // P:
                            gather(j + 1)
                        elif j + 1 < BLOCKS:
                            with pool.If(load_of(pool, j + 1) > 0):
                                gather(j + 1)
                        with pool.If(this > last):
                            split(this)
                    pool.wait_ge(s_y, 1)
                    for n in range(NT):
                        s = n % SLOTS
                        pool.wait_ge(s_jout[s], n // SLOTS)
                        for a in range(2):
                            nc.gpsimd.indirect_dma_start(out=yj[s][a], out_offset=None, in_=y_scr[:, :],
                                                         in_offset=bass.IndirectOffsetOnAxis(
                                                             ap=slots_i[:, a, n:n + 1], axis=0)).then_inc(s_yj[s], 16)

                @block.scalar
                def _(act):
                    act.wait_ge(s_gdiff, 1)
                    nc.scalar.activation(exp_g, exp_g, ACT.Exp).then_inc(s_gexp, 1)
                    act.wait_ge(s_ediff, 1)
                    nc.scalar.activation(ratio, ratio, ACT.Exp).then_inc(s_eexp, 1)
                    def split(n, w, this):
                        act.wait_ge(s_w[n], 16 * this)
                        nc.scalar.activation(flat(w[0]), stage[n], ACT.Copy).then_inc(s_hi[n], 1)

                    def xT_out(turn):
                        act.wait_ge(s_xgT, turn)
                        nc.scalar.activation(flat(xT[0]), wide(2, D), ACT.Copy).then_inc(s_xT_hi, 1)

                    for n, w in enumerate((w_g, w_u, w_d)):
                        split(n, w, 1)
                    xT_out(1)
                    @blocks(act)
                    def _(j, s, i, more, new):
                        act.wait_ge(s_gate, j + 1)
                        nc.scalar.activation(act_g, banks[:, 0, :], ACT.Silu).then_inc(s_silu, 1)
                        new(lambda this: split(0, w_g, this))
                        act.wait_ge(s_actT, j + 1)
                        nc.scalar.activation(flat(actT[0]), banks[:, 4, :], ACT.Copy).then_inc(s_actT_hi, 1)
                        more(lambda: xT_out(j + 2))
                        new(lambda this: split(1, w_u, this))
                        act.wait_ge(s_down, j + 1)
                        act.wait_ge(s_yout[s], 16 * i)
                        nc.scalar.activation(ys[s][:, 0:BANK], banks[:, 5, :], ACT.Copy).then_inc(s_ya, 1)
                        new(lambda this: split(2, w_d, this))
                        act.wait_ge(s_ya, j + 1)
                        act.wait_ge(s_yv, j + 1)
                        act.dma_start(y_scr[bass.ds(j * P, P), :], ys[s]).then_inc(s_yout[s], 16)
                    sent = [act.value_load(y_count_i[0:1, s:s + 1], min_val=16, max_val=16 * BLOCKS) for s in range(2)]
                    for s in range(2):
                        act.wait_ge(s_yout[s], sent[s])
                    nc.scalar.activation(act_g, act_g, ACT.Copy).then_inc(s_y, 1)
                    @turns(act, NT // SLOTS)
                    def _(i):
                        order = Order(act, o_jact, i, SLOTS)
                        for s in range(SLOTS):
                            act.wait_ge(s_jsum[s], i + 1)
                            order.link(nc.scalar.activation(jjunk, yj[s][0], ACT.Square, accum_out=jst[s][:, 0:1]))
                            nc.scalar.activation(jst[s][:, 1:2], jst[s][:, 0:1], ACT.Sqrt, bias=eps_t, scale=1.0 / D
                                                 ).then_inc(s_jdev[s], 1)

                @block.vector
                def _(dve):
                    order = Order(dve, o_route)
                    L = order.link
                    tt, ts = nc.vector.tensor_tensor, nc.vector.tensor_scalar

                    def over(ap, n):
                        return ap.rearrange("p (a o) -> p a o", o=1).to_broadcast([P, ap.shape[1], n])

                    def along(ap, n):
                        return ap.rearrange("p (o a) -> p o a", o=1).to_broadcast([P, n, ap.shape[1]])

                    dve.wait_ge(s_iota, 2)
                    L(nc.vector.tensor_copy(iota, iota_i))
                    L(nc.vector.tensor_copy(token, token_i))
                    L(tt(logits, logits, along(rbias, NT), ALU.add))
                    lg, le = logits[:, :, 0:GROUPS], logits[:, :, GROUPS:]
                    L(nc.vector.tensor_reduce(top_g, lg, AX.X, ALU.max))
                    tt(exp_g, lg, over(top_g, GROUPS), ALU.subtract).then_inc(s_gdiff, 1)

                    def first_of(scores, best, n, cand, low, hot):
                        L(tt(cand, scores, over(best, n), ALU.is_equal))
                        L(nc.vector.scalar_tensor_tensor(out=cand, in0=cand, scalar=-64.0, in1=along(iota[:, 0:n], NT),
                                                         op0=ALU.mult, op1=ALU.add))
                        L(nc.vector.tensor_reduce(low, cand, AX.X, ALU.min))
                        L(tt(hot, cand, over(low, n), ALU.is_equal))

                    first_of(lg, top_g, GROUPS, cand_g, first_g, hot_g)
                    hot_wide = over(hot_g.rearrange("p t g -> p (t g)"), PER_GROUP)
                    by_group = lambda a: a.rearrange("p t (g e) -> p (t g) e", e=PER_GROUP)
                    L(nc.vector.tensor_copy(picked, le))
                    L(tt(by_group(masked), by_group(picked), hot_wide, ALU.mult))
                    L(ts(cand_g, hot_g, BIG, -BIG, ALU.mult, ALU.add))
                    L(tt(by_group(masked), by_group(masked), over(cand_g.rearrange("p t g -> p (t g)"), PER_GROUP), ALU.add))
                    L(nc.vector.tensor_reduce(top[0], masked, AX.X, ALU.max))
                    first_of(masked, top[0], EXPERTS, cand, first, hot[0])
                    L(nc.vector.scalar_tensor_tensor(out=masked, in0=hot[0], scalar=-4.0 * BIG, in1=masked,
                                                     op0=ALU.mult, op1=ALU.add))
                    L(nc.vector.tensor_reduce(top[1], masked, AX.X, ALU.max))
                    first_of(masked, top[1], EXPERTS, cand, first, hot[1])
                    tt(picked, hot[0], hot[1], ALU.add).then_inc(s_picked, 1)
                    tt(ratio, top[1], top[0], ALU.subtract).then_inc(s_ediff, 1)
                    dve.wait_ge(s_gexp, 1)
                    L(nc.vector.tensor_reduce(sum_g, exp_g, AX.X, ALU.add))
                    dve.wait_ge(s_eexp, 1)
                    L(nc.vector.scalar_tensor_tensor(out=sum_g, in0=ratio, scalar=1.0, in1=sum_g, op0=ALU.add, op1=ALU.mult))
                    L(nc.vector.reciprocal(weights[:, 0, :], sum_g))
                    L(tt(weights[:, 1, :], weights[:, 0, :], ratio, ALU.mult))
                    dve.wait_ge(s_rank, 1)
                    L(nc.vector.memset(base[:, 0, :], 0.0))
                    totals = banks[:, 1, :].rearrange("p (t e) -> p t e", e=EXPERTS)
                    for n in range(NT):
                        L(tt(base[:, n + 1, :], base[:, n, :], totals[:, n, :], ALU.add))
                    L(ts(blocks_of.rearrange("p e n -> p (e n)")[:, 0:NT], iota[:, 0:NT], float(P), None, ALU.mult))
                    L(nc.vector.tensor_copy(run[1][:, 0:NT], blocks_of.rearrange("p e n -> p (e n)")[:, 0:NT]))
                    L(tt(blocks_of, over(base[:, NT, :], NT), along(run[1][:, 0:NT], EXPERTS), ALU.is_gt))
                    L(nc.vector.tensor_reduce(counts, blocks_of, AX.X, ALU.add))
                    L(nc.vector.tensor_copy(run[0], counts))
                    side = 0
                    for step in (1, 2, 4, 8, 16):
                        L(nc.vector.tensor_copy(run[1 - side][:, 0:step], run[side][:, 0:step]))
                        L(tt(run[1 - side][:, step:], run[side][:, step:], run[side][:, 0:EXPERTS - step], ALU.add))
                        side = 1 - side
                    ends = run[side]
                    L(tt(reached, over(iota[:, 0:BLOCKS], EXPERTS), along(ends, BLOCKS), ALU.is_ge))
                    L(nc.vector.tensor_reduce(block_expert, reached, AX.X, ALU.add))
                    L(ts(block_expert, block_expert, float(EXPERTS - 1), None, ALU.min))
                    L(nc.vector.tensor_copy(block_expert_i, block_expert))
                    L(tt(run[1 - side], ends, counts, ALU.subtract))
                    L(ts(used, counts, 0.0, None, ALU.is_gt))
                    L(tt(reached, over(iota[:, 0:BLOCKS], EXPERTS), along(run[1 - side], BLOCKS), ALU.is_ge))
                    L(tt(reached, reached, along(used, BLOCKS), ALU.mult))
                    L(nc.vector.memset(load, 0.0))
                    L(nc.vector.tensor_reduce(load[:, 0:BLOCKS], reached, AX.X, ALU.add))
                    L(ts(exists, iota[:, 0:BLOCKS], ends[:, EXPERTS - 1:EXPERTS], None, ALU.is_lt))
                    L(tt(load[:, 0:BLOCKS], load[:, 0:BLOCKS], exists, ALU.mult))
                    L(nc.vector.tensor_reduce(y_count, exists.rearrange("p (i s) -> p s i", s=2), AX.X, ALU.add))
                    L(ts(y_count, y_count, 16.0, None, ALU.mult))
                    L(nc.vector.tensor_copy(y_count_i, y_count))
                    nc.vector.tensor_copy(load_i, load).then_inc(s_blocks, 1)
                    L(ts(run[1 - side], run[1 - side], float(P), None, ALU.mult))
                    slot = cand
                    L(tt(slot, banks[:, 0, :].rearrange("p (t e) -> p t e", e=EXPERTS), base[:, 0:NT, :], ALU.add))
                    L(tt(slot, slot, along(run[1 - side], NT), ALU.add))
                    for a in range(2):
                        L(tt(masked, slot, hot[a], ALU.mult))
                        L(nc.vector.tensor_reduce(slots_of[:, a, :], masked, AX.X, ALU.add))
                    L(nc.vector.tensor_copy(slots_i, slots_of))
                    hi_i, lo_i = picked.rearrange("p a b -> p (a b)")[:, 0:2 * NT].bitcast(I32), cand.rearrange(
                        "p a b -> p (a b)")[:, 0:2 * NT].bitcast(I32)
                    L(ts(hi_i, flat(slots_i), 7, None, ALU.logical_shift_right))
                    L(ts(lo_i, flat(slots_i), P - 1, None, ALU.bitwise_and))
                    L(nc.vector.tensor_copy(flat(slots_hi), hi_i))
                    L(nc.vector.tensor_copy(flat(slots_lo), lo_i))
                    for a in range(2):
                        L(tt(of_block[a], along(iota[:, 0:BLOCKS], NT), over(slots_hi[:, a, :], BLOCKS), ALU.is_equal))
                        L(tt(of_block[a], of_block[a], over(token, BLOCKS), ALU.mult))
                        tt(in_block[a], along(iota, NT), over(slots_lo[:, a, :], P), ALU.is_equal).then_inc(s_onehot, 1)
                    dve.wait_ge(s_list, 1)
                    nc.vector.tensor_copy(slot_token, banks[:, 2, 0:BLOCKS]).then_inc(s_lists, 1)

                    def rest(out, whole, high):
                        return tt(flat(out), whole, flat(high).bitcast(F32), ALU.subtract)

                    def split(n, w, this):
                        dve.wait_ge(s_hi[n], this)
                        part = slice(0, SHARE if n == 2 else KD * D_EXPERT)
                        tt(flat(w[1])[:, part], stage[n][:, part], flat(w[0])[:, part].bitcast(F32), ALU.subtract
                           ).then_inc(s_lo[n], 1)

                    def xT_out(turn):
                        dve.wait_ge(s_xT_hi, turn)
                        rest(xT[1], wide(2, D), xT[0]).then_inc(s_xT_lo, 1)

                    for n, w in enumerate((w_g, w_u, w_d)):
                        split(n, w, 1)
                    xT_out(1)
                    @blocks(dve)
                    def _(j, s, i, more, new):
                        dve.wait_ge(s_silu, j + 1)
                        dve.wait_ge(s_up, j + 1)
                        tt(act_u, act_g, banks[:, 1, :], ALU.mult).then_inc(s_act, 1)
                        dve.wait_ge(s_actT_hi, j + 1)
                        rest(actT[1], banks[:, 4, :], actT[0]).then_inc(s_actT_lo, 1)
                        new(lambda this: split(0, w_g, this))
                        more(lambda: xT_out(j + 2))
                        new(lambda this: split(1, w_u, this))
                        dve.wait_ge(s_down, j + 1)
                        dve.wait_ge(s_yout[s], 16 * i)
                        nc.vector.tensor_copy(ys[s][:, BANK:], banks[:, 6, :]).then_inc(s_yv, 1)
                        new(lambda this: split(2, w_d, this))
                    def weigh(s, i):
                        order = Order(dve, o_jsum, i, SLOTS, s)
                        dve.wait_ge(s_yj[s], 32 * i + 32)
                        order.link(ts(yj[s][0], yj[s][0], weights[:, 0, bass.ds(SLOTS * i + s, 1)], None, ALU.mult))
                        nc.vector.scalar_tensor_tensor(
                            out=yj[s][0], in0=yj[s][1], scalar=weights[:, 1, bass.ds(SLOTS * i + s, 1)], in1=yj[s][0],
                            op0=ALU.mult, op1=ALU.add).then_inc(s_jsum[s], 1)

                    weigh(0, 0)
                    @turns(dve, NT // SLOTS, last=True)
                    def _(i):
                        order = Order(dve, o_jdve, i, 2 * SLOTS)
                        for s in range(SLOTS):
                            if s + 1 < SLOTS:
                                weigh(s + 1, i)
                            elif not is_last(i, NT // SLOTS):
                                weigh(0, i + 1)
                            dve.wait_ge(s_jdev[s], i + 1)
                            order.link(nc.vector.reciprocal(jst[s][:, 0:1], jst[s][:, 1:2]))
                            order.link(nc.vector.scalar_tensor_tensor(out=yj[s][1], in0=yj[s][0], scalar=jst[s][:, 0:1],
                                                                      in1=rows[:, 3, :], op0=ALU.mult, op1=ALU.mult))
                            dve.wait_ge(s_xj[s], 16 * i + 16)
                            nc.vector.tensor_tensor(xj[s], xj[s], yj[s][1], ALU.add).then_inc(s_jout[s], 1)

                @block.tensor
                def _(pe):
                    pe.wait_ge(s_picked, 1)
                    flat_picked = picked.rearrange("p t e -> p (t e)")
                    nc.tensor.matmul(banks[:, 0, :], before, flat_picked, start=True, stop=True)
                    nc.tensor.matmul(banks[:, 1, :], ones, flat_picked, start=True, stop=True).then_inc(s_rank, 1)
                    for a in range(2):
                        pe.wait_ge(s_onehot, a + 1)
                        for n in range(NT):
                            ins = nc.tensor.matmul(banks[:, 2, 0:BLOCKS], in_block[a][:, n, :], of_block[a][:, n, :],
                                                   start=(a == 0 and n == 0), stop=(a == 1 and n == NT - 1))
                    ins.then_inc(s_list, 1)
                    pe.wait_ge(s_lists, 1)

                    def turn_tokens(s, turn, half):
                        if not half:
                            pe.wait_ge(s_xg[s], 16 * turn)
                        for k in range(4 * half, 4 * half + 4):
                            ins = nc.tensor.transpose(wide(2, D)[:, k * P:(k + 1) * P], xg[s][:, k * P:(k + 1) * P], ident)
                        if half:
                            ins.then_inc(s_xgT, 1)

                    def product(bank, xs, ready, w, chunks, columns=slice(0, BANK)):
                        for n, (a, b) in enumerate(((0, 0), (1, 0), (0, 1))):
                            if ready:
                                ready(n)
                            for k in range(chunks):
                                ins = nc.tensor.matmul(banks[:, bank, :], xs[a][:, k, :], w[b][:, k, columns],
                                                       start=(n == 0 and k == 0), stop=(n == 2 and k == chunks - 1))
                        return ins

                    for half in range(2):
                        turn_tokens(0, 1, half)
                    @blocks(pe)
                    def _(j, s, i, more, new):
                        this = load_of(pe, j)

                        def operands(n, x_hi, x_lo):
                            def ready(part):
                                if part == 0:
                                    pe.wait_ge(x_hi, j + 1)
                                    pe.wait_ge(s_hi[n], this)
                                elif part == 1:
                                    pe.wait_ge(x_lo, j + 1)
                                else:
                                    pe.wait_ge(s_lo[n], this)
                                    if n == 2:
                                        pe.wait_ge(s_lo_pool, this)
                            return ready

                        pe.wait_ge(s_act, j)
                        product(0, xT, operands(0, s_xT_hi, s_xT_lo), w_g, KD).then_inc(s_gate, 1)
                        product(1, xT, operands(1, s_xT_hi, s_xT_lo), w_u, KD).then_inc(s_up, 1)
                        more(lambda: turn_tokens(1 - s, i + 1 + s, 0))
                        pe.wait_ge(s_act, j + 1)
                        for k in range(KF):
                            ins = nc.tensor.transpose(banks[:, 4, k * P:(k + 1) * P], act_u[:, k * P:(k + 1) * P], ident)
                        ins.then_inc(s_actT, 1)
                        more(lambda: turn_tokens(1 - s, i + 1 + s, 1))
                        pe.wait_ge(s_ya, j)
                        pe.wait_ge(s_yv, j)
                        product(5, actT, operands(2, s_actT_hi, s_actT_lo), w_d, KF)
                        product(6, actT, None, w_d, KF, slice(BANK, D)).then_inc(s_down, 1)

        project()
        branch_w = Arena(mixing.enter_context(nc.sbuf_tensor("branch_w", [P, 2 * KC * D], F32)), 2 * KC * D)
        w_co, w_ao = branch_w.take(KC * D), branch_w.take(KC * D)
        attend()
        branches()
        merge()
        mixing.close()
        experts()


NAMES = ["x", "c", "w_ada", "b_ada", "g_pre_mix", "g_post_mix", "w_in", "w_dw", "b_dw", "conv_ln_g", "conv_ln_b",
         "w_conv_out", "q_norm_g", "k_norm_g", "w_attn_out", "w_out", "g_pre_ffn", "g_post_ffn", "w_group",
         "b_group", "w_router", "b_router", "w_e_gate", "w_e_up", "w_e_down"]


def rope_tables():
    half = HEAD // 2
    freq = np.float32(ROPE_THETA) ** (-np.arange(0, half, 2, dtype=np.float32) / np.float32(half))
    pos = np.arange(S)
    row = (pos // GRID_W).astype(np.float32)[:, None] * freq
    column = (pos % GRID_W).astype(np.float32)[:, None] * freq
    cos = np.concatenate([np.cos(row), np.cos(row), np.cos(column), np.cos(column)] * 2, 1)
    sin = np.concatenate([-np.sin(row), np.sin(row), -np.sin(column), np.sin(column)] * 2, 1)
    channel = np.arange(P)
    swap = channel[:, None] == (channel ^ (half // 2))
    mean = (channel[:, None] // HEAD == channel // HEAD) / HEAD
    return {"in_" + name: np.ascontiguousarray(a, np.float32) for name, a in (
        ("rope_cos", cos.T), ("rope_sin", sin.T), ("rope_swap", swap), ("head_mean", mean))}


def kernel(**inputs):
    import concourse.bacc as _bacc
    from concourse.bass_utils import run_bass_kernel_spmd as _run

    nc = _bacc.Bacc("TRN2", target_bir_lowering=False, num_devices=1)
    arrays, tensors = {}, {}
    for name in NAMES:
        arrays[f"in_{name}"] = np.ascontiguousarray(inputs[name])
    arrays.update(rope_tables())
    for name, a in arrays.items():
        tensors[name[3:]] = nc.dram_tensor(name, a.shape, mybir.dt.from_np(a.dtype), kind="ExternalInput").ap()
    out = nc.dram_tensor("out_0", (1, S, D), F32, kind="ExternalOutput").ap()
    encoder_block(nc, tensors, out)
    r = _run(nc, [arrays], core_ids=[0])
    return r.results[0]["out_0"]
```
